# Optimizing a Trainium2 kernel written in Bass

```python
import math, functools
import jax, jax.numpy as jnp
from jax import lax
import numpy as np

D_MODEL = 1024
BATCH = 1
SEQ = 1024
DEPTH = 2
DEC_BATCH = 8
DEC_SEQ = 8
PAST_LEN = 2048
PAGE_SIZE = 128

DIFF_HEADS = 4
DIFF_HEAD_DIM = 64
DIFF_QK_DIM = 2 * DIFF_HEAD_DIM
DIFF_V_DIM = 2 * DIFF_HEAD_DIM
DIFF_WIDTH = DIFF_HEADS * DIFF_V_DIM
CONV_WIDTH = 512
CONV_K = 3
EVEN_IN = 4 * DIFF_HEADS * DIFF_HEAD_DIM + 2 * DIFF_WIDTH + 4 * CONV_WIDTH
EVEN_MIX = DIFF_WIDTH + CONV_WIDTH
GLA_HEADS = 4
GLA_DK = 128
GLA_DV = 256
GLA_KEY_WIDTH = GLA_HEADS * GLA_DK
GLA_WIDTH = GLA_HEADS * GLA_DV
GLA_RANK = 16
GLA_TAU = 16.0
GLA_CHUNK = 64
ODD_IN = 2 * GLA_KEY_WIDTH + 2 * GLA_WIDTH + GLA_RANK

QBLOCK = 128
N_EVEN = (DEPTH + 1) // 2
N_ODD = DEPTH // 2
EPS = 1e-5
NEG = -1e30

kernel_name = 'hybrid_diffattn_shortconv_gla_step'

def _rmsnorm(x, w):
    xf = x.astype(jnp.float32)
    y = xf * lax.rsqrt(jnp.mean(xf * xf, axis=-1, keepdims=True) + EPS)
    return (y * w.astype(jnp.float32)).astype(x.dtype)

def _diff_attend(q1, q2, segs, lam):
    scale = DIFF_HEAD_DIM ** -0.5

    def scores(q, kk, mask):
        s = jnp.einsum('bqhd,bkhd->bhqk', q, kk).astype(jnp.float32) * scale
        return jnp.where(mask, s, NEG)

    s1 = jnp.concatenate([scores(q1, k[..., :DIFF_HEAD_DIM], m) for k, _, m in segs], axis=-1)
    s2 = jnp.concatenate([scores(q2, k[..., DIFF_HEAD_DIM:], m) for k, _, m in segs], axis=-1)
    p = jax.nn.softmax(s1, axis=-1) - lam * jax.nn.softmax(s2, axis=-1)
    out = 0.0
    start = 0
    for k, v, _ in segs:
        n = k.shape[1]
        out = out + jnp.einsum('bhqk,bkhd->bqhd', p[..., start:start + n], v.astype(jnp.float32))
        start += n
    return out

def _prompt_diff_attention(q1, q2, k, v, lam):
    B, T, H, dh = q1.shape
    nb = T // QBLOCK
    key_pos = jnp.arange(T)

    def block(args):
        i, qb1, qb2 = args
        qpos = i * QBLOCK + jnp.arange(QBLOCK)
        mask = key_pos[None, :] <= qpos[:, None]
        return _diff_attend(qb1, qb2, [(k, v, mask)], lam)

    qb1 = q1.reshape(B, nb, QBLOCK, H, dh).swapaxes(0, 1)
    qb2 = q2.reshape(B, nb, QBLOCK, H, dh).swapaxes(0, 1)
    out = lax.map(block, (jnp.arange(nb), qb1, qb2))
    return out.swapaxes(0, 1).reshape(B, T, H, DIFF_V_DIM)

def _sample_diff_attention(q1, q2, k, v, lam, past_k, past_v):
    Tn = q1.shape[1]
    past_mask = jnp.ones((Tn, past_k.shape[1]), dtype=bool)
    new_mask = jnp.tril(jnp.ones((Tn, Tn), dtype=bool))
    return _diff_attend(q1, q2, [(past_k, past_v, past_mask), (k, v, new_mask)], lam)

def _even_mixer(xn, w_in, w_out, subln_w, conv_w, lam, lambda_init, conv_prefix, attend):
    B, T, _ = xn.shape
    hd = DIFF_HEADS * DIFF_HEAD_DIM
    cuts = np.cumsum([hd, hd, hd, hd, DIFF_WIDTH, DIFF_WIDTH, CONV_WIDTH, CONV_WIDTH, CONV_WIDTH])
    q1, q2, k1, k2, v, g_a, b_gate, c_gate, h, g_b = jnp.split(xn @ w_in, cuts.tolist(), axis=-1)
    q1 = q1.reshape(B, T, DIFF_HEADS, DIFF_HEAD_DIM)
    q2 = q2.reshape(B, T, DIFF_HEADS, DIFF_HEAD_DIM)
    k_rows = jnp.concatenate([k1.reshape(B, T, DIFF_HEADS, DIFF_HEAD_DIM),
                              k2.reshape(B, T, DIFF_HEADS, DIFF_HEAD_DIM)], axis=-1)
    v_rows = v.reshape(B, T, DIFF_HEADS, DIFF_V_DIM)
    att = attend(q1, q2, k_rows, v_rows, lam)
    att = (_rmsnorm(att, subln_w) * (1.0 - lambda_init)).astype(xn.dtype)
    a_out = att.reshape(B, T, DIFF_WIDTH) * jax.nn.silu(g_a)
    u = c_gate * h
    full = jnp.concatenate([conv_prefix.astype(u.dtype), u], axis=1)
    conv = sum(conv_w[j] * full[:, j:j + T] for j in range(CONV_K))
    b_out = b_gate * conv * jax.nn.silu(g_b)
    y = jnp.concatenate([a_out, b_out], axis=-1) @ w_out
    return y, k_rows, v_rows, full[:, -(CONV_K - 1):]

def _gla_chunked(q, k, v, log_a, s0, chunk):
    B, T, H, dk = q.shape
    dv = v.shape[-1]
    n = T // chunk

    def to_chunks(t):
        return t.astype(jnp.float32).reshape(B, n, chunk, H, t.shape[-1]).swapaxes(0, 1)

    tri = jnp.tril(jnp.ones((chunk, chunk), dtype=bool))[None, :, :, None, None]

    def step(S, inp):
        qc, kc, vc, lac = inp
        b = jnp.cumsum(lac, axis=1)
        o_inter = jnp.einsum('bchk,bhkv->bchv', qc * jnp.exp(b), S)
        diff = b[:, :, None] - b[:, None, :]
        decay = jnp.where(tri, jnp.exp(jnp.where(tri, diff, 0.0)), 0.0)
        A = jnp.einsum('bihk,bjhk,bijhk->bhij', qc, kc, decay)
        o_intra = jnp.einsum('bhij,bjhv->bihv', A, vc)
        b_last = b[:, -1]
        S_new = jnp.exp(b_last)[..., None] * S + jnp.einsum(
            'bjhk,bjhv->bhkv', kc * jnp.exp(b_last[:, None] - b), vc)
        return S_new, o_inter + o_intra

    s_fin, o = lax.scan(step, s0.astype(jnp.float32),
                        (to_chunks(q), to_chunks(k), to_chunks(v), to_chunks(log_a)))
    return o.swapaxes(0, 1).reshape(B, T, H, dv), s_fin

def _gla_mixer(xn, w_in, w_gate_up, b_gate, norm_w, w_out, s0, chunk):
    B, T, _ = xn.shape
    cuts = np.cumsum([GLA_KEY_WIDTH, GLA_KEY_WIDTH, GLA_WIDTH, GLA_WIDTH])
    q, k, v, g, lr = jnp.split(xn @ w_in, cuts.tolist(), axis=-1)
    q = q.reshape(B, T, GLA_HEADS, GLA_DK) * (GLA_DK ** -0.5)
    k = k.reshape(B, T, GLA_HEADS, GLA_DK)
    v = v.reshape(B, T, GLA_HEADS, GLA_DV)
    z = (lr @ w_gate_up + b_gate).astype(jnp.float32)
    log_a = (jax.nn.log_sigmoid(z) / GLA_TAU).reshape(B, T, GLA_HEADS, GLA_DK)
    o, s_new = _gla_chunked(q, k, v, log_a, s0, chunk)
    o = _rmsnorm(o, norm_w).astype(xn.dtype).reshape(B, T, GLA_WIDTH)
    y = (o * jax.nn.silu(g)) @ w_out
    return y, s_new

def setup_inputs(seed: int = 0) -> dict:
    key = jax.random.key(seed)
    ks = jax.random.split(key, 20)
    f32 = jnp.float32
    n_pages = PAST_LEN // PAGE_SIZE
    n_used = DEC_BATCH * n_pages
    n_phys = n_used + max(n_used // 4, 1)

    def nrm(k, shape, s):
        return jax.random.normal(k, shape, f32) * s

    page_table = jax.random.permutation(ks[6], n_phys)[:n_used].reshape(DEC_BATCH, n_pages).astype(jnp.int32)
    return {
        'x_prompt': nrm(ks[0], (BATCH, SEQ, D_MODEL), 1.0),
        'x_sample': nrm(ks[1], (DEC_BATCH, DEC_SEQ, D_MODEL), 1.0),
        'cache_k': nrm(ks[2], (N_EVEN, n_phys, PAGE_SIZE, DIFF_HEADS, DIFF_QK_DIM), 1.0),
        'cache_v': nrm(ks[3], (N_EVEN, n_phys, PAGE_SIZE, DIFF_HEADS, DIFF_V_DIM), 1.0),
        'state_conv': nrm(ks[4], (N_EVEN, DEC_BATCH, CONV_K - 1, CONV_WIDTH), 1.0),
        'state_gla': nrm(ks[5], (N_ODD, DEC_BATCH, GLA_HEADS, GLA_DK, GLA_DV), 1.0),
        'page_table': page_table,
        'norm_w': 1.0 + nrm(ks[7], (DEPTH, D_MODEL), 0.01),
        'norm_f': 1.0 + nrm(ks[8], (D_MODEL,), 0.01),
        'w_in_even': nrm(ks[9], (N_EVEN, D_MODEL, EVEN_IN), D_MODEL ** -0.5),
        'w_out_even': nrm(ks[10], (N_EVEN, EVEN_MIX, D_MODEL), EVEN_MIX ** -0.5),
        'diff_lambda': nrm(ks[11], (N_EVEN, 4, DIFF_HEAD_DIM), 0.1),
        'diff_subln_w': 1.0 + nrm(ks[12], (N_EVEN, DIFF_V_DIM), 0.01),
        'conv_w': nrm(ks[13], (N_EVEN, CONV_K, CONV_WIDTH), CONV_K ** -0.5),
        'w_in_odd': nrm(ks[14], (N_ODD, D_MODEL, ODD_IN), D_MODEL ** -0.5),
        'w_gate_up': nrm(ks[15], (N_ODD, GLA_RANK, GLA_KEY_WIDTH), GLA_RANK ** -0.5),
        'b_gate': nrm(ks[16], (N_ODD, GLA_KEY_WIDTH), 0.1),
        'gla_norm_w': 1.0 + nrm(ks[17], (N_ODD, GLA_DV), 0.01),
        'w_out_odd': nrm(ks[18], (N_ODD, GLA_WIDTH, D_MODEL), GLA_WIDTH ** -0.5),
    }

def reference(x_prompt, x_sample, cache_k, cache_v, state_conv, state_gla, page_table,
              norm_w, norm_f, w_in_even, w_out_even, diff_lambda, diff_subln_w, conv_w,
              w_in_odd, w_gate_up, b_gate, gla_norm_w, w_out_odd):
    xp, xs = x_prompt, x_sample
    Bp, Tp = xp.shape[0], xp.shape[1]
    Bs, Ts = xs.shape[0], xs.shape[1]
    kp_l, vp_l, ks_l, vs_l, cp_l, cs_l, gp_l, gs_l = [], [], [], [], [], [], [], []
    for layer in range(DEPTH):
        i = layer // 2
        xnp = _rmsnorm(xp, norm_w[layer])
        xns = _rmsnorm(xs, norm_w[layer])
        if layer % 2 == 0:
            lambda_init = 0.8 - 0.6 * math.exp(-0.3 * layer)
            lp = diff_lambda[i].astype(jnp.float32)
            lam = jnp.exp(jnp.sum(lp[0] * lp[1])) - jnp.exp(jnp.sum(lp[2] * lp[3])) + lambda_init
            yp, kr, vr, cb = _even_mixer(
                xnp, w_in_even[i], w_out_even[i], diff_subln_w[i], conv_w[i], lam, lambda_init,
                jnp.zeros((Bp, CONV_K - 1, CONV_WIDTH), xnp.dtype), _prompt_diff_attention)
            past_k = cache_k[i, page_table].reshape(Bs, -1, DIFF_HEADS, DIFF_QK_DIM)
            past_v = cache_v[i, page_table].reshape(Bs, -1, DIFF_HEADS, DIFF_V_DIM)
            ys, krs, vrs, cbs = _even_mixer(
                xns, w_in_even[i], w_out_even[i], diff_subln_w[i], conv_w[i], lam, lambda_init,
                state_conv[i], functools.partial(_sample_diff_attention, past_k=past_k, past_v=past_v))
            kp_l.append(kr); vp_l.append(vr); ks_l.append(krs); vs_l.append(vrs)
            cp_l.append(cb); cs_l.append(cbs)
        else:
            yp, sp = _gla_mixer(xnp, w_in_odd[i], w_gate_up[i], b_gate[i], gla_norm_w[i], w_out_odd[i],
                                jnp.zeros((Bp, GLA_HEADS, GLA_DK, GLA_DV), jnp.float32), min(GLA_CHUNK, Tp))
            ys, ss = _gla_mixer(xns, w_in_odd[i], w_gate_up[i], b_gate[i], gla_norm_w[i], w_out_odd[i],
                                state_gla[i], Ts)
            gp_l.append(sp); gs_l.append(ss)
        xp = xp + yp
        xs = xs + ys
    y_prompt = _rmsnorm(xp, norm_f)
    y_sample = _rmsnorm(xs, norm_f)
    return (y_prompt, y_sample, jnp.stack(kp_l), jnp.stack(vp_l), jnp.stack(ks_l), jnp.stack(vs_l),
            jnp.stack(cp_l), jnp.stack(cs_l), jnp.stack(gp_l), jnp.stack(gs_l))


_drawn_inputs = setup_inputs


def setup_inputs(seed=0):
    import zlib

    import numpy as np

    out = dict(_drawn_inputs(seed))
    spreads = {}
    factors = {'norm_w': 2.794, 'norm_f': 5.97, 'diff_subln_w': 8.0, 'gla_norm_w': 8.0}
    for name, (base, spread) in spreads.items():
        noise = np.random.default_rng([zlib.crc32(name.encode()), seed]).standard_normal(out[name].shape)
        drawn = base * np.exp(spread * noise) if base else spread * noise
        out[name] = __import__('jax').numpy.asarray(drawn.astype(out[name].dtype))
    for name, factor in factors.items():
        out[name] = (out[name] * factor).astype(out[name].dtype)
    return out
```

```python
import math
from contextlib import ExitStack

import concourse.bass as bass
from concourse import mybir

F32 = mybir.dt.float32
F32R = mybir.dt.float32r
BF16 = mybir.dt.bfloat16
I32 = mybir.dt.int32
ACT = mybir.ActivationFunctionType
ALU = mybir.AluOpType
AX = mybir.AxisListType.X
ds = bass.ds

P = 128
EPS = 1e-5
NEG = -1e30


class Chain:

    def __init__(self, eng, sem):
        self.eng, self.sem, self.base, self.k = eng, sem, 0, 0

    def link(self, ins):
        ins.then_inc(self.sem, 1)
        self.k += 1
        self.eng.wait_ge(self.sem, self.base + self.k)

    def enter(self, i, per, first=0):
        self.start = self.base + self.k
        self.base, self.k, self.per = i * per + (self.start - first * per), 0, per

    def leave(self, trips):
        assert self.k == self.per, (self.k, self.per)
        self.base, self.k = self.start + trips * self.per, 0


def build_step(nc, a, o, scr):
    D = a["norm_w"].shape[1]
    SEQ = a["x_prompt"].shape[1]
    DB, DS = a["x_sample"].shape[:2]
    NS = DB * DS
    TOK = SEQ + NS
    NT = SEQ // P
    KT = D // P
    PAGES = a["page_table"].shape[1]
    NPHYS, PAGE = a["cache_k"].shape[1:3]
    H = a["cache_k"].shape[3]
    DH = a["cache_k"].shape[4] // 2
    HW = H * 2 * DH
    DV = a["state_gla"].shape[4]
    GH = a["state_gla"].shape[2]
    CW = a["conv_w"].shape[2]
    CH = 256
    NCH0 = a["w_in_even"].shape[2] // CH
    NCH1 = (a["w_in_odd"].shape[2] - 16) // CH
    ODD = a["w_in_odd"].shape[2]
    SC = DH ** -0.5
    LAM0 = 0.8 - 0.6 * math.exp(0.0)
    QK_SC = float(P) ** -0.5
    HALVES = [64, 32, 16, 8, 4, 2, 1]
    assert P == PAGE and NS == 64 and HW == 512 and D == 1024 and GH == H == 4
    TS = [(0, 512), (512, 1024), (1024, TOK)]

    act0, act1 = scr
    a0 = act0.rearrange("(m p) t -> m p t", p=P)
    a1 = act1.rearrange("(m p) t -> m p t", p=P)

    top = ExitStack()
    with top:
        def sem(n):
            return top.enter_context(nc.semaphore(n))

        def sb(n, shape, dt=F32, where=top):
            return where.enter_context(nc.sbuf_tensor(n, shape, dt))

        ident = sb("ident", [P, P])
        ones = sb("ones", [P, P])
        identb = sb("identb", [P, P], BF16)
        causal = sb("causal", [P, P], BF16)
        new_mask = sb("new_mask", [DS, H * 2 * DS])
        decay_m = sb("decay_m", [P, 11, P])
        lvl_mask = sb("lvl_mask", [P, 7, P])
        norm_bc = sb("norm_bc", [P, D])
        vec_rows = sb("vec_rows", [15, P])
        vec = sb("vec", [P, 15])
        lam_in = sb("lam_in", [P, 4, DH])
        lam_pr = sb("lam_pr", [P, 2, DH])
        lam_s = sb("lam_s", [P, 4])
        neg_lam = lam_s[:, 3:4]
        eps_b = sb("eps_b", [P, 1])
        ssq = sb("ssq", [P, NT + 1])
        rstd = sb("rstd", [P, NT + 1])
        pages_sb = sb("pages_sb", [1, DB * PAGES], I32)
        x1 = sb("x1", [P, NT + 1, D])
        attT = sb("attT", [P, H, TOK])

        pj = ExitStack()
        xh = sb("xh", [P, KT, TOK], F32R, pj)
        xl = sb("xl", [P, KT, TOK], F32R, pj)
        wraw = sb("wraw", [P, 2, KT, CH], F32, pj)
        wh = sb("wh", [P, 2, KT, CH], F32R, pj)
        wl = sb("wl", [P, 2, KT, CH], F32R, pj)
        stage = sb("stage", [P, 2, TOK], F32, pj)
        xs = sb("xs", [P, 2, D], F32, pj)
        pj.close()

        at = ExitStack()
        q_pair = sb("q_pair", [P, DB, H, 2 * DS], F32, at)
        smax = sb("smax", [P, 2, 64], F32, at)
        hd = ExitStack()
        q_in = sb("q_in", [P, TOK], F32, hd)
        k_in = sb("k_in", [P, TOK], F32, hd)
        v_in = sb("v_in", [P, TOK], F32, hd)
        k_row = sb("k_row", [P, NT + 1, P], F32, hd)
        v_row = sb("v_row", [P, NT + 1, P], F32, hd)
        prob = sb("prob", [P, 2, 2, SEQ], F32, hd)
        probT = sb("probT", [P, 2, SEQ], F32, hd)
        row_st = sb("row_st", [P, 2, 6], F32, hd)
        hd.close()
        kring = sb("kring", [P, 4, 4, HW], F32, at)
        vring = sb("vring", [P, 4, 4, HW], F32, at)
        k_new = sb("k_new", [DS, HW], F32, at)
        v_new = sb("v_new", [DS, HW], F32, at)
        kT = sb("kT", [P, 3, H * P], F32, at)
        p_s = sb("p_s", [P, PAGES, 64], F32, at)
        p_new = sb("p_new", [DS, 64], F32, at)
        mrow = sb("mrow", [64, 1], F32, at)
        mdiag = sb("mdiag", [64, 64], F32, at)
        s_out = sb("s_out", [P, 2, 64], F32, at)
        at.close()

        gt = ExitStack()
        xh_ = sb("xh_hold", [P, 2 * KT, TOK], F32, gt)
        gate_in = sb("gate_in", [P, TOK], F32, gt)
        g_e = sb("g_e", [P, TOK], F32, gt)
        sq0 = sb("sq0", [P, TOK], F32, gt)
        rs0 = sb("rs0", [P, TOK], F32, gt)
        cin = sb("cin", [P, 3, TOK], F32, gt)
        u_p = sb("u_p", [P, 2 + SEQ], F32, gt)
        u_s = sb("u_s", [P, DB, 2 + DS], F32, gt)
        conv = sb("conv", [P, TOK], F32, gt)
        u_last = sb("u_last", [P, 4, 2 * DB + 2], F32, gt)
        u_rows = sb("u_rows", [2 * DB + 2, CW], F32, gt)
        st_rows = sb("st_rows", [2 * DB, CW], F32, gt)
        st_T = sb("st_T", [P, 4, 2 * DB], F32, gt)
        gt.close()

        gl = ExitStack()
        woh = sb("woh", [P, KT, D], F32R, gl)
        wol = sb("wol", [P, KT, D], F32R, gl)
        qk_c = sb("qk_c", [P, 2, 2 * GH, P], F32, gl)
        v_c = sb("v_c", [P, 2, 2 * GH, P], F32, gl)
        g_c = sb("g_c", [P, 2, 2 * GH, P], F32, gl)
        lr_c = sb("lr_c", [17, 2, P], F32, gl)
        w_up = sb("w_up", [17, GH * P], F32, gl)
        zt = sb("zt", [P, GH * P], F32, gl)
        la = sb("la", [P, GH * P], F32, gl)
        ee = sb("ee", [P, 2, GH, P], F32, gl)
        e_last = sb("e_last", [P, GH, DB], F32, gl)
        qb = sb("qb", [P, GH, P], F32, gl)
        ks = sb("ks", [P, GH, P], F32, gl)
        kst = sb("kst", [P, GH * P], F32, gl)
        xlev = sb("xlev", [P, 2, GH, P], F32, gl)
        aT = sb("aT", [P, GH, P], F32, gl)
        v_tok = sb("v_tok", [P, GH * DV], F32, gl)
        st_g = sb("st_g", [P, GH, DV], F32, gl)
        sq1 = sb("sq1", [P, 2, GH, P], F32, gl)
        rs1 = sb("rs1", [P, GH * P], F32, gl)
        sg = sb("sg", [P, 2 * GH, P], F32, gl)
        mh = sb("mh", [P, 2 * GH, P], F32R, gl)
        ml = sb("ml", [P, 2 * GH, P], F32R, gl)
        gl.close()
        free = attT[:, :, :].rearrange("p h t -> p (h t)")
        s0_b = free[:, 0:2 * GH * DV].rearrange("p (s h v) -> p s h v", s=2, h=GH)
        wo_raw = free[:, 0:2 * KT * P].rearrange("p (s k n) -> p s k n", s=2, k=KT)
        v_m = free[:, 2 * GH * DV:3 * GH * DV]
        y_o = v_m
        mt = free[:, 3 * GH * DV:4 * GH * DV].rearrange("p (m t) -> p m t", t=P)

        ps = top.enter_context(nc.psum_tensor("ps", [P, 8, 512], F32))

        phase_end = sem("phase_end")
        passed_pe, passed_dve, passed_pool = sem("passed_pe"), sem("passed_dve"), sem("passed_pool")
        passed_sp = sem("passed_sp")
        x_in = [sem("x_in0"), sem("x_in1")]
        norm_in = sem("norm_in")
        vec_in = sem("vec_in")
        vecT_ready = sem("vecT_ready")
        lam_ready = sem("lam_ready")
        lam_exp = sem("lam_exp")
        act_step = sem("act_step")
        dve_step = sem("dve_step")
        pool_step = sem("pool_step")
        block = top.enter_context(nc.Block())
        def rd(t):
            return t.bitcast(F32)

        def wait_apart(eng, passed, *waits):
            for q, n in waits:
                eng.wait_ge(q, n)
            eng.sem_inc(passed, 1)

        class Norm:
            def __init__(self, l):
                self.rstd = sem(f"n{l}_rstd")
                self.xs_ready = sem(f"n{l}_xs_ready")
                self.T_ready = sem(f"n{l}_T_ready")
                self.hi = sem(f"n{l}_hi")
                self.lo = sem(f"n{l}_lo")

        class Proj:
            def __init__(self, l):
                self.raw_in = [sem(f"p{l}_raw_in{s}") for s in range(2)]
                self.hi = sem(f"p{l}_hi")
                self.lo = sem(f"p{l}_lo")
                self.acc_ready = sem(f"p{l}_acc_ready")
                self.acc_used = sem(f"p{l}_acc_used")
                self.stored = [sem(f"p{l}_stored{s}") for s in range(2)]

        norms = [Norm(0), Norm(1)]
        projs = [Proj(0), Proj(1)]
        po = Proj(2)

        def barrier(eng, n):
            eng.drain().then_inc(phase_end, 1)
            eng.wait_ge(phase_end, 5 * (n + 1))

        def cols(m):
            return ds(m * P, P)

        att_in = sem("att_in")
        kv_T = sem("kv_T")
        kv_T_used = sem("kv_T_used")
        kv_out = sem("kv_out")
        rows_ready = sem("rows_ready")
        probT_ready = sem("probT_ready")
        s_ready = sem("s_ready")
        m_ready = sem("m_ready")
        p_exp = sem("p_exp")
        p_mix = sem("p_mix")
        o_ready = sem("o_ready")
        o_used = sem("o_used")
        qp_zero = sem("qp_zero")
        pt_in = sem("pt_in")
        k_page = [sem(f"k_page{s}") for s in range(4)]
        v_page = [sem(f"v_page{s}") for s in range(4)]
        new_in = sem("new_in")
        kT_ready = sem("kT_ready")
        kT_used = [sem("kT_used_act"), sem("kT_used_dve")]
        kp_ready = sem("kp_ready")
        sc_ready = sem("sc_ready")
        mx_ready = sem("mx_ready")
        mT_ready = sem("mT_ready")
        md_ready = sem("md_ready")
        mb_ready = sem("mb_ready")
        ss_ready = sem("ss_ready")
        ps_exp = sem("ps_exp")
        v_used = sem("v_used")
        so_ready = sem("so_ready")
        so_used = sem("so_used")
        ga_in = sem("ga_in")
        cv_in = sem("cv_in")
        sq_ready = sem("sq_ready")
        sq_sum = sem("sq_sum")
        rs_ready = sem("rs_ready")
        ge_ready = sem("ge_ready")
        mixed = sem("mixed")
        mix_hi = sem("mix_hi")
        mix_lo = sem("mix_lo")
        st_in = sem("st_in")
        stT_ready = sem("stT_ready")
        stT_rows = sem("stT_rows")
        ul_ready = sem("ul_ready")
        ulT_ready = sem("ulT_ready")
        ul_rows = sem("ul_rows")
        conv_out = sem("conv_out")
        wo_in = [sem(f"wo_in{s}") for s in range(2)]
        wo_hi = sem("wo_hi")
        wo_lo = sem("wo_lo")
        up_in = sem("up_in")
        g_in = [sem(f"g_in{s}") for s in range(2)]
        g_zero = sem("g_zero")
        g_ones = sem("g_ones")
        ge_gla = sem("ge_gla")
        sg_one = sem("sg_one")
        sg_rec = sem("sg_rec")
        sg_ready = sem("sg_ready")
        z_ready = sem("z_ready")
        z_abs = sem("z_abs")
        la_ready = sem("la_ready")
        vT_ready = sem("vT_ready")
        v_ready = sem("v_ready")
        e_ready = sem("e_ready")
        e_exp = sem("e_exp")
        e_used = sem("e_used")
        q_scaled = sem("q_scaled")
        x_ready = sem("x_ready")
        a_ready = sem("a_ready")
        a_used = sem("a_used")
        ks_ready = sem("ks_ready")
        ksT_ready = sem("ksT_ready")
        kst_ready = sem("kst_ready")
        qb_ready = sem("qb_ready")
        oT_ready = sem("oT_ready")
        sd_ready = sem("sd_ready")
        st_ready = sem("st_ready")
        sq1_ready = sem("sq1_ready")
        r_ready = sem("r_ready")
        rs1_ready = sem("rs1_ready")
        m_mixed = sem("m_mixed")
        mh_ready = sem("mh_ready")
        ml_ready = sem("ml_ready")
        y_ready = sem("y_ready")
        y_used = sem("y_used")
        y_ssq = sem("y_ssq")
        y_rstd = sem("y_rstd")
        y_norm = sem("y_norm")
        y_out = sem("y_out")
        s0_in = [sem(f"s0_in{s}") for s in range(2)]
        s0_out = [sem(f"s0_out{s}") for s in range(2)]
        vm_ready = sem("vm_ready")
        sdb_ready = sem("sdb_ready")
        s0_new = sem("s0_new")
        gp_out = sem("gp_out")

        xp_v = a["x_prompt"][0].rearrange("(t p) d -> p t d", p=P)
        xs_v = a["x_sample"].rearrange("b s d -> (b s) d")
        w0_v = a["w_in_even"][0].rearrange("(k p) n -> p k n", p=P)
        w1_v = a["w_in_odd"][0].rearrange("(k p) n -> p k n", p=P)
        wo0_v = a["w_out_even"][0].rearrange("(k p) n -> p k n", p=P)
        wo1_v = a["w_out_odd"][0].rearrange("(k p) n -> p k n", p=P)
        kp_o = o["k_prompt"][0, 0].rearrange("(t p) h d -> p t h d", p=P)
        vp_o = o["v_prompt"][0, 0].rearrange("(t p) h d -> p t h d", p=P)
        ks_o = o["k_sample"][0].rearrange("b s h d -> (b s) h d")
        vs_o = o["v_sample"][0].rearrange("b s h d -> (b s) h d")
        ks_b = o["k_sample"][0].rearrange("b s h d -> b s (h d)")
        vs_b = o["v_sample"][0].rearrange("b s h d -> b s (h d)")
        ck = a["cache_k"][0].rearrange("n p h d -> n p (h d)")
        cv_ = a["cache_v"][0].rearrange("n p h d -> n p (h d)")
        yp_o = o["y_prompt"][0].rearrange("(t p) d -> t p d", p=P)
        ys_o = o["y_sample"].rearrange("b s d -> (b s) d")

        def acc(m):
            return ps[:, 3 * m:3 * m + 3, :].rearrange("p a b -> p (a b)")

        @block.sync
        def _(sp):
            sp.dma_start(x1[:, 0:4, :], xp_v[:, 0:4, :]).then_inc(x_in[0], 16)
            sp.dma_start(norm_bc[:, :], a["norm_w"][0:1, :].to_broadcast([P, D])).then_inc(norm_in, 16)
            sp.dma_start(x1[:, 4:NT, :], xp_v[:, 4:NT, :]).then_inc(x_in[1], 16)
            sp.dma_start(x1[64:P, NT, :], xs_v).then_inc(x_in[1], 16)
            sp.dma_start(vec_rows[0:12, :], a["conv_w"][0].rearrange("k (j p) -> (k j) p", p=P)).then_inc(vec_in, 16)
            sp.dma_start(vec_rows[12:13, :], a["diff_subln_w"]).then_inc(vec_in, 16)
            sp.dma_start(vec_rows[13:15, :], a["gla_norm_w"].rearrange("a (d p) -> (a d) p", p=P)).then_inc(vec_in, 16)
            sp.dma_start(lam_in[:, :, :].rearrange("p a d -> p (a d)"),
                         a["diff_lambda"].rearrange("a b d -> a (b d)").to_broadcast([P, 4 * DH])).then_inc(vec_in, 16)
            sp.dma_start(pages_sb[:, :], a["page_table"].rearrange("(a b) g -> a (b g)", a=1)).then_inc(pt_in, 16)

            def stream(p, view, n):
                for s in range(2):
                    sp.dma_start(wraw[:, s], view[:, :, s * CH:(s + 1) * CH]).then_inc(p.raw_in[s], 16)
                with sp.Fori(1, n // 2) as j:
                    for s in range(2):
                        sp.wait_ge(p.lo, 2 * j + s - 1)
                        sp.dma_start(wraw[:, s], view[:, :, ds((2 * j + s) * CH, CH)]).then_inc(p.raw_in[s], 16)

            stream(projs[0], w0_v, NCH0)
            barrier(sp, 0)

            def head_loads(h):
                if not (isinstance(h, int) and h == 0):
                    wait_apart(sp, passed_sp, (s_ready, NT * h))
                    wait_apart(sp, passed_sp, (rows_ready, 6 * h))
                for dst, first in ((q_in, 0), (k_in, 2 * H * DH)):
                    for half in range(2):
                        sp.dma_start(dst[half * DH:(half + 1) * DH, :],
                                     act0[ds(h * DH + first + half * H * DH, DH), :]).then_inc(att_in, 16)
                sp.dma_start(v_in[:, :], act0[ds(h * P + 4 * H * DH, P), :]).then_inc(att_in, 16)

            head_loads(0)
            with sp.Fori(1, H) as h:
                head_loads(h)
            barrier(sp, 1)

            sp.wait_ge(pt_in, 16)

            def key_pages(b, first):
                for s in range(4):
                    if not first:
                        sp.wait_ge(kT_ready, (PAGES + 1) * b + 4 * s + 4 - (PAGES + 1))
                    for g in range(4):
                        page = sp.value_load(pages_sb[0:1, ds(b * PAGES + 4 * s + g, 1)], min_val=0, max_val=NPHYS - 1)
                        sp.dma_start(kring[:, s, g, :], ck[ds(page, 1), :, :].rearrange("a p d -> p (a d)")).then_inc(k_page[s], 16)

            key_pages(0, True)
            with sp.Fori(1, DB) as b:
                key_pages(b, False)
            barrier(sp, 2)

            sp.dma_start(st_rows[:, :], a["state_conv"][0].rearrange("b r c -> (b r) c")).then_inc(st_in, 16)
            for h in range(H):
                if h:
                    sp.wait_ge(mixed, h)
                sp.dma_start(gate_in[:, :], a0[12 + h]).then_inc(ga_in, 16)
            for j in range(4):
                sp.wait_ge(mixed, H + j)
                for n in range(3):
                    sp.dma_start(cin[:, n, :], a0[16 + 4 * n + j]).then_inc(cv_in, 16)
                sp.dma_start(gate_in[:, :], a0[28 + j]).then_inc(ga_in, 16)
            sp.wait_ge(norms[0].xs_ready, NT + 1)
            sp.dma_start(norm_bc[:, :], a["norm_w"][1:2, :].to_broadcast([P, D])).then_inc(norm_in, 16)
            barrier(sp, 3)
            stream(po, wo0_v, D // CH)
            barrier(sp, 4)
            stream(projs[1], w1_v, NCH1)
            sp.wait_ge(projs[1].lo, NCH1 - 1)
            sp.dma_start(wraw[:, 0, :, 0:P], w1_v[:, :, ODD - P:ODD]).then_inc(projs[1].raw_in[0], 16)
            sp.wait_ge(norms[1].xs_ready, NT + 1)
            sp.dma_start(norm_bc[:, :], a["norm_f"].rearrange("(a d) -> a d", a=1).to_broadcast([P, D])).then_inc(norm_in, 16)
            barrier(sp, 5)

            def chunk_loads(s, lo, t0, n):
                for dst, m in ((qk_c, 0), (v_c, 2 * GH), (g_c, 4 * GH)):
                    sp.dma_start(dst[:, s, :, lo:P], a1[m:m + 2 * GH, :, ds(t0, n)].rearrange("m p t -> p m t")).then_inc(g_in[s], 16)
                sp.dma_start(lr_c[0:16, s, lo:P], act1[25 * P - 16:25 * P, ds(t0, n)]).then_inc(g_in[s], 16)

            def y_store(c):
                sp.wait_ge(y_norm, c + 1)
                if isinstance(c, int) and c == NT:
                    sp.dma_start(ys_o, y_o[P - NS:P, :]).then_inc(y_out, 16)
                else:
                    sp.dma_start(yp_o[ds(c, 1), :, :].rearrange("a p d -> p (a d)"), y_o[:, :]).then_inc(y_out, 16)

            sp.dma_start(w_up[0:16, :], a["w_gate_up"][0]).then_inc(up_in, 16)
            sp.dma_start(w_up[16:17, :], a["b_gate"]).then_inc(up_in, 16)
            sp.wait_ge(g_ones, 1)
            chunk_loads(0, 0, 0, P)
            for n in range(2):
                sp.dma_start(wo_raw[:, n], wo1_v[:, :, n * P:(n + 1) * P]).then_inc(wo_in[n], 16)
            chunk_loads(1, 0, P, P)
            for n in range(2, D // P):
                sp.wait_ge(wo_lo, n - 1)
                sp.dma_start(wo_raw[:, n % 2], wo1_v[:, :, n * P:(n + 1) * P]).then_inc(wo_in[n % 2], 16)
            with sp.Fori(0, NT // 2 - 1) as j:
                for s in range(2):
                    sp.wait_ge(m_mixed, 2 * j + s + 1)
                    chunk_loads(s, 0, (2 * j + s + 2) * P, P)
                    y_store(2 * j + s)
            sp.wait_ge(m_mixed, NT - 1)
            chunk_loads(0, P - NS, SEQ, NS)
            s0v = a["state_gla"][0].rearrange("b h k v -> b k h v")
            s0o = o["gla_sample"][0].rearrange("b h k v -> b k h v")
            for b in range(2):
                sp.dma_start(s0_b[:, b], s0v[b]).then_inc(s0_in[b], 16)
            y_store(NT - 2)
            y_store(NT - 1)
            for b in range(DB):
                sp.wait_ge(s0_new, b + 1)
                sp.dma_start(s0o[b], s0_b[:, b % 2]).then_inc(s0_out[b % 2], 16)
                if b + 2 < DB:
                    sp.wait_ge(s0_out[b % 2], 16 * (b // 2 + 1))
                    sp.dma_start(s0_b[:, b % 2], s0v[b + 2]).then_inc(s0_in[b % 2], 16)
            y_store(NT)
            sp.wait_ge(y_out, 16 * (NT + 1))
            for s in range(2):
                sp.wait_ge(s0_out[s], 16 * DB // 2)
            barrier(sp, 6)

        @block.gpsimd
        def _(pool):
            ch = Chain(pool, pool_step)

            def sel(view, pattern, base, mult, fill, op=ALU.is_ge):
                ch.link(pool.affine_select(out=view, in_=view, pattern=pattern, compare_op=op, fill=fill,
                                           base=base, channel_multiplier=mult))

            ch.link(pool.memset(x1[0:64, NT, :], 0.0))
            ch.link(pool.memset(eps_b[:, :], EPS))
            ch.link(pool.memset(ones[:, :], 1.0))
            ch.link(pool.memset(ident[:, :], 0.0))
            sel(ident[:, :], [[-1, P]], 0, 1, 1.0, ALU.not_equal)
            ch.link(pool.memset(identb[:, :], 0.0))
            sel(identb[:, :], [[-1, P]], 0, 1, 1.0, ALU.not_equal)
            ch.link(pool.memset(causal[:, :], 0.0))
            sel(causal[:, :], [[-1, P]], 0, 1, NEG)
            ch.link(pool.memset(new_mask[:, :], 0.0))
            nm = new_mask[:, :].rearrange("p (n i) -> p n i", i=DS)
            sel(nm, [[0, 2 * H], [1, DS]], 0, -1, NEG)
            ch.link(pool.memset(decay_m[:, :, :], 1.0))
            sel(decay_m[:, 0, :], [[1, P]], 0, -1, 0.0)
            sel(decay_m[:, 1, :], [[-1, P]], -1, 1, 0.0)
            blk = decay_m[:, 9, :].rearrange("p (n i) -> p n i", i=DS)
            sel(blk, [[DS, P // DS], [1, DS]], 0, -1, 0.0)
            sel(blk, [[-DS, P // DS], [0, DS]], 0, 1, 0.0)
            blk = decay_m[:, 10, :].rearrange("p (n i) -> p n i", i=DS)
            sel(blk, [[-DS, P // DS], [-1, DS]], -1, 1, 0.0)
            sel(blk, [[DS, P // DS], [0, DS]], DS - 1, -1, 0.0)
            ch.link(pool.memset(lvl_mask[:, :, :], 1.0))
            for l, hf in enumerate(HALVES):
                n = P // (2 * hf)
                v = decay_m[:, 2 + l, :].rearrange("p (n two r) -> p n two r", two=2, r=hf)
                sel(v[:, :, 1, :], [[-2 * hf, n], [0, hf]], -hf, 1, 0.0)
                sel(v[:, :, 1, :], [[2 * hf, n], [1, hf]], hf, -1, 0.0)
                sel(v[:, :, 0, :], [[-2 * hf, n], [-1, hf]], -1, 1, 0.0)
                sel(v[:, :, 0, :], [[2 * hf, n], [0, hf]], hf - 1, -1, 0.0)
                m = lvl_mask[:, l, :].rearrange("p (n two r) -> p n two r", two=2, r=hf)
                sel(m[:, :, 1, :], [[-2 * hf, n], [0, hf]], 0, 1, 0.0)
                sel(m[:, :, 1, :], [[2 * hf, n], [0, hf]], hf - 1, -1, 0.0)
                ch.link(pool.memset(m[:, :, 0, :], 0.0))
            n_const = ch.k

            def low_parts(p, n):
                with pool.Fori(0, n // 2) as j:
                    for s in range(2):
                        pool.wait_ge(p.hi, 2 * j + s + 1)
                        pool.tensor_tensor(wl[:, s], wraw[:, s], rd(wh[:, s]), ALU.subtract).then_inc(p.lo, 1)

            low_parts(projs[0], NCH0)
            barrier(pool, 0)

            ch.link(pool.memset(q_pair[:, :, :, :], 0.0))
            pool.memset(smax[:, 0, :], 0.0).then_inc(qp_zero, 1)
            with pool.Fori(0, H) as h:
                pool.wait_ge(rows_ready, 6 * h + 6)
                hs = ds(h, 1)
                pool.dma_start(kp_o[:, :, hs, :].rearrange("p t a d -> p t (a d)"), k_row[:, 0:NT, :]).then_inc(kv_out, 16)
                pool.dma_start(ks_o[:, hs, :].rearrange("t a d -> t (a d)"), k_row[64:P, NT, :]).then_inc(kv_out, 16)
                pool.dma_start(vp_o[:, :, hs, :].rearrange("p t a d -> p t (a d)"), v_row[:, 0:NT, :]).then_inc(kv_out, 16)
                pool.dma_start(vs_o[:, hs, :].rearrange("t a d -> t (a d)"), v_row[64:P, NT, :]).then_inc(kv_out, 16)
            pool.wait_ge(kv_out, 64 * H)
            barrier(pool, 1)

            pool.wait_ge(pt_in, 16)

            def value_pages(b, first):
                if not first:
                    pool.wait_ge(so_ready, b)
                pool.dma_start(k_new[:, :], ks_b[ds(b, 1), :, :].rearrange("a s d -> (a s) d")).then_inc(new_in, 16)
                pool.dma_start(v_new[:, :], vs_b[ds(b, 1), :, :].rearrange("a s d -> (a s) d")).then_inc(new_in, 16)
                for s in range(4):
                    if not first:
                        pool.wait_ge(v_used, 4 * b + s - 3)
                    for g in range(4):
                        page = pool.value_load(pages_sb[0:1, ds(b * PAGES + 4 * s + g, 1)], min_val=0, max_val=NPHYS - 1)
                        pool.dma_start(vring[:, s, g, :], cv_[ds(page, 1), :, :].rearrange("a p d -> p (a d)")).then_inc(v_page[s], 16)

            value_pages(0, True)
            with pool.Fori(1, DB) as b:
                value_pages(b, False)
            barrier(pool, 2)

            ch.link(pool.memset(u_p[:, 0:2], 0.0))
            for j in range(4):
                pool.wait_ge(cv_in, 48 * (j + 1))
                if j:
                    pool.wait_ge(mixed, H + j)
                else:
                    pool.wait_ge(stT_rows, 1)
                ch.link(pool.tensor_copy(u_s[:, :, 0:2], st_T[:, j, :].rearrange("p (b r) -> p b r", r=2)))
                ch.link(pool.tensor_tensor(u_s[:, :, 2:2 + DS], cin[:, 1, SEQ:TOK].rearrange("p (b s) -> p b s", s=DS),
                                           cin[:, 2, SEQ:TOK].rearrange("p (b s) -> p b s", s=DS), ALU.mult))
                ch.link(pool.tensor_tensor(u_p[:, 2:2 + SEQ], cin[:, 1, 0:SEQ], cin[:, 2, 0:SEQ], ALU.mult))
                ch.link(pool.tensor_copy(u_last[:, j, 0:2 * DB].rearrange("p (b r) -> p b r", r=2), u_s[:, :, DS:DS + 2]))
                pool.tensor_copy(u_last[:, j, 2 * DB:2 * DB + 2], u_p[:, SEQ:SEQ + 2]).then_inc(ul_ready, 1)
            pool.wait_ge(ul_rows, 1)
            pool.dma_start(o["conv_sample"][0].rearrange("b r c -> (b r) c"), u_rows[0:2 * DB, :]).then_inc(conv_out, 16)
            pool.dma_start(o["conv_prompt"][0, 0], u_rows[2 * DB:2 * DB + 2, :]).then_inc(conv_out, 16)
            pool.wait_ge(conv_out, 32)
            barrier(pool, 3)
            low_parts(po, D // CH)
            barrier(pool, 4)
            low_parts(projs[1], NCH1)
            pool.wait_ge(projs[1].hi, NCH1 + 1)
            pool.tensor_tensor(wl[:, 0, :, 0:P], wraw[:, 0, :, 0:P], rd(wh[:, 0, :, 0:P]), ALU.subtract).then_inc(projs[1].lo, 1)
            barrier(pool, 5)

            pool.memset(lr_c[:, :, :], 1.0).then_inc(g_ones, 1)
            ch.link(pool.memset(st_g[:, :, :], 0.0))
            pool.memset(aT[:, :, :], 0.0).then_inc(g_zero, 1)
            for n in range(D // P):
                pool.wait_ge(wo_hi, n + 1)
                pool.tensor_tensor(wol[:, :, n * P:(n + 1) * P], wo_raw[:, n % 2],
                                   rd(woh[:, :, n * P:(n + 1) * P]), ALU.subtract).then_inc(wo_lo, 1)

            def chunk(c, s, t0, use):
                wait_apart(pool, passed_pool, (g_in[s], 64 * (use + 1)))
                pool.tensor_scalar(qk_c[:, s, 0:GH, :], qk_c[:, s, 0:GH, :], QK_SC, None, ALU.mult).then_inc(q_scaled, 1)
                wait_apart(pool, passed_pool, (ge_gla, c + 1))
                pool.tensor_scalar(sg[:, :, :], sg[:, :, :], 1.0, None, ALU.add).then_inc(sg_one, 1)
                wait_apart(pool, passed_pool, (e_exp, 9 * c + 1), (q_scaled, c + 1),
                           *([] if isinstance(c, int) and c == 0 else [(st_ready, GH * c)]))
                if isinstance(c, int) and c == NT:
                    ch.link(pool.tensor_copy(e_last[:, :, :], ee[:, 0, :, P - NS + DS - 1:P:DS]))
                else:
                    ch.link(pool.tensor_copy(e_last[:, :, 0:1], ee[:, 0, :, P - 1:P]))
                pool.tensor_tensor(qb[:, :, :], qk_c[:, s, 0:GH, :], ee[:, 0, :, :], ALU.mult).then_inc(qb_ready, 1)
                pool.wait_ge(e_exp, 9 * c + 2)
                pool.tensor_tensor(ks[:, :, :], qk_c[:, s, GH:2 * GH, :], ee[:, 1, :, :], ALU.mult).then_inc(ks_ready, 1)
                pool.wait_ge(sg_rec, c + 1)
                pool.tensor_tensor(sg[:, :, :], sg[:, :, :], g_c[:, s, :, :], ALU.mult).then_inc(sg_ready, 1)

            chunk(0, 0, 0, 0)
            with pool.Fori(0, NT // 2 - 1) as j:
                ch.enter(j, 2)
                chunk(2 * j + 1, 1, 0, j)
                chunk(2 * j + 2, 0, 0, j + 1)
            ch.leave(NT // 2 - 1)
            chunk(NT - 1, 1, 0, NT // 2 - 1)
            pool.wait_ge(st_ready, GH * NT)
            pool.dma_start(o["gla_prompt"][0, 0].rearrange("h k v -> k h v"), st_g[:, :, :]).then_inc(gp_out, 16)
            pool.wait_ge(oT_ready, NT)
            pool.memset(aT[:, :, :], 0.0).then_inc(g_zero, 1)
            chunk(NT, 0, P - NS, NT // 2)
            pool.wait_ge(gp_out, 16)
            barrier(pool, 6)

        @block.scalar
        def _(act):
            ch = Chain(act, act_step)

            def rsqrt(out, src, mean, sem_=None):
                ch.link(act.activation(out, src, ACT.Ln, bias=eps_b[:, :], scale=mean))
                ins = act.activation(out, out, ACT.Exp, scale=-0.5)
                ins.then_inc(sem_, 1)

            def norm_high(n):
                def high(t, slot, c0, n0):
                    for q in range(2):
                        act.wait_ge(n.T_ready, 2 * t + q + 1)
                        src = ps[:, 2 * slot + q, :].rearrange("p (k i) -> p k i", i=P)[:, :, P - n0:P]
                        act.activation(xh[:, 4 * q:4 * q + 4, ds(c0, n0)], src, ACT.Copy).then_inc(n.hi, 1)
                with act.Fori(0, NT // 2) as j:
                    for s in range(2):
                        high(2 * j + s, s, (2 * j + s) * P, P)
                high(NT, 0, SEQ, NS)

            def norm_stats(n):
                for t in range(NT + 1):
                    if n is norms[0] and t in (0, 4):
                        act.wait_ge(x_in[t // 4], 16 if t == 0 else 32)
                        if t == 4:
                            act.wait_ge(pool_step, 2)
                    ch.link(act.activation(xs[:, t % 2, :], x1[:, t, :], ACT.Square, accum_out=ssq[:, t:t + 1]))
                rsqrt(rstd[:, :], ssq[:, :], 1.0 / D, n.rstd)

            def high_parts(p, n, view, base, after=0):
                def hi(j, s):
                    act.wait_ge(p.raw_in[s], 16 * (j + 1))
                    if not (isinstance(j, int) and j == 0):
                        act.wait_ge(p.acc_ready, base * (2 * j + s - 1))
                    act.activation(wh[:, s], wraw[:, s], ACT.Copy).then_inc(p.hi, 1)

                def store(j, s):
                    if view is None:
                        return
                    for m in range(2):
                        u = 4 * j + 2 * s + m
                        act.wait_ge(p.acc_used, u + 1)
                        act.dma_start(view[ds(u, 1), :, :].rearrange("a p t -> p (a t)"), stage[:, m]).then_inc(p.stored[m], 16)

                hi(0, 0)
                hi(0, 1)
                store(0, 0)
                with act.Fori(1, n // 2) as j:
                    hi(j, 0)
                    store(j - 1, 1)
                    hi(j, 1)
                    store(j, 0)
                if after:
                    act.wait_ge(p.raw_in[0], 16 * (n // 2 + 1))
                    act.wait_ge(p.acc_ready, base * (n - 1))
                    act.activation(wh[:, 0, :, 0:P], wraw[:, 0, :, 0:P], ACT.Copy).then_inc(p.hi, 1)
                store(n // 2 - 1, 1)
                if after:
                    act.wait_ge(p.acc_used, 2 * n + 1)
                    act.dma_start(view[2 * n], stage[:, 0]).then_inc(p.stored[0], 16)
                if view is not None:
                    act.wait_ge(p.stored[0], 16 * (n + after))
                    act.wait_ge(p.stored[1], 16 * n)

            act.wait_ge(vec_in, 64)
            act.wait_ge(lam_ready, 1)
            act.activation(lam_s[:, 0:2], lam_s[:, 0:2], ACT.Exp).then_inc(lam_exp, 1)
            norm_stats(norms[0])
            norm_high(norms[0])
            high_parts(projs[0], NCH0, a0, 2)
            barrier(act, 0)

            def head(h):
                def group(n, dst, width, sem_):
                    act.wait_ge(kv_T, 18 * h + n + 1)
                    act.activation(dst, ps[:, 4 + n % 2, 0:width], ACT.Copy).then_inc(sem_, 1)

                act.wait_ge(kv_out, 64 * h)
                act.wait_ge(o_ready, NT * h)
                for n in range(6):
                    row, t0 = (k_row, v_row)[n // 3], 4 * (n % 3)
                    nt = min(4, NT + 1 - t0)
                    group(n, row[:, t0:t0 + nt, :].rearrange("p t d -> p (t d)"), nt * P, rows_ready)
                n = 6
                for i in range(NT):
                    nk = (i + 1) * P
                    act.wait_ge(m_ready, NT * h + i + 1)
                    for w in range(2):
                        ins = act.activation(prob[:, i % 2, w, 0:nk], ps[:, 2 * w:2 * w + 2, :].rearrange("p a b -> p (a b)")[:, 0:nk],
                                             ACT.Exp, bias=row_st[:, i % 2, 2 + w:3 + w], scale=SC,
                                             accum_out=row_st[:, i % 2, 4 + w:5 + w])
                        ins.then_inc(p_exp, 1)
                    if i >= 1:
                        n = tail(h, i - 1, n, group)
                tail(h, NT - 1, n, group)

            def tail(h, i, n, group):
                for t0 in range(0, i + 1, 4):
                    nt = min(4, i + 1 - t0)
                    group(n, probT[:, i % 2, t0 * P:(t0 + nt) * P], nt * P, probT_ready)
                    n += 1
                act.wait_ge(o_ready, NT * h + i + 1)
                act.activation(attT[:, ds(h, 1), i * P:(i + 1) * P].rearrange("p a t -> p (a t)"),
                               ps[:, 6 + i % 2, 0:P], ACT.Copy).then_inc(o_used, 1)
                return n

            head(0)
            with act.Fori(1, H) as h:
                head(h)
            barrier(act, 1)

            with act.Fori(0, DB) as b:
                for g in range(0, PAGES + 1, 2):
                    w = P if g < PAGES else DS
                    act.wait_ge(kT_ready, (PAGES + 1) * b + g + 1)
                    act.wait_ge(kp_ready, (PAGES + 1) * b + max(g - 2, 0) + 1)
                    act.activation(kT[:, g % 3, 0:H * w], ps[:, g % 3, 0:H * w], ACT.Copy).then_inc(kT_used[0], 1)
                act.wait_ge(ss_ready, b + 2)
                act.activation(p_new[:, :], p_new[:, :], ACT.Exp, scale=SC).then_inc(ps_exp, 1)
                act.activation(p_s[:, :, :], p_s[:, :, :], ACT.Exp, scale=SC).then_inc(ps_exp, 1)
            barrier(act, 2)

            for h in range(H):
                if h:
                    act.wait_ge(mixed, h)
                act.activation(sq0[:, :], attT[:, h, :], ACT.Square).then_inc(sq_ready, 1)
                act.wait_ge(ga_in, 16 * (h + 1))
                act.activation(g_e[:, :], gate_in[:, :], ACT.Exp, scale=-1.0).then_inc(ge_ready, 1)
                act.wait_ge(sq_sum, h + 1)
                rsqrt(rs0[:, :], acc(h % 2)[:, 0:TOK], 1.0 / P, rs_ready)
                act.wait_ge(mixed, h + 1)
                act.activation(xh[:, h, :], conv[:, :], ACT.Copy).then_inc(mix_hi, 1)
            for j in range(4):
                act.wait_ge(ga_in, 16 * (H + j + 1))
                act.wait_ge(mixed, H + j)
                act.activation(g_e[:, :], gate_in[:, :], ACT.Exp, scale=-1.0).then_inc(ge_ready, 1)
                act.wait_ge(mixed, H + j + 1)
                act.activation(xh[:, H + j, :], conv[:, :], ACT.Copy).then_inc(mix_hi, 1)
            barrier(act, 3)
            high_parts(po, D // CH, None, NT + 1)
            barrier(act, 4)
            norm_stats(norms[1])
            norm_high(norms[1])
            high_parts(projs[1], NCH1, a1, 2, 1)
            barrier(act, 5)

            for n in range(D // P):
                act.wait_ge(wo_in[n % 2], 16 * (n // 2 + 1))
                act.activation(woh[:, :, n * P:(n + 1) * P], wo_raw[:, n % 2], ACT.Copy).then_inc(wo_hi, 1)

            def front(c, s, use, levels):
                act.wait_ge(z_ready, c + 1)
                ch.link(act.activation(zt[:, :], ps[:, 0, :], ACT.Abs))
                ch.link(act.activation(zt[:, :], zt[:, :], ACT.Exp, scale=-1.0))
                act.activation(zt[:, :], zt[:, :], ACT.Ln, bias=1.0).then_inc(z_abs, 1)
                for n in range(2):
                    act.wait_ge(vT_ready, 2 * c + n + 1)
                    act.activation(v_tok[:, n * 512:(n + 1) * 512], ps[:, 2 + n, :], ACT.Copy).then_inc(v_ready, 1)
                act.wait_ge(g_in[s], 64 * (use + 1))
                if not (isinstance(c, int) and c == 0):
                    act.wait_ge(m_mixed, c)
                act.activation(sg[:, :, :], g_c[:, s, :, :], ACT.Exp, scale=-1.0).then_inc(ge_gla, 1)
                exps(c, 0, 2)

            def exps(c, l0, l1):
                for l in range(l0, l1):
                    act.wait_ge(e_ready, 9 * c + l + 1)
                    if l >= 4:
                        act.wait_ge(x_ready, 7 * c + l - 3)
                    elif l >= 2:
                        act.wait_ge((qb_ready, ks_ready)[l - 2], c + 1)
                    else:
                        act.wait_ge(x_ready, 7 * c)
                    act.activation(ee[:, l % 2, :, :].rearrange("p h i -> p (h i)"), ps[:, (1 + l) % 2, :],
                                   ACT.Exp, scale=1.0 / 16).then_inc(e_exp, 1)

            def gated(c):
                act.wait_ge(m_mixed, c + 1)
                act.wait_ge(y_ready, 2 * c)
                act.activation(mh[:, :, :], mt[:, :, :], ACT.Copy).then_inc(mh_ready, 1)

            def final(c, t):
                act.wait_ge(y_used, 2 * c + 2)
                if not (isinstance(c, int) and c == 0):
                    act.wait_ge(y_norm, c)
                    act.wait_ge(y_out, 16 * c)
                ch.link(act.activation(y_o[:, :], x1[:, ds(t, 1), :].rearrange("p a d -> p (a d)"), ACT.Square, accum_out=ssq[:, 0:1]))
                rsqrt(rstd[:, 0:1], ssq[:, 0:1], 1.0 / D, y_rstd)

            def back(c):
                act.wait_ge(ksT_ready, c + 1)
                act.activation(kst[:, :], ps[:, 2, :], ACT.Copy).then_inc(kst_ready, 1)
                act.wait_ge(oT_ready, c + 1)
                for d in range(2):
                    act.activation(sq1[:, d, :, :].rearrange("p h i -> p (h i)"), ps[:, 6 + d, :], ACT.Square).then_inc(sq1_ready, 1)

            def r1(c):
                act.wait_ge(r_ready, c + 1)
                rsqrt(rs1[:, :], ps[:, 5, :], 1.0 / DV, rs1_ready)

            def body(c, s, use, L=9):
                r1(c - 1)
                front(c, s, use, L)
                gated(c - 1)
                exps(c, 2, 4)
                if L > 4:
                    exps(c, 4, 6 if L > 6 else L)
                final(c - 1, c - 1)
                if L > 6:
                    exps(c, 6, L)
                back(c)

            front(0, 0, 0, 9)
            exps(0, 2, 9)
            back(0)
            with act.Fori(0, NT // 2 - 1) as j:
                ch.enter(j, 2 * 5)
                body(2 * j + 1, 1, j)
                body(2 * j + 2, 0, j + 1)
            ch.leave(NT // 2 - 1)
            body(NT - 1, 1, NT // 2 - 1)
            body(NT, 0, NT // 2, 5)
            r1(NT)
            gated(NT)
            final(NT, NT)
            barrier(act, 6)

        @block.vector
        def _(v):
            ch = Chain(v, dve_step)

            def normalize(n, ready):
                def scale(t, s):
                    if not (isinstance(t, int) and t < 2):
                        v.wait_ge(n.T_ready, 2 * t - 2)
                    src = x1[:, ds(t, 1), :].rearrange("p a d -> p (a d)")
                    v.scalar_tensor_tensor(out=xs[:, s, :], in0=src, scalar=rstd_col(t), in1=norm_bc[:, :],
                                           op0=ALU.mult, op1=ALU.mult).then_inc(n.xs_ready, 1)

                def rstd_col(t):
                    return rstd[:, ds(t, 1)]

                def low(t, slot, c0, n0):
                    for q in range(2):
                        v.wait_ge(n.hi, 2 * t + q + 1)
                        src = ps[:, 2 * slot + q, :].rearrange("p (k i) -> p k i", i=P)[:, :, P - n0:P]
                        v.tensor_tensor(xl[:, 4 * q:4 * q + 4, ds(c0, n0)], src, rd(xh[:, 4 * q:4 * q + 4, ds(c0, n0)]),
                                        ALU.subtract).then_inc(n.lo, 1)

                v.wait_ge(n.rstd, 1)
                v.wait_ge(norm_in, ready)
                scale(0, 0)
                scale(1, 1)
                with v.Fori(0, NT // 2 - 1) as j:
                    for s in range(2):
                        low(2 * j + s, s, (2 * j + s) * P, P)
                        scale(2 * j + s + 2, s)
                low(NT - 2, 0, (NT - 2) * P, P)
                scale(NT, 0)
                low(NT - 1, 1, (NT - 1) * P, P)
                low(NT, 0, SEQ, NS)

            def units_out(p, n, after=0):
                def unit(j, s, m):
                    v.wait_ge(p.acc_ready, 4 * j + 2 * s + m + 1)
                    if not (isinstance(j, int) and j == 0 and s == 0):
                        v.wait_ge(p.stored[m], 16 * (2 * j + s))
                    v.tensor_copy(stage[:, m], acc(m)[:, 0:TOK]).then_inc(p.acc_used, 1)

                for s in range(2):
                    for m in range(2):
                        unit(0, s, m)
                with v.Fori(1, n // 2) as j:
                    for s in range(2):
                        for m in range(2):
                            unit(j, s, m)
                if after:
                    unit(n // 2, 0, 0)

            v.wait_ge(vec_in, 64)
            lp = lam_in[:, :, :].rearrange("p (a b) d -> p a b d", b=2)
            ch.link(v.tensor_tensor(lam_pr[:, :, :], lp[:, :, 0, :], lp[:, :, 1, :], ALU.mult))
            v.tensor_reduce(lam_s[:, 0:2], lam_pr[:, :, :], AX, ALU.add).then_inc(lam_ready, 1)
            v.wait_ge(lam_exp, 1)
            ch.link(v.scalar_tensor_tensor(out=neg_lam, in0=lam_s[:, 1:2], scalar=LAM0, in1=lam_s[:, 0:1],
                                           op0=ALU.subtract, op1=ALU.subtract))
            v.wait_ge(vecT_ready, 1)
            ch.link(v.tensor_copy(vec[:, :], ps[:, 7, 0:15]))
            ch.link(v.tensor_scalar(vec[:, 12:13], vec[:, 12:13], 1.0 - LAM0, None, ALU.mult))
            normalize(norms[0], 16)
            units_out(projs[0], NCH0)
            barrier(v, 0)

            v.wait_ge(qp_zero, 1)

            def head(h):
                v.wait_ge(att_in, 80 * h + 80)
                for w in range(2):
                    r = slice(w * DH, (w + 1) * DH)
                    ch.link(v.tensor_copy(q_pair[r, :, ds(h, 1), w * DS:(w + 1) * DS].rearrange("p b a s -> p b (a s)"),
                                          q_in[r, SEQ:TOK].rearrange("p (b s) -> p b s", s=DS)))
                for i in range(NT):
                    nk = (i + 1) * P
                    st = row_st[:, i % 2, :]
                    v.wait_ge(s_ready, NT * h + i + 1)
                    for w in range(2):
                        ch.link(v.tensor_reduce(st[:, w:w + 1], ps[:, 2 * w:2 * w + 2, :].rearrange("p a b -> p (a b)")[:, 0:nk], AX, ALU.max))
                    v.tensor_scalar(st[:, 2:4], st[:, 0:2], -SC, None, ALU.mult).then_inc(m_ready, 1)
                    v.wait_ge(p_exp, 2 * (NT * h + i + 1))
                    ch.link(v.reciprocal(st[:, 4:6], st[:, 4:6]))
                    ch.link(v.tensor_scalar(st[:, 5:6], st[:, 5:6], neg_lam, None, ALU.mult))
                    ch.link(v.tensor_scalar(prob[:, i % 2, 0, 0:nk], prob[:, i % 2, 0, 0:nk], st[:, 4:5], None, ALU.mult))
                    v.scalar_tensor_tensor(out=prob[:, i % 2, 0, 0:nk], in0=prob[:, i % 2, 1, 0:nk], scalar=st[:, 5:6],
                                           in1=prob[:, i % 2, 0, 0:nk], op0=ALU.mult, op1=ALU.add).then_inc(p_mix, 1)

            head(0)
            with v.Fori(1, H) as h:
                ch.enter(h, 2 + 5 * NT, 1)
                head(h)
            ch.leave(H - 1)
            barrier(v, 1)

            v.sem_inc(ss_ready, 1)
            v.sem_inc(so_used, 1)
            with v.Fori(0, DB) as b:
                ch.enter(b, 7)
                for g in range(1, PAGES + 1, 2):
                    v.wait_ge(kT_ready, (PAGES + 1) * b + g + 1)
                    v.wait_ge(kp_ready, (PAGES + 1) * b + max(g - 2, 0) + 1)
                    v.tensor_copy(kT[:, g % 3, :], ps[:, g % 3, :]).then_inc(kT_used[1], 1)
                v.wait_ge(kp_ready, (PAGES + 1) * (b + 1) + 1)
                sc = ps[:, 3:5, :].rearrange("p a b -> p (a b)").rearrange("p (g c) -> p g c", c=64)
                ch.link(v.tensor_reduce(smax[:, 0, :], sc.rearrange("p g c -> p c g"), AX, ALU.max))
                ch.link(v.tensor_tensor(p_new[:, :], ps[0:DS, 5, 0:64], new_mask[:, :], ALU.add))
                v.tensor_tensor(smax[0:DS, 0, :], smax[0:DS, 0, :], p_new[:, :], ALU.max).then_inc(mx_ready, 1)
                v.wait_ge(mT_ready, b + 1)
                ch.link(v.tensor_reduce(mrow[:, :], ps[0:64, 6, 0:P], AX, ALU.max))
                v.tensor_scalar(mdiag[:, :], ident[0:64, 0:64], mrow[:, :], None, ALU.mult).then_inc(md_ready, 1)
                v.wait_ge(mb_ready, b + 1)
                ch.link(v.tensor_copy(smax[:, 1, :], ps[:, 6, P:P + 64]))
                ch.link(v.tensor_tensor(p_new[:, :], p_new[:, :], smax[0:DS, 1, :], ALU.subtract))
                v.tensor_tensor(p_s[:, :, :], sc, smax[:, 1:2, :].to_broadcast([P, PAGES, 64]), ALU.subtract).then_inc(ss_ready, 1)
                v.wait_ge(so_ready, b + 1)
                ch.link(v.reciprocal(s_out[:, 0, :], ps[:, 7, 64:128]))
                ch.link(v.tensor_tensor(s_out[:, 1, :], ps[:, 7, 0:64], s_out[:, 0, :], ALU.mult))
                so = s_out[:, 1, :].rearrange("p (h w s) -> p h w s", h=H, w=2)
                v.scalar_tensor_tensor(out=attT[:, :, ds(b * DS + SEQ, DS)], in0=so[:, :, 1, :], scalar=neg_lam,
                                       in1=so[:, :, 0, :], op0=ALU.mult, op1=ALU.add).then_inc(so_used, 1)
            ch.leave(DB)
            barrier(v, 2)

            v.wait_ge(stT_ready, 1)
            v.tensor_copy(st_T[:, :, :], ps[:, 7, 0:64].rearrange("p (j r) -> p j r", r=2 * DB)).then_inc(stT_rows, 1)

            def silu(n):
                v.wait_ge(ge_ready, n + 1)
                ch.link(v.tensor_scalar(g_e[:, :], g_e[:, :], 1.0, None, ALU.add))
                ch.link(v.reciprocal(g_e[:, :], g_e[:, :]))
                ch.link(v.tensor_tensor(g_e[:, :], g_e[:, :], gate_in[:, :], ALU.mult))

            def lows(k):
                v.wait_ge(mix_hi, k + 1)
                ch.link(v.tensor_tensor(xl[:, k, :], conv[:, :], rd(xh[:, k, :]), ALU.subtract))

            for h in range(H):
                silu(h)
                v.wait_ge(rs_ready, h + 1)
                ch.link(v.scalar_tensor_tensor(out=conv[:, :], in0=attT[:, h, :], scalar=vec[:, 12:13], in1=rs0[:, :],
                                               op0=ALU.mult, op1=ALU.mult))
                v.tensor_tensor(conv[:, :], conv[:, :], g_e[:, :], ALU.mult).then_inc(mixed, 1)
                lows(h)
            for j in range(4):
                v.wait_ge(ul_ready, j + 1)
                tap = [vec[:, 4 * k + j:4 * k + j + 1] for k in range(3)]
                cs = conv[:, SEQ:TOK].rearrange("p (b s) -> p b s", s=DS)
                ch.link(v.tensor_scalar(conv[:, 0:SEQ], u_p[:, 0:SEQ], tap[0], None, ALU.mult))
                ch.link(v.tensor_scalar(cs, u_s[:, :, 0:DS], tap[0], None, ALU.mult))
                for k in (1, 2):
                    ch.link(v.scalar_tensor_tensor(out=conv[:, 0:SEQ], in0=u_p[:, k:k + SEQ], scalar=tap[k], in1=conv[:, 0:SEQ],
                                                   op0=ALU.mult, op1=ALU.add))
                    ch.link(v.scalar_tensor_tensor(out=cs, in0=u_s[:, :, k:k + DS], scalar=tap[k], in1=cs,
                                                   op0=ALU.mult, op1=ALU.add))
                ch.link(v.tensor_tensor(conv[:, :], conv[:, :], cin[:, 0, :], ALU.mult))
                silu(H + j)
                v.tensor_tensor(conv[:, :], conv[:, :], g_e[:, :], ALU.mult).then_inc(mixed, 1)
                lows(H + j)
            v.wait_ge(ulT_ready, 1)
            v.tensor_copy(u_rows[:, :], ps[0:2 * DB + 2, 7, :]).then_inc(ul_rows, 1)
            barrier(v, 3)

            v.sem_inc(po.acc_used, 1)
            with v.Fori(0, D // CH // 2) as j:
                for s in range(2):
                    for t in range(NT + 1):
                        n = (NT + 1) * s + t
                        r = slice(0, P) if t < NT else slice(64, P)
                        v.wait_ge(po.acc_ready, 2 * (NT + 1) * j + n + 1)
                        x = x1[r, t, ds((2 * j + s) * CH, CH)]
                        v.tensor_tensor(x, ps[r, n % 6, 0:CH], x, ALU.add).then_inc(po.acc_used, 1)
            barrier(v, 4)
            normalize(norms[1], 32)
            units_out(projs[1], NCH1, 1)
            barrier(v, 5)

            def gate(c):
                v.wait_ge(rs1_ready, c + 1)
                v.wait_ge(mh_ready, c)
                for d in range(2):
                    out = mt.rearrange("p (h d) i -> p h d i", d=2)[:, :, d, :]
                    ch.link(v.scalar_tensor_tensor(out=out, in0=ps[:, 6 + d, :].rearrange("p (h i) -> p h i", i=P),
                                                   scalar=vec[:, 13 + d:14 + d], in1=rs1[:, :].rearrange("p (h i) -> p h i", i=P),
                                                   op0=ALU.mult, op1=ALU.mult))
                v.wait_ge(sg_ready, c + 1)
                v.tensor_tensor(mt, mt, sg[:, :, :], ALU.mult).then_inc(m_mixed, 1)

            def log_decay(c):
                v.wait_ge(z_abs, c + 1)
                v.scalar_tensor_tensor(out=la[:, :], in0=ps[:, 0, :], scalar=0.0, in1=zt[:, :],
                                       op0=ALU.min, op1=ALU.subtract).then_inc(la_ready, 1)
                v.wait_ge(sg_one, c + 1)
                v.reciprocal(sg[:, :, :], sg[:, :, :]).then_inc(sg_rec, 1)

            def level(c, s, i, hf):
                v.wait_ge(e_exp, 9 * c + i + 3)
                v.wait_ge(q_scaled, c + 1)
                v.wait_ge(a_ready, 8 * c + max(i - 1, 0))
                e = ee[:, i % 2, :, :].rearrange("p h (n two r) -> p (h n) two r", two=2, r=hf)
                x = xlev[:, i % 2, :, :].rearrange("p h (n two r) -> p (h n) two r", two=2, r=hf)
                for w, m0 in ((0, GH), (1, 0)):
                    src = qk_c[:, s, m0:m0 + GH, :].rearrange("p h (n two r) -> p (h n) two r", two=2, r=hf)
                    ins = v.tensor_tensor(x[:, :, w, :], src[:, :, w, :], e[:, :, w, :], ALU.mult)
                    if w == 0:
                        ch.link(ins)
                    else:
                        ins.then_inc(x_ready, 1)

            def pairs(c, i, mask):
                m = mask.bitcast(I32).to_broadcast([P, GH, P])
                wait_apart(v, passed_dve, (a_ready, 8 * c + i + 1), (a_used, 8 * c + i))
                v.copy_predicated(aT[:, :, :], m, ps[:, 4 + i % 2, :].rearrange("p (h i) -> p h i", i=P)).then_inc(a_used, 1)

            def low(c):
                v.wait_ge(mh_ready, c + 1)
                v.wait_ge(y_ready, 2 * c)
                v.tensor_tensor(ml[:, :, :], mt, rd(mh[:, :, :]), ALU.subtract).then_inc(ml_ready, 1)

            def residual(c, t, r):
                for n in range(2):
                    v.wait_ge(y_ready, 2 * c + n + 1)
                    x = x1[r, ds(t, 1), n * 512:(n + 1) * 512].rearrange("p a d -> p (a d)")
                    v.tensor_tensor(x, ps[r, 4 + n, :], x, ALU.add).then_inc(y_used, 1)

            def out_norm(c, t):
                v.wait_ge(y_rstd, c + 1)
                v.scalar_tensor_tensor(out=y_o[:, :], in0=x1[:, ds(t, 1), :].rearrange("p a d -> p (a d)"), scalar=rstd[:, 0:1],
                                       in1=norm_bc[:, :], op0=ALU.mult, op1=ALU.mult).then_inc(y_norm, 1)

            def levels(c, s, halves, after_first=None):
                L = len(halves)
                first = HALVES.index(halves[0])
                v.wait_ge(g_zero, 2 if isinstance(c, int) and c == NT else 1)
                v.wait_ge(oT_ready, c)
                for i in range(L + 1):
                    pairs(c, i, lvl_mask[:, first + i:first + i + 1, :] if i < L else ident[:, None, :])
                    if i + 2 < L:
                        level(c, s, i + 2, halves[i + 2])

            def state(c):
                v.wait_ge(sd_ready, c + 1)
                for h in range(GH):
                    v.scalar_tensor_tensor(out=st_g[:, h, :], in0=st_g[:, h, :], scalar=e_last[:, h, 0:1],
                                           in1=ps[:, 2 + h // 2, (h % 2) * DV:(h % 2 + 1) * DV],
                                           op0=ALU.mult, op1=ALU.add).then_inc(st_ready, 1)

            def body(c, s, halves):
                gate(c - 1)
                log_decay(c)
                low(c - 1)
                level(c, s, 0, halves[0])
                level(c, s, 1, halves[1])
                residual(c - 1, c - 1, slice(0, P))
                levels(c, s, halves)
                out_norm(c - 1, c - 1)

            v.wait_ge(norm_in, 48)
            log_decay(0)
            v.wait_ge(g_zero, 1)
            level(0, 0, 0, HALVES[0])
            level(0, 0, 1, HALVES[1])
            levels(0, 0, HALVES)
            state(0)
            with v.Fori(0, NT // 2 - 1) as j:
                ch.enter(j, 2 * (2 + 7))
                body(2 * j + 1, 1, HALVES)
                state(2 * j + 1)
                body(2 * j + 2, 0, HALVES)
                state(2 * j + 2)
            ch.leave(NT // 2 - 1)
            body(NT - 1, 1, HALVES)
            state(NT - 1)
            body(NT, 0, HALVES[4:])
            for b in range(DB):
                i = P - NS + b * DS + DS - 1
                if b:
                    v.wait_ge(sdb_ready, b)
                else:
                    v.wait_ge(y_out, 16 * NT)
                v.wait_ge(v_ready, 2 * NT + 2)
                v.tensor_scalar(v_m, v_tok[:, :], decay_m[:, 9, i:i + 1], None, ALU.mult).then_inc(vm_ready, 1)
                v.wait_ge(sdb_ready, b + 1)
                for h in range(GH):
                    ins = v.scalar_tensor_tensor(out=s0_b[:, b % 2, h, :], in0=s0_b[:, b % 2, h, :], scalar=e_last[:, h, b:b + 1],
                                                 in1=ps[:, 2 + h // 2, (h % 2) * DV:(h % 2 + 1) * DV],
                                                 op0=ALU.mult, op1=ALU.add)
                ins.then_inc(s0_new, 1)
            gate(NT)
            low(NT)
            residual(NT, NT, slice(64, P))
            out_norm(NT, NT)
            barrier(v, 6)

        @block.tensor
        def _(pe):
            def transposes(n):
                def tile(t, s):
                    pe.wait_ge(n.xs_ready, t + 1)
                    if not (isinstance(t, int) and t < 2):
                        pe.wait_ge(n.lo, 2 * t - 2)
                    for q in range(2):
                        for k in range(4):
                            ins = pe.transpose(ps[:, 2 * s + q, k * P:(k + 1) * P], xs[:, s, (4 * q + k) * P:(4 * q + k + 1) * P], ident[:, :])
                        ins.then_inc(n.T_ready, 1)
                tile(0, 0)
                tile(1, 1)
                with pe.Fori(1, NT // 2) as j:
                    tile(2 * j, 0)
                    tile(2 * j + 1, 1)
                tile(NT, 0)

            def split_product(out, lh, ll, rh, rl, k, last):
                pe.matmul(out, lh, rh, start=(k == 0), stop=False)
                pe.matmul(out, lh, rl, start=False, stop=False)
                return pe.matmul(out, ll, rh, start=False, stop=last)

            def project(p, n, norm, after=0):
                def unit(j, s, m):
                    if not (isinstance(j, int) and j == 0 and s == 0):
                        pe.wait_ge(p.acc_used, 4 * j + 2 * s + m - 1)
                    for k in range(KT):
                        w = (slice(None), s, k, slice(m * P, (m + 1) * P))
                        for wt, xt in ((wh, xh), (wh, xl), (wl, xh)):
                            for c0, c1 in TS:
                                ins = pe.matmul(acc(m)[:, c0:c1], wt[w], xt[:, k, c0:c1],
                                                start=(k == 0 and wt is wh and xt is xh),
                                                stop=(k == KT - 1 and wt is wl))
                    ins.then_inc(p.acc_ready, 1)

                def pair(j):
                    for s in range(2):
                        pe.wait_ge(p.lo, 2 * j + s + 1)
                        for m in range(2):
                            unit(j, s, m)

                pe.wait_ge(norm.lo, 2 * (NT + 1))
                pair(0)
                with pe.Fori(1, n // 2) as j:
                    pair(j)
                if after:
                    pe.wait_ge(p.lo, n + 1)
                    unit(n // 2, 0, 0)

            pe.wait_ge(pool_step, 5)
            pe.wait_ge(vec_in, 64)
            pe.transpose(ps[:, 7, 0:15], vec_rows[:, :], ident[0:15, 0:15]).then_inc(vecT_ready, 1)
            transposes(norms[0])
            project(projs[0], NCH0, norms[0])
            barrier(pe, 0)

            def head(h):
                pe.wait_ge(att_in, 80 * h + 80)

                def bank_free(n):
                    if n < 2:
                        pe.wait_ge(probT_ready, 12 * h)
                    elif n < 8:
                        pe.wait_ge(rows_ready, 6 * h + n - 1)
                    else:
                        pe.wait_ge(probT_ready, 12 * h + n - 7)

                for n in range(6):
                    src, t0 = (k_in, v_in)[n // 3], 4 * (n % 3)
                    bank_free(n)
                    for t in range(t0, min(t0 + 4, NT + 1)):
                        c0 = t * P if t < NT else TOK - P
                        ins = pe.transpose(ps[:, 4 + n % 2, (t - t0) * P:(t - t0 + 1) * P], src[:, c0:c0 + P], ident[:, :])
                    ins.then_inc(kv_T, 1)

                def scores(i):
                    nk = (i + 1) * P
                    pe.wait_ge(p_exp, 2 * (NT * h + i))
                    for w in range(2):
                        r = slice(w * DH, (w + 1) * DH)
                        for b in range(0, nk, 512):
                            e = min(b + 512, nk)
                            bank = ps[:, 2 * w + b // 512, 0:e - b]
                            diag = e == nk
                            ins = pe.matmul(bank, q_in[r, i * P:(i + 1) * P], k_in[r, b:e], start=True, stop=not diag)
                            if diag:
                                ins = pe.matmul(bank[:, e - b - P:e - b], identb[:, :], causal[:, :], start=False, stop=True)
                    ins.then_inc(s_ready, 1)

                def values(i, n):
                    pe.wait_ge(p_mix, NT * h + i + 1)
                    for t0 in range(0, i + 1, 4):
                        bank_free(n)
                        for t in range(t0, min(t0 + 4, i + 1)):
                            ins = pe.transpose(ps[:, 4 + n % 2, (t - t0) * P:(t - t0 + 1) * P], prob[:, i % 2, 0, t * P:(t + 1) * P], ident[:, :])
                        ins.then_inc(kv_T, 1)
                        n += 1
                    pe.wait_ge(probT_ready, 12 * h + n - 6)
                    if i == 0:
                        pe.wait_ge(rows_ready, 6 * h + 6)
                    pe.wait_ge(o_used, NT * h + max(i - 1, 0))
                    for t in range(i + 1):
                        ins = pe.matmul(ps[:, 6 + i % 2, 0:P], v_row[:, t, :], probT[:, i % 2, t * P:(t + 1) * P],
                                        start=(t == 0), stop=(t == i))
                    ins.then_inc(o_ready, 1)
                    return n

                n = 6
                scores(0)
                for i in range(NT):
                    if i + 1 < NT:
                        scores(i + 1)
                    n = values(i, n)

            head(0)
            with pe.Fori(1, H) as h:
                head(h)
            barrier(pe, 1)

            G = PAGES + 1
            pe.sem_inc(kp_ready, 1)
            with pe.Fori(0, DB) as b:
                def scores(g):
                    n = P if g < PAGES else DS
                    wait_apart(pe, passed_pe, (kT_used[g % 2], (9, 8)[g % 2] * b + g // 2 + 1),
                               *([(ss_ready, b + 1)] if g == 0 else []))
                    for h in range(H):
                        out = ps[0:n, 3 + g // 8, (g % 8) * 64 + h * 16:(g % 8) * 64 + h * 16 + 16]
                        ins = pe.matmul(out, kT[:, g % 3, h * n:(h + 1) * n], q_pair[:, ds(b, 1), h, :].rearrange("p a s -> p (a s)"),
                                        start=True, stop=True)
                    ins.then_inc(kp_ready, 1)

                for g in range(G):
                    n = P if g < PAGES else DS
                    if g % 4 == 0 and g < PAGES:
                        pe.wait_ge(k_page[g // 4], 64 * b + 64)
                    if g == PAGES:
                        wait_apart(pe, passed_pe, (new_in, 32 * b + 32))
                    for h in range(H):
                        src = kring[:, g // 4, g % 4, h * P:(h + 1) * P] if g < PAGES else k_new[:, h * P:(h + 1) * P]
                        ins = pe.transpose(ps[:, g % 3, h * n:(h + 1) * n], src, ident[0:n, 0:n])
                    ins.then_inc(kT_ready, 1)
                    if g >= 1:
                        scores(g - 1)
                scores(G - 1)
                wait_apart(pe, passed_pe, (mx_ready, b + 1))
                pe.transpose(ps[0:64, 6, 0:P], smax[:, 0, :], ident[:, :]).then_inc(mT_ready, 1)
                pe.wait_ge(md_ready, b + 1)
                pe.matmul(ps[:, 6, P:P + 64], ones[0:64, :], mdiag[:, :], start=True, stop=True).then_inc(mb_ready, 1)
                pe.wait_ge(ps_exp, 2 * b + 2)
                pe.wait_ge(so_used, b + 1)
                for g in range(G):
                    if g < PAGES:
                        pr, one, last = p_s[:, g, :], ones[:, :], False
                        if g % 4 == 0:
                            pe.wait_ge(v_page[g // 4], 64 * b + 64)
                    else:
                        pr, one, last = p_new[:, :], ones[0:DS, :], True
                    pe.matmul(ps[:, 7, 64:128], one, pr, start=(g == 0), stop=last, skip_group_check=True)
                    for h in range(H):
                        val = vring[:, g // 4, g % 4, h * P:(h + 1) * P] if g < PAGES else v_new[:, h * P:(h + 1) * P]
                        ins = pe.matmul(ps[:, 7, h * 16:(h + 1) * 16], val, pr[:, h * 16:(h + 1) * 16],
                                        start=False, stop=last, skip_group_check=True)
                    if g < PAGES and g % 4 == 3:
                        ins.then_inc(v_used, 1)
                ins.then_inc(so_ready, 1)
            barrier(pe, 2)

            pe.wait_ge(st_in, 16)
            for j in range(4):
                ins = pe.transpose(ps[:, 7, j * 2 * DB:(j + 1) * 2 * DB], st_rows[:, j * P:(j + 1) * P], ident[0:2 * DB, 0:2 * DB])
            ins.then_inc(stT_ready, 1)
            for h in range(H):
                pe.wait_ge(sq_ready, h + 1)
                for c0, c1 in TS:
                    ins = pe.matmul(acc(h % 2)[:, c0:c1], ones[:, :], sq0[:, c0:c1], start=True, stop=True)
                ins.then_inc(sq_sum, 1)
            pe.wait_ge(ul_ready, 4)
            pe.wait_ge(stT_rows, 1)
            for j in range(4):
                ins = pe.transpose(ps[0:2 * DB + 2, 7, j * P:(j + 1) * P], u_last[:, j, :], ident[:, :])
            ins.then_inc(ulT_ready, 1)
            barrier(pe, 3)

            with pe.Fori(0, D // CH // 2) as j:
                for s in range(2):
                    pe.wait_ge(po.lo, 2 * j + s + 1)
                    for t in range(NT + 1):
                        n = (NT + 1) * s + t
                        pe.wait_ge(po.acc_used, 2 * (NT + 1) * j + max(n - 5, 0) + 1)
                        c0 = t * P if t < NT else TOK - P
                        for k in range(KT):
                            ins = split_product(ps[:, n % 6, 0:CH], xh[:, k, c0:c0 + P], xl[:, k, c0:c0 + P],
                                                wh[:, s, k, :], wl[:, s, k, :], k, k == KT - 1)
                        ins.then_inc(po.acc_ready, 1)
            barrier(pe, 4)
            transposes(norms[1])
            project(projs[1], NCH1, norms[1], 1)
            barrier(pe, 5)

            def front(c, s, use):
                pe.wait_ge(g_in[s], 64 * (use + 1))
                pe.wait_ge(e_exp, 9 * c)
                pe.matmul(ps[:, 0, :], lr_c[:, s, :], w_up[:, :], start=True, stop=True).then_inc(z_ready, 1)
                if not (isinstance(c, int) and c == 0):
                    pe.wait_ge(st_ready, GH * c)
                for n in range(2):
                    for m in range(4):
                        ins = pe.transpose(ps[:, 2 + n, m * P:(m + 1) * P], v_c[:, s, 4 * n + m, :], ident[:, :])
                    ins.then_inc(vT_ready, 1)
                pe.wait_ge(la_ready, c + 1)

            def decay(c, l, mat):
                pe.wait_ge(e_exp, 9 * c + max(l - 1, 0))
                for h in range(GH):
                    ins = pe.matmul(ps[:, (1 + l) % 2, h * P:(h + 1) * P], la[:, h * P:(h + 1) * P], decay_m[:, mat, :], start=True, stop=True)
                ins.then_inc(e_ready, 1)

            def out_proj(c):
                pe.wait_ge(ml_ready, c + 1)
                for n in range(2):
                    for k in range(KT):
                        cs_ = slice(n * 512, (n + 1) * 512)
                        ins = split_product(ps[:, 4 + n, :], mh[:, k, :], ml[:, k, :], woh[:, k, cs_], wol[:, k, cs_], k, k == KT - 1)
                    ins.then_inc(y_ready, 1)

            def pair_products(c, s, i, diag):
                if i < 2:
                    pe.wait_ge(y_used, max_prev(c))
                else:
                    pe.wait_ge(a_used, 8 * c + i - 1)
                if not diag:
                    pe.wait_ge(x_ready, 7 * c + i + 1)
                for h in range(GH):
                    lt = qk_c[:, s, GH + h, :] if diag else xlev[:, i % 2, h, :]
                    rt = qk_c[:, s, h, :] if diag else xlev[:, i % 2, h, :]
                    ins = pe.matmul(ps[:, 4 + i % 2, h * P:(h + 1) * P], lt, rt, start=True, stop=True)
                ins.then_inc(a_ready, 1)

            def max_prev(c):
                return 2 * c

            def mats(L):
                return [0, 1] + list(range(2, 9)) if L == 7 else [9, 10, 6, 7, 8]

            def middle(c, s, L):
                m = mats(L)
                for i in range(L):
                    if i + 4 < L + 2:
                        decay(c, i + 4, m[i + 4])
                    pair_products(c, s, i, False)
                pe.wait_ge(q_scaled, c + 1)
                pair_products(c, s, L, True)
                pe.wait_ge(ks_ready, c + 1)
                pe.wait_ge(v_ready, 2 * c + 2)
                for h in range(GH):
                    ins = pe.transpose(ps[:, 2, h * P:(h + 1) * P], ks[:, h, :], ident[:, :])
                ins.then_inc(ksT_ready, 1)
                pe.wait_ge(a_used, 8 * c + L + 1)
                pe.wait_ge(qb_ready, c + 1)
                if not (isinstance(c, int) and c == 0):
                    pe.wait_ge(m_mixed, c)
                    pe.wait_ge(st_ready, GH * c)

            def out_prompt(c):
                for h in range(GH):
                    for d in range(2):
                        v0 = h * DV + d * P
                        out = ps[:, 6 + d, h * P:(h + 1) * P]
                        pe.matmul(out, v_tok[:, v0:v0 + P], aT[:, h, :], start=True, stop=False)
                        ins = pe.matmul(out, st_g[:, h, d * P:(d + 1) * P], qb[:, h, :], start=False, stop=True)
                ins.then_inc(oT_ready, 1)
                pe.wait_ge(kst_ready, c + 1)
                for h in range(GH):
                    ins = pe.matmul(ps[:, 2 + h // 2, (h % 2) * DV:(h % 2 + 1) * DV], kst[:, h * P:(h + 1) * P], v_tok[:, h * DV:(h + 1) * DV],
                                    start=True, stop=True)
                ins.then_inc(sd_ready, 1)

            def out_sample(c):
                for h in range(GH):
                    for d in range(2):
                        v0 = h * DV + d * P
                        pe.matmul(ps[:, 6 + d, h * P:(h + 1) * P], v_tok[:, v0:v0 + P], aT[:, h, :],
                                  start=(h == 0), stop=False, skip_group_check=True)
                for b in range(DB):
                    pe.wait_ge(s0_in[b % 2], 16 * (b // 2 + 1))
                    i0 = P - NS + b * DS
                    for h in range(GH):
                        for d in range(2):
                            ins = pe.matmul(ps[:, 6 + d, h * P + i0:h * P + i0 + DS], s0_b[:, b % 2, h, d * P:(d + 1) * P],
                                            qb[:, h, i0:i0 + DS], start=False, stop=(b == DB - 1), skip_group_check=True)
                    if b == DB - 1:
                        ins.then_inc(oT_ready, 1)
                    if b == 0:
                        pe.wait_ge(kst_ready, c + 1)
                    else:
                        pe.wait_ge(s0_new, b)
                    pe.wait_ge(vm_ready, b + 1)
                    for h in range(GH):
                        ins = pe.matmul(ps[:, 2 + h // 2, (h % 2) * DV:(h % 2 + 1) * DV], kst[:, h * P:(h + 1) * P], v_m[:, h * DV:(h + 1) * DV],
                                        start=True, stop=True)
                    ins.then_inc(sdb_ready, 1)

            def row_sums(c):
                pe.wait_ge(sq1_ready, 2 * c + 2)
                for h in range(GH):
                    for d in range(2):
                        ins = pe.matmul(ps[:, 5, h * P:(h + 1) * P], ones[:, :], sq1[:, d, h, :], start=(d == 0), stop=(d == 1))
                ins.then_inc(r_ready, 1)

            def chunk(c, s, use, L=7):
                m = mats(L)
                front(c, s, use)
                for l in range(4):
                    decay(c, l, m[l])
                if not (isinstance(c, int) and c == 0):
                    out_proj(c - 1)
                middle(c, s, L)
                if isinstance(c, int) and c == NT:
                    out_sample(c)
                else:
                    out_prompt(c)
                row_sums(c)

            pe.wait_ge(up_in, 32)
            pe.wait_ge(g_zero, 1)
            chunk(0, 0, 0)
            pe.wait_ge(wo_lo, D // P)
            with pe.Fori(0, NT // 2 - 1) as j:
                chunk(2 * j + 1, 1, j)
                chunk(2 * j + 2, 0, j + 1)
            chunk(NT - 1, 1, NT // 2 - 1)
            chunk(NT, 0, NT // 2, 3)
            out_proj(NT)
            barrier(pe, 6)


_INS = ['x_prompt', 'x_sample', 'cache_k', 'cache_v', 'state_conv', 'state_gla', 'page_table', 'norm_w', 'norm_f',
        'w_in_even', 'w_out_even', 'diff_lambda', 'diff_subln_w', 'conv_w', 'w_in_odd', 'w_gate_up', 'b_gate',
        'gla_norm_w', 'w_out_odd']


def kernel(**inputs):
    import numpy as _np
    import concourse.bacc as _bacc
    from concourse import mybir as _mybir
    from concourse.bass_utils import run_bass_kernel_spmd as _run

    nc = _bacc.Bacc("TRN2", target_bir_lowering=False, num_devices=1)
    arrays, a = {}, {}
    for name in _INS:
        v = _np.ascontiguousarray(inputs[name])
        arrays[f"in_{name}"] = v
        a[name] = nc.dram_tensor(f"in_{name}", v.shape, _mybir.dt.from_np(v.dtype), kind="ExternalInput").ap()
    B, T, D = inputs['x_prompt'].shape
    b, t, _ = inputs['x_sample'].shape
    L, _, _, H, K = inputs['cache_k'].shape
    V = inputs['cache_v'].shape[4]
    _, _, C1, CW = inputs['state_conv'].shape
    LO, _, GH, GK, GV = inputs['state_gla'].shape
    shapes = {
        'y_prompt': (B, T, D), 'y_sample': (b, t, D),
        'k_prompt': (L, B, T, H, K), 'v_prompt': (L, B, T, H, V),
        'k_sample': (L, b, t, H, K), 'v_sample': (L, b, t, H, V),
        'conv_prompt': (L, B, C1, CW), 'conv_sample': (L, b, C1, CW),
        'gla_prompt': (LO, B, GH, GK, GV), 'gla_sample': (LO, b, GH, GK, GV),
    }
    f32 = _mybir.dt.float32
    o = {n: nc.dram_tensor(f"out_{n}", s, f32, kind="ExternalOutput").ap() for n, s in shapes.items()}
    scr = [nc.dram_tensor(f"act{l}", (m * 128, T + b * t), f32, kind="Internal").ap() for l, m in ((0, 32), (1, 25))]
    build_step(nc, a, o, scr)
    r = _run(nc, [arrays], core_ids=[0])
    return tuple(r.results[0][f"out_{n}"] for n in shapes)
```

```python
import math
from contextlib import ExitStack

import concourse.bass as bass
from concourse import mybir

F32 = mybir.dt.float32
F32R = mybir.dt.float32r
BF16 = mybir.dt.bfloat16
I32 = mybir.dt.int32
ACT = mybir.ActivationFunctionType
ALU = mybir.AluOpType
AX = mybir.AxisListType.X
ds = bass.ds

P = 128
EPS = 1e-5
NEG = -1e30


class Chain:

    def __init__(self, eng, sem):
        self.eng, self.sem, self.base, self.k = eng, sem, 0, 0

    def link(self, ins):
        ins.then_inc(self.sem, 1)
        self.k += 1
        self.eng.wait_ge(self.sem, self.base + self.k)

    def enter(self, i, per, first=0):
        self.start = self.base + self.k
        self.base, self.k, self.per = i * per + (self.start - first * per), 0, per

    def leave(self, trips):
        assert self.k == self.per, (self.k, self.per)
        self.base, self.k = self.start + trips * self.per, 0


def build_step(nc, a, o, scr):
    D = a["norm_w"].shape[1]
    SEQ = a["x_prompt"].shape[1]
    DB, DS = a["x_sample"].shape[:2]
    NS = DB * DS
    TOK = SEQ + NS
    NT = SEQ // P
    KT = D // P
    PAGES = a["page_table"].shape[1]
    NPHYS, PAGE = a["cache_k"].shape[1:3]
    H = a["cache_k"].shape[3]
    DH = a["cache_k"].shape[4] // 2
    HW = H * 2 * DH
    DV = a["state_gla"].shape[4]
    GH = a["state_gla"].shape[2]
    CW = a["conv_w"].shape[2]
    CH = 256
    NCH0 = a["w_in_even"].shape[2] // CH
    NCH1 = (a["w_in_odd"].shape[2] - 16) // CH
    ODD = a["w_in_odd"].shape[2]
    GATES = (3, NCH0 // 2 - 1)
    SC = DH ** -0.5
    LAM0 = 0.8 - 0.6 * math.exp(0.0)
    QK_SC = float(P) ** -0.5
    HALVES = [64, 32, 16, 8, 4, 2, 1]
    assert P == PAGE and NS == 64 and HW == 512 and D == 1024 and GH == H == 4
    NQ = H * 2 * DS
    QB = NQ + 2 * DS
    UP = 2 + SEQ
    UW = UP + DB * (2 + DS) - 2
    TS = [(0, 512), (512, 1024), (1024, TOK)]

    act0, act1 = scr
    a0 = act0.rearrange("(m p) t -> m p t", p=P)
    a1 = act1.rearrange("(m p) t -> m p t", p=P)

    top = ExitStack()
    with top:
        def sem(n):
            return top.enter_context(nc.semaphore(n))

        def sb(n, shape, dt=F32, where=top):
            return where.enter_context(nc.sbuf_tensor(n, shape, dt))

        ident = sb("ident", [P, P])
        ones = sb("ones", [P, P])
        identb = sb("identb", [P, P], BF16)
        causal = sb("causal", [P, P], BF16)
        new_mask = sb("new_mask", [DS, H * 2 * DS])
        decay_m = sb("decay_m", [P, 11, P])
        lvl_mask = sb("lvl_mask", [P, 7, P])
        norm_bc = sb("norm_bc", [P, D])
        vec_rows = sb("vec_rows", [15, P])
        vec = sb("vec", [P, 15])
        lam_s = sb("lam_s", [P, 4])
        neg_lam = lam_s[:, 3:4]
        eps_b = sb("eps_b", [P, 1])
        ssq = sb("ssq", [P, NT + 1])
        rstd = sb("rstd", [P, NT + 1])
        pages_sb = sb("pages_sb", [1, DB * PAGES], I32)
        u_last = sb("u_last", [P, 4, 2 * DB + 2])
        st_T = sb("st_T", [P, 4, 2 * DB])
        x1 = sb("x1", [P, NT + 1, D])
        attT = sb("attT", [P, H, TOK])

        pj = ExitStack()
        xh = sb("xh", [P, KT, TOK], F32R, pj)
        xl = sb("xl", [P, KT, TOK], F32R, pj)
        wraw = sb("wraw", [P, 2, KT, CH], F32, pj)
        wh = sb("wh", [P, 2, KT, CH], F32R, pj)
        wl = sb("wl", [P, 2, KT, CH], F32R, pj)
        stage = sb("stage", [P, 2, TOK], F32, pj)
        xs = sb("xs", [P, 2, D], F32, pj)
        gate_e = xs[:, :, :].rearrange("p s d -> p (s d)")[:, 0:TOK]
        st_rows = stage[0:2 * DB, 0, 0:CW]
        lam_in = stage[:, 1, 0:4 * DH].rearrange("p (a d) -> p a d", a=4)
        lam_pr = stage[:, 1, 4 * DH:6 * DH].rearrange("p (a d) -> p a d", a=2)
        pj.close()

        at = ExitStack()
        q_pair = sb("q_pair", [P, DB, H, 2 * DS], F32, at)
        q_b = sb("q_b", [P, H * QB], F32, at)
        kring = sb("kring", [P, 4, 4, HW], F32, at)
        cb = ExitStack()
        cin = sb("cin", [P, 4, TOK], F32, cb)
        u_pad = sb("u_pad", [P, UW + 2], F32, cb)
        conv = sb("conv", [P, UW], F32, cb)
        tap_u = sb("tap_u", [P, UW], F32, cb)
        cb.close()
        vring = sb("vring", [P, 4, 4, HW], F32, at)
        hd = ExitStack()
        q_in = sb("q_in", [P, TOK], F32, hd)
        k_in = sb("k_in", [P, TOK], F32, hd)
        v_in = sb("v_in", [P, TOK], F32, hd)
        k_row = sb("k_row", [P, NT + 1, P], F32, hd)
        v_row = sb("v_row", [P, NT + 1, P], F32, hd)
        prob = sb("prob", [P, 2, 2, SEQ], F32, hd)
        probT = sb("probT", [P, 2, SEQ], F32, hd)
        row_st = sb("row_st", [P, 2, 6], F32, hd)
        hd.close()
        k_new = sb("k_new", [DS, HW], F32, at)
        v_new = sb("v_new", [DS, HW], F32, at)
        kT = sb("kT", [P, 2, H, 4 * P], F32, at)
        kT_new = sb("kT_new", [P, H, DS], F32, at)
        p_s = sb("p_s", [NQ, PAGES * P + DS], F32, at)
        pT = sb("pT", [P, PAGES, NQ], F32, at)
        pT_new = sb("pT_new", [DS, NQ], F32, at)
        s_max = sb("s_max", [NQ, 6], F32, at)
        s_sum = sb("s_sum", [NQ, 6], F32, at)
        s_sign = sb("s_sign", [NQ, 3], F32, at)
        s_pick = sb("s_pick", [NQ, H, DS], F32, at)
        s_out = sb("s_out", [NQ, HW], F32, at)
        at.close()

        gt = ExitStack()
        xh_ = sb("xh_hold", [P, 2 * KT, TOK], F32, gt)
        branch = sb("branch", [P, 2 * H, TOK], F32, gt)
        sq0 = sb("sq0", [P, 2, TOK], F32, gt)
        rs0 = sb("rs0", [P, 2, TOK], F32, gt)
        att_g = sb("att_g", [P, 2, TOK], F32, gt)
        u_rows = sb("u_rows", [2 * DB + 2, CW], F32, gt)
        gt.close()

        gl = ExitStack()
        woh = sb("woh", [P, KT, D], F32R, gl)
        wol = sb("wol", [P, KT, D], F32R, gl)
        qk_c = sb("qk_c", [P, 2, 2 * GH, P], F32, gl)
        v_c = sb("v_c", [P, 2, 2 * GH, P], F32, gl)
        g_c = sb("g_c", [P, 2, 2 * GH, P], F32, gl)
        lr_c = sb("lr_c", [17, 2, P], F32, gl)
        w_up = sb("w_up", [17, GH * P], F32, gl)
        zt = sb("zt", [P, GH * P], F32, gl)
        la = sb("la", [P, GH * P], F32, gl)
        ee = sb("ee", [P, 2, GH, P], F32, gl)
        e_last = sb("e_last", [P, GH, DB], F32, gl)
        qb = sb("qb", [P, GH, P], F32, gl)
        ks = sb("ks", [P, GH, P], F32, gl)
        kst = sb("kst", [P, GH * P], F32, gl)
        xlev = sb("xlev", [P, 2, GH, P], F32, gl)
        aT = sb("aT", [P, GH, P], F32, gl)
        v_tok = sb("v_tok", [P, GH * DV], F32, gl)
        st_g = sb("st_g", [P, GH, DV], F32, gl)
        sq1 = sb("sq1", [P, 2, GH, P], F32, gl)
        rs1 = sb("rs1", [P, GH * P], F32, gl)
        sg = sb("sg", [P, 2 * GH, P], F32, gl)
        mh = sb("mh", [P, 2 * GH, P], F32R, gl)
        ml = sb("ml", [P, 2 * GH, P], F32R, gl)
        gl.close()
        free = attT[:, :, :].rearrange("p h t -> p (h t)")
        s0_b = free[:, 0:2 * GH * DV].rearrange("p (s h v) -> p s h v", s=2, h=GH)
        wo_raw = free[:, 0:2 * KT * P].rearrange("p (s k n) -> p s k n", s=2, k=KT)
        v_m = free[:, 2 * GH * DV:3 * GH * DV]
        y_o = v_m
        mt = free[:, 3 * GH * DV:4 * GH * DV].rearrange("p (m t) -> p m t", t=P)

        ps = top.enter_context(nc.psum_tensor("ps", [P, 8, 512], F32))

        phase_end = sem("phase_end")
        passed_pe, passed_dve, passed_pool = sem("passed_pe"), sem("passed_dve"), sem("passed_pool")
        passed_sp = sem("passed_sp")
        x_in = [sem("x_in0"), sem("x_in1")]
        norm_in = sem("norm_in")
        vec_in = sem("vec_in")
        vecT_ready = sem("vecT_ready")
        lam_ready = sem("lam_ready")
        lam_exp = sem("lam_exp")
        act_step = sem("act_step")
        dve_step = sem("dve_step")
        pool_step = sem("pool_step")
        block = top.enter_context(nc.Block())
        def rd(t):
            return t.bitcast(F32)

        def wait_apart(eng, passed, *waits):
            for q, n in waits:
                eng.wait_ge(q, n)
            eng.sem_inc(passed, 1)

        class Norm:
            def __init__(self, l):
                self.rstd = sem(f"n{l}_rstd")
                self.xs_ready = sem(f"n{l}_xs_ready")
                self.T_ready = sem(f"n{l}_T_ready")
                self.hi = sem(f"n{l}_hi")
                self.lo = sem(f"n{l}_lo")

        class Proj:
            def __init__(self, l):
                self.raw_in = [sem(f"p{l}_raw_in{s}") for s in range(2)]
                self.hi = sem(f"p{l}_hi")
                self.lo = sem(f"p{l}_lo")
                self.acc_ready = sem(f"p{l}_acc_ready")
                self.acc_used = sem(f"p{l}_acc_used")
                self.stored = [sem(f"p{l}_stored{s}") for s in range(2)]

        norms = [Norm(0), Norm(1)]
        projs = [Proj(0), Proj(1)]
        po = Proj(2)

        def barrier(eng, n):
            eng.drain().then_inc(phase_end, 1)
            eng.wait_ge(phase_end, 5 * (n + 1))

        def cols(m):
            return ds(m * P, P)

        att_in = sem("att_in")
        kv_T = sem("kv_T")
        kv_out = sem("kv_out")
        rows_ready = sem("rows_ready")
        probT_ready = sem("probT_ready")
        s_ready = sem("s_ready")
        m_ready = sem("m_ready")
        p_exp = sem("p_exp")
        p_mix = sem("p_mix")
        o_ready = sem("o_ready")
        o_used = sem("o_used")
        qp_zero = sem("qp_zero")
        pt_in = sem("pt_in")
        k_page = [sem(f"k_page{s}") for s in range(4)]
        v_page = [sem(f"v_page{s}") for s in range(4)]
        new_in = sem("new_in")
        kT_ready = sem("kT_ready")
        kT_used = [sem("kT_used_act"), sem("kT_used_dve")]
        q_ready = sem("q_ready")
        sc_ready = sem("sc_ready")
        mx_ready = sem("mx_ready")
        ps_exp = sem("ps_exp")
        pT_ready = sem("pT_ready")
        pT_used = [sem("pT_used_dve"), sem("pT_used_act")]
        v_used = sem("v_used")
        so_ready = sem("so_ready")
        so_scaled = sem("so_scaled")
        sp_ready = sem("sp_ready")
        gates_in = sem("gates_in")
        products_in = sem("products_in")
        cv_in = sem("cv_in")
        cv_out = sem("cv_out")
        sq_ready = sem("sq_ready")
        sq_sum = sem("sq_sum")
        rs_ready = sem("rs_ready")
        ge_ready = sem("ge_ready")
        mixed = sem("mixed")
        mix_hi = sem("mix_hi")
        br_hi = sem("br_hi")
        st_in = sem("st_in")
        stT_ready = sem("stT_ready")
        stT_rows = sem("stT_rows")
        u_ready = sem("u_ready")
        ulT_ready = sem("ulT_ready")
        ul_rows = sem("ul_rows")
        conv_out = sem("conv_out")
        wo_in = [sem(f"wo_in{s}") for s in range(2)]
        wo_hi = sem("wo_hi")
        wo_lo = sem("wo_lo")
        up_in = sem("up_in")
        g_in = [sem(f"g_in{s}") for s in range(2)]
        g_zero = sem("g_zero")
        g_ones = sem("g_ones")
        ge_gla = sem("ge_gla")
        sg_one = sem("sg_one")
        sg_rec = sem("sg_rec")
        sg_ready = sem("sg_ready")
        z_ready = sem("z_ready")
        z_abs = sem("z_abs")
        la_ready = sem("la_ready")
        vT_ready = sem("vT_ready")
        v_ready = sem("v_ready")
        e_ready = sem("e_ready")
        e_exp = sem("e_exp")
        q_scaled = sem("q_scaled")
        x_ready = sem("x_ready")
        a_ready = sem("a_ready")
        a_used = sem("a_used")
        ks_ready = sem("ks_ready")
        ksT_ready = sem("ksT_ready")
        kst_ready = sem("kst_ready")
        qb_ready = sem("qb_ready")
        oT_ready = sem("oT_ready")
        sd_ready = sem("sd_ready")
        st_ready = sem("st_ready")
        sq1_ready = sem("sq1_ready")
        r_ready = sem("r_ready")
        rs1_ready = sem("rs1_ready")
        m_mixed = sem("m_mixed")
        mh_ready = sem("mh_ready")
        ml_ready = sem("ml_ready")
        y_ready = sem("y_ready")
        y_used = sem("y_used")
        y_rstd = sem("y_rstd")
        y_norm = sem("y_norm")
        y_out = sem("y_out")
        s0_in = [sem(f"s0_in{s}") for s in range(2)]
        s0_out = [sem(f"s0_out{s}") for s in range(2)]
        vm_ready = sem("vm_ready")
        sdb_ready = sem("sdb_ready")
        s0_new = sem("s0_new")
        gp_out = sem("gp_out")

        xp_v = a["x_prompt"][0].rearrange("(t p) d -> p t d", p=P)
        xs_v = a["x_sample"].rearrange("b s d -> (b s) d")
        w0_v = a["w_in_even"][0].rearrange("(k p) n -> p k n", p=P)
        w1_v = a["w_in_odd"][0].rearrange("(k p) n -> p k n", p=P)
        wo0_v = a["w_out_even"][0].rearrange("(k p) n -> p k n", p=P)
        wo1_v = a["w_out_odd"][0].rearrange("(k p) n -> p k n", p=P)
        kp_o = o["k_prompt"][0, 0].rearrange("(t p) h d -> p t h d", p=P)
        vp_o = o["v_prompt"][0, 0].rearrange("(t p) h d -> p t h d", p=P)
        ks_o = o["k_sample"][0].rearrange("b s h d -> (b s) h d")
        vs_o = o["v_sample"][0].rearrange("b s h d -> (b s) h d")
        ks_b = o["k_sample"][0].rearrange("b s h d -> b s (h d)")
        vs_b = o["v_sample"][0].rearrange("b s h d -> b s (h d)")
        ck = a["cache_k"][0].rearrange("n p h d -> n p (h d)")
        cv_ = a["cache_v"][0].rearrange("n p h d -> n p (h d)")
        yp_o = o["y_prompt"][0].rearrange("(t p) d -> t p d", p=P)
        ys_o = o["y_sample"].rearrange("b s d -> (b s) d")

        def acc(m):
            return ps[:, 3 * m:3 * m + 3, :].rearrange("p a b -> p (a b)")

        @block.sync
        def _(sp):
            sp.dma_start(x1[:, 0:4, :], xp_v[:, 0:4, :]).then_inc(x_in[0], 16)
            sp.dma_start(norm_bc[:, :], a["norm_w"][0:1, :].to_broadcast([P, D])).then_inc(norm_in, 16)
            sp.dma_start(x1[:, 4:NT, :], xp_v[:, 4:NT, :]).then_inc(x_in[1], 16)
            sp.dma_start(x1[64:P, NT, :], xs_v).then_inc(x_in[1], 16)
            sp.dma_start(vec_rows[0:12, :], a["conv_w"][0].rearrange("k (j p) -> (k j) p", p=P)).then_inc(vec_in, 16)
            sp.dma_start(vec_rows[12:13, :], a["diff_subln_w"]).then_inc(vec_in, 16)
            sp.dma_start(vec_rows[13:15, :], a["gla_norm_w"].rearrange("a (d p) -> (a d) p", p=P)).then_inc(vec_in, 16)
            sp.dma_start(stage[:, 1, 0:4 * DH],
                         a["diff_lambda"].rearrange("a b d -> a (b d)").to_broadcast([P, 4 * DH])).then_inc(vec_in, 16)
            sp.dma_start(st_rows, a["state_conv"][0].rearrange("b r c -> (b r) c")).then_inc(st_in, 16)
            sp.dma_start(pages_sb[:, :], a["page_table"].rearrange("(a b) g -> a (b g)", a=1)).then_inc(pt_in, 16)

            def stream(p, view, n):
                for s in range(2):
                    sp.dma_start(wraw[:, s], view[:, :, s * CH:(s + 1) * CH]).then_inc(p.raw_in[s], 16)
                with sp.Fori(1, n // 2) as j:
                    for s in range(2):
                        sp.wait_ge(p.lo, 2 * j + s - 1)
                        sp.dma_start(wraw[:, s], view[:, :, ds((2 * j + s) * CH, CH)]).then_inc(p.raw_in[s], 16)

            stream(projs[0], w0_v, NCH0)
            barrier(sp, 0)

            def head_loads(h):
                if not (isinstance(h, int) and h == 0):
                    wait_apart(sp, passed_sp, (s_ready, NT * h))
                    wait_apart(sp, passed_sp, (rows_ready, 6 * h))
                for dst, first in ((q_in, 0), (k_in, 2 * H * DH)):
                    for half in range(2):
                        sp.dma_start(dst[half * DH:(half + 1) * DH, :],
                                     act0[ds(h * DH + first + half * H * DH, DH), :]).then_inc(att_in, 16)
                sp.dma_start(v_in[:, :], act0[ds(h * P + 4 * H * DH, P), :]).then_inc(att_in, 16)

            def key_pages(b, first):
                for s in range(4):
                    if not first:
                        sp.wait_ge(kT_ready, (PAGES + 1) * b + 4 * s + 4 - (PAGES + 1))
                    for g in range(4):
                        page = sp.value_load(pages_sb[0:1, ds(b * PAGES + 4 * s + g, 1)], min_val=0, max_val=NPHYS - 1)
                        sp.dma_start(kring[:, s, g, :], ck[ds(page, 1), :, :].rearrange("a p d -> p (a d)")).then_inc(k_page[s], 16)

            head_loads(0)
            sp.wait_ge(pt_in, 16)
            key_pages(0, True)
            with sp.Fori(1, H) as h:
                head_loads(h)
            barrier(sp, 1)

            with sp.Fori(1, DB) as b:
                key_pages(b, False)
            barrier(sp, 2)

            for u in range(2 * H):
                sp.dma_start(branch[:, u, :], a0[12 + u if u < H else 24 + u]).then_inc(gates_in if u < H else products_in, 16)
            sp.wait_ge(norms[0].xs_ready, NT + 1)
            sp.dma_start(norm_bc[:, :], a["norm_w"][1:2, :].to_broadcast([P, D])).then_inc(norm_in, 16)
            barrier(sp, 3)
            stream(po, wo0_v, D // CH)
            barrier(sp, 4)
            stream(projs[1], w1_v, NCH1)
            sp.wait_ge(projs[1].lo, NCH1 - 1)
            sp.dma_start(wraw[:, 0, :, 0:P], w1_v[:, :, ODD - P:ODD]).then_inc(projs[1].raw_in[0], 16)
            sp.wait_ge(norms[1].xs_ready, NT + 1)
            sp.dma_start(norm_bc[:, :], a["norm_f"].rearrange("(a d) -> a d", a=1).to_broadcast([P, D])).then_inc(norm_in, 16)
            barrier(sp, 5)

            def chunk_loads(s, lo, t0, n):
                for dst, m in ((qk_c, 0), (v_c, 2 * GH), (g_c, 4 * GH)):
                    sp.dma_start(dst[:, s, :, lo:P], a1[m:m + 2 * GH, :, ds(t0, n)].rearrange("m p t -> p m t")).then_inc(g_in[s], 16)
                sp.dma_start(lr_c[0:16, s, lo:P], act1[25 * P - 16:25 * P, ds(t0, n)]).then_inc(g_in[s], 16)

            def y_store(c):
                sp.wait_ge(y_norm, c + 1)
                if isinstance(c, int) and c == NT:
                    sp.dma_start(ys_o, y_o[P - NS:P, :]).then_inc(y_out, 16)
                else:
                    sp.dma_start(yp_o[ds(c, 1), :, :].rearrange("a p d -> p (a d)"), y_o[:, :]).then_inc(y_out, 16)

            sp.dma_start(w_up[0:16, :], a["w_gate_up"][0]).then_inc(up_in, 16)
            sp.dma_start(w_up[16:17, :], a["b_gate"]).then_inc(up_in, 16)
            sp.wait_ge(g_ones, 1)
            chunk_loads(0, 0, 0, P)
            for n in range(2):
                sp.dma_start(wo_raw[:, n], wo1_v[:, :, n * P:(n + 1) * P]).then_inc(wo_in[n], 16)
            chunk_loads(1, 0, P, P)
            for n in range(2, D // P):
                sp.wait_ge(wo_lo, n - 1)
                sp.dma_start(wo_raw[:, n % 2], wo1_v[:, :, n * P:(n + 1) * P]).then_inc(wo_in[n % 2], 16)
            with sp.Fori(0, NT // 2 - 1) as j:
                for s in range(2):
                    sp.wait_ge(m_mixed, 2 * j + s + 1)
                    chunk_loads(s, 0, (2 * j + s + 2) * P, P)
                    y_store(2 * j + s)
            sp.wait_ge(m_mixed, NT - 1)
            chunk_loads(0, P - NS, SEQ, NS)
            s0v = a["state_gla"][0].rearrange("b h k v -> b k h v")
            s0o = o["gla_sample"][0].rearrange("b h k v -> b k h v")
            for b in range(2):
                sp.dma_start(s0_b[:, b], s0v[b]).then_inc(s0_in[b], 16)
            y_store(NT - 2)
            y_store(NT - 1)
            for b in range(DB):
                sp.wait_ge(s0_new, b + 1)
                sp.dma_start(s0o[b], s0_b[:, b % 2]).then_inc(s0_out[b % 2], 16)
                if b + 2 < DB:
                    sp.wait_ge(s0_out[b % 2], 16 * (b // 2 + 1))
                    sp.dma_start(s0_b[:, b % 2], s0v[b + 2]).then_inc(s0_in[b % 2], 16)
            y_store(NT)
            sp.wait_ge(y_out, 16 * (NT + 1))
            for s in range(2):
                sp.wait_ge(s0_out[s], 16 * DB // 2)
            barrier(sp, 6)

        @block.gpsimd
        def _(pool):
            ch = Chain(pool, pool_step)

            def sel(view, pattern, base, mult, fill, op=ALU.is_ge):
                ch.link(pool.affine_select(out=view, in_=view, pattern=pattern, compare_op=op, fill=fill,
                                           base=base, channel_multiplier=mult))

            ch.link(pool.memset(x1[0:64, NT, :], 0.0))
            ch.link(pool.memset(eps_b[:, :], EPS))
            ch.link(pool.memset(ones[:, :], 1.0))
            ch.link(pool.memset(ident[:, :], 0.0))
            sel(ident[:, :], [[-1, P]], 0, 1, 1.0, ALU.not_equal)
            ch.link(pool.memset(identb[:, :], 0.0))
            sel(identb[:, :], [[-1, P]], 0, 1, 1.0, ALU.not_equal)
            ch.link(pool.memset(causal[:, :], 0.0))
            sel(causal[:, :], [[-1, P]], 0, 1, NEG)
            ch.link(pool.memset(new_mask[:, :], 0.0))
            nm = new_mask[:, :].rearrange("p (n i) -> p n i", i=DS)
            sel(nm, [[0, 2 * H], [1, DS]], 0, -1, NEG)
            ch.link(pool.memset(decay_m[:, :, :], 1.0))
            sel(decay_m[:, 0, :], [[1, P]], 0, -1, 0.0)
            sel(decay_m[:, 1, :], [[-1, P]], -1, 1, 0.0)
            blk = decay_m[:, 9, :].rearrange("p (n i) -> p n i", i=DS)
            sel(blk, [[DS, P // DS], [1, DS]], 0, -1, 0.0)
            sel(blk, [[-DS, P // DS], [0, DS]], 0, 1, 0.0)
            blk = decay_m[:, 10, :].rearrange("p (n i) -> p n i", i=DS)
            sel(blk, [[-DS, P // DS], [-1, DS]], -1, 1, 0.0)
            sel(blk, [[DS, P // DS], [0, DS]], DS - 1, -1, 0.0)
            ch.link(pool.memset(lvl_mask[:, :, :], 1.0))
            for l, hf in enumerate(HALVES):
                n = P // (2 * hf)
                v = decay_m[:, 2 + l, :].rearrange("p (n two r) -> p n two r", two=2, r=hf)
                sel(v[:, :, 1, :], [[-2 * hf, n], [0, hf]], -hf, 1, 0.0)
                sel(v[:, :, 1, :], [[2 * hf, n], [1, hf]], hf, -1, 0.0)
                sel(v[:, :, 0, :], [[-2 * hf, n], [-1, hf]], -1, 1, 0.0)
                sel(v[:, :, 0, :], [[2 * hf, n], [0, hf]], hf - 1, -1, 0.0)
                m = lvl_mask[:, l, :].rearrange("p (n two r) -> p n two r", two=2, r=hf)
                sel(m[:, :, 1, :], [[-2 * hf, n], [0, hf]], 0, 1, 0.0)
                sel(m[:, :, 1, :], [[2 * hf, n], [0, hf]], hf - 1, -1, 0.0)
                ch.link(pool.memset(m[:, :, 0, :], 0.0))
            n_const = ch.k

            def low_parts(p, n):
                with pool.Fori(0, n // 2) as j:
                    for s in range(2):
                        pool.wait_ge(p.hi, 2 * j + s + 1)
                        pool.tensor_tensor(wl[:, s], wraw[:, s], rd(wh[:, s]), ALU.subtract).then_inc(p.lo, 1)

            low_parts(projs[0], NCH0)
            barrier(pool, 0)

            ch.link(pool.memset(q_pair[:, :, :, :], 0.0))
            pool.memset(q_b[:, :], 0.0).then_inc(qp_zero, 1)

            def value_pages(b, first):
                for s in range(4):
                    if not first:
                        pool.wait_ge(v_used, 4 * b + s - 3)
                    for g in range(4):
                        page = pool.value_load(pages_sb[0:1, ds(b * PAGES + 4 * s + g, 1)], min_val=0, max_val=NPHYS - 1)
                        pool.dma_start(vring[:, s, g, :], cv_[ds(page, 1), :, :].rearrange("a p d -> p (a d)")).then_inc(v_page[s], 16)

            ch.link(pool.memset(u_pad[:, 0:2], 0.0))
            pool.wait_ge(stT_rows, 1)
            for h in range(H):
                pool.wait_ge(rows_ready, 6 * h + 6)
                pool.dma_start(kp_o[:, :, h, :], k_row[:, 0:NT, :]).then_inc(kv_out, 16)
                pool.dma_start(ks_o[:, h, :], k_row[64:P, NT, :]).then_inc(kv_out, 16)
                pool.dma_start(vp_o[:, :, h, :], v_row[:, 0:NT, :]).then_inc(kv_out, 16)
                pool.dma_start(vs_o[:, h, :], v_row[64:P, NT, :]).then_inc(kv_out, 16)
                if h:
                    pool.wait_ge(cv_out, 16 * h)
                for n in range(4):
                    pool.dma_start(cin[:, n, :], a0[16 + 4 * n + h]).then_inc(cv_in, 16)
                pool.wait_ge(cv_in, 64 * (h + 1))
                u_s = u_pad[:, UP:UP + DB * (2 + DS)].rearrange("p (b s) -> p b s", s=2 + DS)
                ch.link(pool.tensor_copy(u_s[:, :, 0:2], st_T[:, h, :].rearrange("p (b r) -> p b r", r=2)))
                ch.link(pool.tensor_tensor(u_s[:, :, 2:2 + DS], cin[:, 1, SEQ:TOK].rearrange("p (b s) -> p b s", s=DS),
                                           cin[:, 2, SEQ:TOK].rearrange("p (b s) -> p b s", s=DS), ALU.mult))
                ch.link(pool.tensor_tensor(u_pad[:, 2:UP], cin[:, 1, 0:SEQ], cin[:, 2, 0:SEQ], ALU.mult))
                ch.link(pool.tensor_copy(u_last[:, h, 0:2 * DB].rearrange("p (b r) -> p b r", r=2), u_s[:, :, DS:DS + 2]))
                ch.link(pool.tensor_copy(u_last[:, h, 2 * DB:2 * DB + 2], u_pad[:, SEQ:SEQ + 2]))
                for k in range(3):
                    dst = tap_u if k else conv
                    ch.link(pool.tensor_scalar(dst[:, :], u_pad[:, k:k + UW], vec[:, 4 * k + h:4 * k + h + 1], None, ALU.mult))
                    if k:
                        ch.link(pool.tensor_tensor(conv[:, :], conv[:, :], tap_u[:, :], ALU.add))
                ch.link(pool.tensor_tensor(cin[:, 3, :], cin[:, 3, :], cin[:, 0, :], ALU.mult))
                ch.link(pool.tensor_tensor(cin[:, 3, 0:SEQ], cin[:, 3, 0:SEQ], conv[:, 0:SEQ], ALU.mult))
                prod_s = cin[:, 3, SEQ:TOK].rearrange("p (b s) -> p b s", s=DS)
                for b in range(DB):
                    c0 = UP + b * (2 + DS)
                    ins = pool.tensor_tensor(prod_s[:, b, :], prod_s[:, b, :], conv[:, c0:c0 + DS], ALU.mult)
                ch.link(ins)
                pool.dma_start(a0[28 + h], cin[:, 3, :]).then_inc(cv_out, 16)
            pool.sem_inc(u_ready, 1)
            pool.wait_ge(cv_out, 16 * H)
            pool.wait_ge(kv_out, 64 * H)
            barrier(pool, 1)

            def new_rows(b):
                pool.dma_start(k_new[:, :], ks_b[ds(b, 1), :, :].rearrange("a s d -> (a s) d")).then_inc(new_in, 16)
                pool.dma_start(v_new[:, :], vs_b[ds(b, 1), :, :].rearrange("a s d -> (a s) d")).then_inc(new_in, 16)

            new_rows(0)
            value_pages(0, True)
            with pool.Fori(1, DB) as b:
                value_pages(b, False)
                pool.wait_ge(so_ready, b)
                new_rows(b)
            barrier(pool, 2)

            for j in range(4):
                pool.wait_ge(br_hi, j + 1)
                pool.tensor_tensor(xl[:, H + j, :], branch[:, H + j, :], rd(xh[:, H + j, :]), ALU.subtract)
            pool.wait_ge(ul_rows, 1)
            pool.dma_start(o["conv_sample"][0].rearrange("b r c -> (b r) c"), u_rows[0:2 * DB, :]).then_inc(conv_out, 16)
            pool.dma_start(o["conv_prompt"][0, 0], u_rows[2 * DB:2 * DB + 2, :]).then_inc(conv_out, 16)
            pool.wait_ge(conv_out, 32)
            barrier(pool, 3)
            low_parts(po, D // CH)
            barrier(pool, 4)
            low_parts(projs[1], NCH1)
            pool.wait_ge(projs[1].hi, NCH1 + 1)
            pool.tensor_tensor(wl[:, 0, :, 0:P], wraw[:, 0, :, 0:P], rd(wh[:, 0, :, 0:P]), ALU.subtract).then_inc(projs[1].lo, 1)
            barrier(pool, 5)

            pool.memset(lr_c[:, :, :], 1.0).then_inc(g_ones, 1)
            ch.link(pool.memset(st_g[:, :, :], 0.0))
            pool.memset(aT[:, :, :], 0.0).then_inc(g_zero, 1)
            for n in range(D // P):
                pool.wait_ge(wo_hi, n + 1)
                pool.tensor_tensor(wol[:, :, n * P:(n + 1) * P], wo_raw[:, n % 2],
                                   rd(woh[:, :, n * P:(n + 1) * P]), ALU.subtract).then_inc(wo_lo, 1)

            def chunk(c, s, t0, use):
                wait_apart(pool, passed_pool, (g_in[s], 64 * (use + 1)))
                pool.tensor_scalar(qk_c[:, s, 0:GH, :], qk_c[:, s, 0:GH, :], QK_SC, None, ALU.mult).then_inc(q_scaled, 1)
                wait_apart(pool, passed_pool, (ge_gla, c + 1))
                pool.tensor_scalar(sg[:, :, :], sg[:, :, :], 1.0, None, ALU.add).then_inc(sg_one, 1)
                wait_apart(pool, passed_pool, (e_exp, 9 * c + 1), (q_scaled, c + 1),
                           *([] if isinstance(c, int) and c == 0 else [(st_ready, GH * c)]))
                if isinstance(c, int) and c == NT:
                    ch.link(pool.tensor_copy(e_last[:, :, :], ee[:, 0, :, P - NS + DS - 1:P:DS]))
                else:
                    ch.link(pool.tensor_copy(e_last[:, :, 0:1], ee[:, 0, :, P - 1:P]))
                pool.tensor_tensor(qb[:, :, :], qk_c[:, s, 0:GH, :], ee[:, 0, :, :], ALU.mult).then_inc(qb_ready, 1)
                pool.wait_ge(e_exp, 9 * c + 2)
                pool.tensor_tensor(ks[:, :, :], qk_c[:, s, GH:2 * GH, :], ee[:, 1, :, :], ALU.mult).then_inc(ks_ready, 1)
                pool.wait_ge(sg_rec, c + 1)
                pool.tensor_tensor(sg[:, :, :], sg[:, :, :], g_c[:, s, :, :], ALU.mult).then_inc(sg_ready, 1)

            chunk(0, 0, 0, 0)
            with pool.Fori(0, NT // 2 - 1) as j:
                ch.enter(j, 2)
                chunk(2 * j + 1, 1, 0, j)
                chunk(2 * j + 2, 0, 0, j + 1)
            ch.leave(NT // 2 - 1)
            chunk(NT - 1, 1, 0, NT // 2 - 1)
            pool.wait_ge(st_ready, GH * NT)
            pool.dma_start(o["gla_prompt"][0, 0].rearrange("h k v -> k h v"), st_g[:, :, :]).then_inc(gp_out, 16)
            pool.wait_ge(oT_ready, NT)
            pool.memset(aT[:, :, :], 0.0).then_inc(g_zero, 1)
            chunk(NT, 0, P - NS, NT // 2)
            pool.wait_ge(gp_out, 16)
            barrier(pool, 6)

        @block.scalar
        def _(act):
            ch = Chain(act, act_step)

            def rsqrt(out, src, mean, sem_=None):
                ch.link(act.activation(out, src, ACT.Ln, bias=eps_b[:, :], scale=mean))
                ins = act.activation(out, out, ACT.Exp, scale=-0.5)
                ins.then_inc(sem_, 1)

            def norm_high(n):
                def high(t, slot, c0, n0):
                    for q in range(2):
                        act.wait_ge(n.T_ready, 2 * t + q + 1)
                        src = ps[:, 2 * slot + q, :].rearrange("p (k i) -> p k i", i=P)[:, :, P - n0:P]
                        act.activation(xh[:, 4 * q:4 * q + 4, ds(c0, n0)], src, ACT.Copy).then_inc(n.hi, 1)
                with act.Fori(0, NT // 2) as j:
                    for s in range(2):
                        high(2 * j + s, s, (2 * j + s) * P, P)
                high(NT, 0, SEQ, NS)

            def norm_stats(n):
                for t in range(NT + 1):
                    if n is norms[0] and t in (0, 4):
                        act.wait_ge(x_in[t // 4], 16 if t == 0 else 32)
                        if t == 4:
                            act.wait_ge(pool_step, 2)
                    ch.link(act.activation(xs[:, t % 2, :], x1[:, t, :], ACT.Square, accum_out=ssq[:, t:t + 1]))
                rsqrt(rstd[:, :], ssq[:, :], 1.0 / D, n.rstd)

            def high_parts(p, n, view, base, after=0, gates=()):
                def hi(j, s):
                    act.wait_ge(p.raw_in[s], 16 * (j + 1))
                    if not (isinstance(j, int) and j == 0):
                        act.wait_ge(p.acc_ready, base * (2 * j + s - 1))
                    act.activation(wh[:, s], wraw[:, s], ACT.Copy).then_inc(p.hi, 1)

                def store(j, s, gate=False):
                    if view is None:
                        return
                    for m in range(2):
                        u = 4 * j + 2 * s + m
                        if gate:
                            act.wait_ge(p.acc_ready, u + 1)
                            act.wait_ge(p.acc_used, u)
                            act.activation(gate_e, acc(m)[:, 0:TOK], ACT.Exp, scale=-1.0).then_inc(ge_ready, 1)
                        act.wait_ge(p.acc_used, u + 1)
                        act.dma_start(view[ds(u, 1), :, :].rearrange("a p t -> p (a t)"), stage[:, m]).then_inc(p.stored[m], 16)

                def pair(j, last_gate=False, gate=False):
                    hi(j, 0)
                    store(j - 1, 1, last_gate)
                    hi(j, 1)
                    store(j, 0, gate)

                hi(0, 0)
                hi(0, 1)
                store(0, 0)
                start = 1
                for g in (*gates, n // 2):
                    if start < g:
                        with act.Fori(start, g) as j:
                            pair(j)
                    start = g
                    if g < n // 2:
                        pair(g, False, True)
                        start = g + 1
                        if start < n // 2:
                            pair(start, True, False)
                            start += 1
                if after:
                    act.wait_ge(p.raw_in[0], 16 * (n // 2 + 1))
                    act.wait_ge(p.acc_ready, base * (n - 1))
                    act.activation(wh[:, 0, :, 0:P], wraw[:, 0, :, 0:P], ACT.Copy).then_inc(p.hi, 1)
                store(n // 2 - 1, 1, n // 2 - 1 in gates)
                if after:
                    act.wait_ge(p.acc_used, 2 * n + 1)
                    act.dma_start(view[2 * n], stage[:, 0]).then_inc(p.stored[0], 16)
                if view is not None:
                    act.wait_ge(p.stored[0], 16 * (n + after))
                    act.wait_ge(p.stored[1], 16 * n)

            act.wait_ge(vec_in, 64)
            act.wait_ge(lam_ready, 1)
            act.activation(lam_s[:, 0:2], lam_s[:, 0:2], ACT.Exp).then_inc(lam_exp, 1)
            norm_stats(norms[0])
            norm_high(norms[0])
            high_parts(projs[0], NCH0, a0, 2, gates=GATES)
            barrier(act, 0)

            def head(h):
                def group(n, dst, width, sem_):
                    act.wait_ge(kv_T, 18 * h + n + 1)
                    act.activation(dst, ps[:, 4 + n % 2, 0:width], ACT.Copy).then_inc(sem_, 1)

                act.wait_ge(kv_out, 64 * h)
                act.wait_ge(o_ready, NT * h)
                for n in range(6):
                    row, t0 = (k_row, v_row)[n // 3], 4 * (n % 3)
                    nt = min(4, NT + 1 - t0)
                    group(n, row[:, t0:t0 + nt, :].rearrange("p t d -> p (t d)"), nt * P, rows_ready)
                n = 6
                for i in range(NT):
                    nk = (i + 1) * P
                    act.wait_ge(m_ready, NT * h + i + 1)
                    for w in range(2):
                        ins = act.activation(prob[:, i % 2, w, 0:nk], ps[:, 2 * w:2 * w + 2, :].rearrange("p a b -> p (a b)")[:, 0:nk],
                                             ACT.Exp, bias=row_st[:, i % 2, 2 + w:3 + w], scale=SC,
                                             accum_out=row_st[:, i % 2, 4 + w:5 + w])
                        ins.then_inc(p_exp, 1)
                    if i >= 1:
                        n = tail(h, i - 1, n, group)
                tail(h, NT - 1, n, group)

            def tail(h, i, n, group):
                for t0 in range(0, i + 1, 4):
                    nt = min(4, i + 1 - t0)
                    group(n, probT[:, i % 2, t0 * P:(t0 + nt) * P], nt * P, probT_ready)
                    n += 1
                act.wait_ge(o_ready, NT * h + i + 1)
                act.activation(attT[:, ds(h, 1), i * P:(i + 1) * P].rearrange("p a t -> p (a t)"),
                               ps[:, 6 + i % 2, 0:P], ACT.Copy).then_inc(o_used, 1)
                return n

            head(0)
            with act.Fori(1, H) as h:
                head(h)
            barrier(act, 1)

            def key_page(b, g):
                act.wait_ge(kT_ready, (PAGES + 1) * b + g + 1)
                if g < PAGES:
                    s = g // 4
                    act.activation(kT[:, s % 2, :, (g % 4) * P:(g % 4 + 1) * P],
                                   ps[:, 0, :].rearrange("p (h k) -> p h k", h=H), ACT.Copy).then_inc(kT_used[0], 1)
                else:
                    act.activation(kT_new[:, :, :], ps[:, 0, 0:H * DS].rearrange("p (h k) -> p h k", h=H),
                                   ACT.Copy).then_inc(kT_used[0], 1)

            def batch(b, last):
                for g in range(8, PAGES + 1, 2):
                    key_page(b, g)
                if not last:
                    key_page(b + 1, 0)
                act.wait_ge(mx_ready, b + 1)
                for s in range(4):
                    act.activation(p_s[:, s * 512:(s + 1) * 512], ps[0:NQ, 2 + s, :], ACT.Exp, bias=s_max[:, 5:6], scale=SC,
                                   accum_out=s_sum[:, s:s + 1]).then_inc(ps_exp, 1)
                act.activation(p_s[:, PAGES * P:PAGES * P + DS], ps[0:NQ, 7, 0:DS], ACT.Exp, bias=s_max[:, 5:6], scale=SC,
                               accum_out=s_sum[:, 4:5]).then_inc(ps_exp, 1)
                if not last:
                    key_page(b + 1, 2)
                act.wait_ge(pT_ready, 3 * b + 3)
                act.activation(pT[:, 8:16, :].rearrange("p g q -> p (g q)"), ps[:, 3, :], ACT.Copy).then_inc(pT_used[1], 1)
                if not last:
                    key_page(b + 1, 4)
                    key_page(b + 1, 6)

            for g in range(0, 8, 2):
                key_page(0, g)
            with act.Fori(0, DB - 1) as b:
                batch(b, False)
            batch(DB - 1, True)
            barrier(act, 2)

            def squares(h):
                if h >= 2:
                    act.wait_ge(sq_sum, h - 1)
                act.activation(sq0[:, h % 2, :], attT[:, h, :], ACT.Square).then_inc(sq_ready, 1)

            squares(0)
            squares(1)
            for h in range(H):
                act.wait_ge(sq_sum, h + 1)
                if h >= 2:
                    act.wait_ge(mixed, h - 1)
                rsqrt(rs0[:, h % 2, :], acc(h % 2)[:, 0:TOK], 1.0 / P, rs_ready)
                act.wait_ge(products_in, 16 * H)
                act.activation(xh[:, H + h, :], branch[:, H + h, :], ACT.Copy).then_inc(br_hi, 1)
                if h + 2 < H:
                    squares(h + 2)
                act.wait_ge(mixed, h + 1)
                act.activation(xh[:, h, :], att_g[:, h % 2, :], ACT.Copy).then_inc(mix_hi, 1)
            barrier(act, 3)
            high_parts(po, D // CH, None, NT + 1)
            barrier(act, 4)
            norm_stats(norms[1])
            norm_high(norms[1])
            high_parts(projs[1], NCH1, a1, 2, 1)
            barrier(act, 5)

            for n in range(D // P):
                act.wait_ge(wo_in[n % 2], 16 * (n // 2 + 1))
                act.activation(woh[:, :, n * P:(n + 1) * P], wo_raw[:, n % 2], ACT.Copy).then_inc(wo_hi, 1)

            def front(c, s, use, levels):
                act.wait_ge(z_ready, c + 1)
                ch.link(act.activation(zt[:, :], ps[:, 0, :], ACT.Abs))
                ch.link(act.activation(zt[:, :], zt[:, :], ACT.Exp, scale=-1.0))
                act.activation(zt[:, :], zt[:, :], ACT.Ln, bias=1.0).then_inc(z_abs, 1)
                for n in range(2):
                    act.wait_ge(vT_ready, 2 * c + n + 1)
                    act.activation(v_tok[:, n * 512:(n + 1) * 512], ps[:, 2 + n, :], ACT.Copy).then_inc(v_ready, 1)
                act.wait_ge(g_in[s], 64 * (use + 1))
                if not (isinstance(c, int) and c == 0):
                    act.wait_ge(m_mixed, c)
                act.activation(sg[:, :, :], g_c[:, s, :, :], ACT.Exp, scale=-1.0).then_inc(ge_gla, 1)
                exps(c, 0, 2)

            def exps(c, l0, l1):
                for l in range(l0, l1):
                    act.wait_ge(e_ready, 9 * c + l + 1)
                    if l >= 4:
                        act.wait_ge(x_ready, 7 * c + l - 3)
                    elif l >= 2:
                        act.wait_ge((qb_ready, ks_ready)[l - 2], c + 1)
                    else:
                        act.wait_ge(x_ready, 7 * c)
                    act.activation(ee[:, l % 2, :, :].rearrange("p h i -> p (h i)"), ps[:, (1 + l) % 2, :],
                                   ACT.Exp, scale=1.0 / 16).then_inc(e_exp, 1)

            def gated(c):
                act.wait_ge(m_mixed, c + 1)
                act.wait_ge(y_ready, 2 * c)
                act.activation(mh[:, :, :], mt[:, :, :], ACT.Copy).then_inc(mh_ready, 1)

            def final(c, t):
                act.wait_ge(y_used, 2 * c + 2)
                if not (isinstance(c, int) and c == 0):
                    act.wait_ge(y_norm, c)
                    act.wait_ge(y_out, 16 * c)
                ch.link(act.activation(y_o[:, :], x1[:, ds(t, 1), :].rearrange("p a d -> p (a d)"), ACT.Square, accum_out=ssq[:, 0:1]))
                rsqrt(rstd[:, 0:1], ssq[:, 0:1], 1.0 / D, y_rstd)

            def back(c):
                act.wait_ge(ksT_ready, c + 1)
                act.activation(kst[:, :], ps[:, 2, :], ACT.Copy).then_inc(kst_ready, 1)
                act.wait_ge(oT_ready, c + 1)
                for d in range(2):
                    act.activation(sq1[:, d, :, :].rearrange("p h i -> p (h i)"), ps[:, 6 + d, :], ACT.Square).then_inc(sq1_ready, 1)

            def r1(c):
                act.wait_ge(r_ready, c + 1)
                rsqrt(rs1[:, :], ps[:, 5, :], 1.0 / DV, rs1_ready)

            def body(c, s, use, L=9):
                r1(c - 1)
                front(c, s, use, L)
                gated(c - 1)
                exps(c, 2, 4)
                if L > 4:
                    exps(c, 4, 6 if L > 6 else L)
                final(c - 1, c - 1)
                if L > 6:
                    exps(c, 6, L)
                back(c)

            front(0, 0, 0, 9)
            exps(0, 2, 9)
            back(0)
            with act.Fori(0, NT // 2 - 1) as j:
                ch.enter(j, 2 * 5)
                body(2 * j + 1, 1, j)
                body(2 * j + 2, 0, j + 1)
            ch.leave(NT // 2 - 1)
            body(NT - 1, 1, NT // 2 - 1)
            body(NT, 0, NT // 2, 5)
            r1(NT)
            gated(NT)
            final(NT, NT)
            barrier(act, 6)

        @block.vector
        def _(v):
            ch = Chain(v, dve_step)

            def normalize(n, ready):
                def scale(t, s):
                    if not (isinstance(t, int) and t < 2):
                        v.wait_ge(n.T_ready, 2 * t - 2)
                    src = x1[:, ds(t, 1), :].rearrange("p a d -> p (a d)")
                    v.scalar_tensor_tensor(out=xs[:, s, :], in0=src, scalar=rstd_col(t), in1=norm_bc[:, :],
                                           op0=ALU.mult, op1=ALU.mult).then_inc(n.xs_ready, 1)

                def rstd_col(t):
                    return rstd[:, ds(t, 1)]

                def low(t, slot, c0, n0):
                    for q in range(2):
                        v.wait_ge(n.hi, 2 * t + q + 1)
                        src = ps[:, 2 * slot + q, :].rearrange("p (k i) -> p k i", i=P)[:, :, P - n0:P]
                        v.tensor_tensor(xl[:, 4 * q:4 * q + 4, ds(c0, n0)], src, rd(xh[:, 4 * q:4 * q + 4, ds(c0, n0)]),
                                        ALU.subtract).then_inc(n.lo, 1)

                v.wait_ge(n.rstd, 1)
                v.wait_ge(norm_in, ready)
                scale(0, 0)
                scale(1, 1)
                with v.Fori(0, NT // 2 - 1) as j:
                    for s in range(2):
                        low(2 * j + s, s, (2 * j + s) * P, P)
                        scale(2 * j + s + 2, s)
                low(NT - 2, 0, (NT - 2) * P, P)
                scale(NT, 0)
                low(NT - 1, 1, (NT - 1) * P, P)
                low(NT, 0, SEQ, NS)

            def units_out(p, n, after=0, gates=()):
                def unit(j, s, m, gate=False):
                    v.wait_ge(p.acc_ready, 4 * j + 2 * s + m + 1)
                    if not (isinstance(j, int) and j == 0 and s == 0):
                        v.wait_ge(p.stored[m], 16 * (2 * j + s))
                    if gate:
                        v.wait_ge(ge_ready, 4 * gates.index(j) + 2 * s + m + 1)
                        ch.link(v.tensor_scalar(gate_e, gate_e, 1.0, None, ALU.add))
                        ch.link(v.reciprocal(gate_e, gate_e))
                        v.tensor_tensor(stage[:, m], acc(m)[:, 0:TOK], gate_e, ALU.mult).then_inc(p.acc_used, 1)
                    else:
                        v.tensor_copy(stage[:, m], acc(m)[:, 0:TOK]).then_inc(p.acc_used, 1)

                def pair(j, gate=False):
                    for s in range(2):
                        for m in range(2):
                            unit(j, s, m, gate)

                pair(0)
                start = 1
                for g in (*gates, n // 2):
                    if start < g:
                        with v.Fori(start, g) as j:
                            pair(j)
                    if g < n // 2:
                        pair(g, True)
                    start = g + 1
                if after:
                    unit(n // 2, 0, 0)

            v.wait_ge(vec_in, 64)
            lp = lam_in.rearrange("p (a b) d -> p a b d", b=2)
            ch.link(v.tensor_tensor(lam_pr, lp[:, :, 0, :], lp[:, :, 1, :], ALU.mult))
            v.tensor_reduce(lam_s[:, 0:2], lam_pr, AX, ALU.add).then_inc(lam_ready, 1)
            v.wait_ge(lam_exp, 1)
            ch.link(v.scalar_tensor_tensor(out=neg_lam, in0=lam_s[:, 1:2], scalar=LAM0, in1=lam_s[:, 0:1],
                                           op0=ALU.subtract, op1=ALU.subtract))
            v.wait_ge(vecT_ready, 1)
            ch.link(v.tensor_copy(vec[:, :], ps[:, 7, 0:15]))
            ch.link(v.tensor_scalar(vec[:, 12:13], vec[:, 12:13], 1.0 - LAM0, None, ALU.mult))
            v.wait_ge(stT_ready, 1)
            v.tensor_copy(st_T[:, :, :], ps[:, 6, 0:8 * DB].rearrange("p (j r) -> p j r", r=2 * DB)).then_inc(stT_rows, 1)
            normalize(norms[0], 16)
            units_out(projs[0], NCH0, gates=GATES)
            barrier(v, 0)

            v.wait_ge(qp_zero, 1)

            def head(h):
                v.wait_ge(att_in, 80 * h + 80)
                for w in range(2):
                    r = slice(w * DH, (w + 1) * DH)
                    ch.link(v.tensor_copy(q_pair[r, :, ds(h, 1), w * DS:(w + 1) * DS].rearrange("p b a s -> p b (a s)"),
                                          q_in[r, SEQ:TOK].rearrange("p (b s) -> p b s", s=DS)))
                for i in range(NT):
                    nk = (i + 1) * P
                    st = row_st[:, i % 2, :]
                    v.wait_ge(s_ready, NT * h + i + 1)
                    for w in range(2):
                        ch.link(v.tensor_reduce(st[:, w:w + 1], ps[:, 2 * w:2 * w + 2, :].rearrange("p a b -> p (a b)")[:, 0:nk], AX, ALU.max))
                    v.tensor_scalar(st[:, 2:4], st[:, 0:2], -SC, None, ALU.mult).then_inc(m_ready, 1)
                    v.wait_ge(p_exp, 2 * (NT * h + i + 1))
                    ch.link(v.reciprocal(st[:, 4:6], st[:, 4:6]))
                    ch.link(v.tensor_scalar(st[:, 5:6], st[:, 5:6], neg_lam, None, ALU.mult))
                    ch.link(v.tensor_scalar(prob[:, i % 2, 0, 0:nk], prob[:, i % 2, 0, 0:nk], st[:, 4:5], None, ALU.mult))
                    v.scalar_tensor_tensor(out=prob[:, i % 2, 0, 0:nk], in0=prob[:, i % 2, 1, 0:nk], scalar=st[:, 5:6],
                                           in1=prob[:, i % 2, 0, 0:nk], op0=ALU.mult, op1=ALU.add).then_inc(p_mix, 1)

            head(0)
            with v.Fori(1, H) as h:
                ch.enter(h, 2 + 5 * NT, 1)
                head(h)
            ch.leave(H - 1)
            barrier(v, 1)

            idv = ident[0:NQ, 0:NQ].rearrange("p (h w s) -> p h w s", h=H, w=2)
            ch.link(v.tensor_tensor(s_pick[:, :, :], idv[:, :, 0, :], idv[:, :, 1, :], ALU.add))
            ch.link(v.tensor_reduce(s_sign[:, 0:1], idv[:, :, 1, :], mybir.AxisListType.XY, ALU.add))
            ch.link(v.tensor_scalar(s_sign[:, 1:2], neg_lam[0:NQ], -1.0, None, ALU.add))
            ch.link(v.tensor_scalar(s_sign[:, 2:3], s_sign[:, 0:1], s_sign[:, 1:2], 1.0, ALU.mult, ALU.add))

            def key_page(b, g):
                s = g // 4
                v.wait_ge(kT_ready, (PAGES + 1) * b + g + 1)
                v.tensor_copy(kT[:, s % 2, :, (g % 4) * P:(g % 4 + 1) * P],
                              ps[:, 1, :].rearrange("p (h k) -> p h k", h=H)).then_inc(kT_used[1], 1)

            def batch_query(b):
                v.tensor_copy(q_b[:, :].rearrange("p (h c) -> p h c", h=H)[:, :, 0:2 * DS],
                              q_pair[:, ds(b, 1), :, :].rearrange("p a h c -> p (a h) c")).then_inc(q_ready, 1)

            def group_max(b, s):
                v.wait_ge(sc_ready, 5 * b + s + 1)
                src = ps[0:NQ, 2 + s, :] if s < 4 else ps[0:NQ, 7, 0:DS]
                ch.link(v.tensor_reduce(s_max[:, s:s + 1], src, AX, ALU.max))

            def batch(b, last):
                group_max(b, 0)
                key_page(b, 9)
                key_page(b, 11)
                group_max(b, 1)
                key_page(b, 13)
                key_page(b, 15)
                for s in range(2, 5):
                    group_max(b, s)
                ch.link(v.tensor_reduce(s_max[:, 5:6], s_max[:, 0:5], AX, ALU.max))
                v.tensor_scalar(s_max[:, 5:6], s_max[:, 5:6], -SC, None, ALU.mult).then_inc(mx_ready, 1)
                if not last:
                    batch_query(b + 1)
                    key_page(b + 1, 1)
                    key_page(b + 1, 3)
                v.wait_ge(pT_ready, 3 * b + 3)
                v.tensor_copy(pT[:, 0:8, :].rearrange("p g q -> p (g q)"), ps[:, 2, :]).then_inc(pT_used[0], 1)
                v.tensor_copy(pT_new[:, :], ps[0:DS, 7, 64:64 + NQ]).then_inc(pT_used[0], 1)
                v.wait_ge(ps_exp, 5 * b + 5)
                ch.link(v.tensor_reduce(s_sum[:, 5:6], s_sum[:, 0:5], AX, ALU.add))
                ch.link(v.reciprocal(s_sum[:, 5:6], s_sum[:, 5:6]))
                ch.link(v.tensor_tensor(s_sum[:, 5:6], s_sum[:, 5:6], s_sign[:, 2:3], ALU.mult))
                v.wait_ge(so_ready, b + 1)
                v.tensor_scalar(s_out[:, :], ps[0:NQ, 6, :], s_sum[:, 5:6], None, ALU.mult).then_inc(so_scaled, 1)
                if not last:
                    key_page(b + 1, 5)
                    key_page(b + 1, 7)
                v.wait_ge(sp_ready, b + 1)
                v.tensor_copy(attT[:, :, ds(b * DS + SEQ, DS)],
                              ps[:, 7, 128:128 + H * DS].rearrange("p (h s) -> p h s", h=H))

            batch_query(0)
            for g in range(1, 8, 2):
                key_page(0, g)
            with v.Fori(0, DB - 1) as b:
                ch.enter(b, 9)
                batch(b, False)
            ch.leave(DB - 1)
            batch(DB - 1, True)
            barrier(v, 2)

            def lows(h):
                v.wait_ge(mix_hi, h + 1)
                ch.link(v.tensor_tensor(xl[:, h, :], att_g[:, h % 2, :], rd(xh[:, h, :]), ALU.subtract))

            for h in range(H):
                v.wait_ge(rs_ready, h + 1)
                ch.link(v.scalar_tensor_tensor(out=att_g[:, h % 2, :], in0=attT[:, h, :], scalar=vec[:, 12:13], in1=rs0[:, h % 2, :],
                                               op0=ALU.mult, op1=ALU.mult))
                v.wait_ge(gates_in, 16 * H)
                v.tensor_tensor(att_g[:, h % 2, :], att_g[:, h % 2, :], branch[:, h, :], ALU.mult).then_inc(mixed, 1)
                if h:
                    lows(h - 1)
            lows(H - 1)
            v.wait_ge(ulT_ready, 1)
            v.tensor_copy(u_rows[:, :], ps[0:2 * DB + 2, 7, :]).then_inc(ul_rows, 1)
            barrier(v, 3)

            v.sem_inc(po.acc_used, 1)
            with v.Fori(0, D // CH // 2) as j:
                for s in range(2):
                    for t in range(NT + 1):
                        n = (NT + 1) * s + t
                        r = slice(0, P) if t < NT else slice(64, P)
                        v.wait_ge(po.acc_ready, 2 * (NT + 1) * j + n + 1)
                        x = x1[r, t, ds((2 * j + s) * CH, CH)]
                        v.tensor_tensor(x, ps[r, n % 6, 0:CH], x, ALU.add).then_inc(po.acc_used, 1)
            barrier(v, 4)
            normalize(norms[1], 32)
            units_out(projs[1], NCH1, 1)
            barrier(v, 5)

            def gate(c):
                v.wait_ge(rs1_ready, c + 1)
                v.wait_ge(mh_ready, c)
                for d in range(2):
                    out = mt.rearrange("p (h d) i -> p h d i", d=2)[:, :, d, :]
                    ch.link(v.scalar_tensor_tensor(out=out, in0=ps[:, 6 + d, :].rearrange("p (h i) -> p h i", i=P),
                                                   scalar=vec[:, 13 + d:14 + d], in1=rs1[:, :].rearrange("p (h i) -> p h i", i=P),
                                                   op0=ALU.mult, op1=ALU.mult))
                v.wait_ge(sg_ready, c + 1)
                v.tensor_tensor(mt, mt, sg[:, :, :], ALU.mult).then_inc(m_mixed, 1)

            def log_decay(c):
                v.wait_ge(z_abs, c + 1)
                v.scalar_tensor_tensor(out=la[:, :], in0=ps[:, 0, :], scalar=0.0, in1=zt[:, :],
                                       op0=ALU.min, op1=ALU.subtract).then_inc(la_ready, 1)
                v.wait_ge(sg_one, c + 1)
                v.reciprocal(sg[:, :, :], sg[:, :, :]).then_inc(sg_rec, 1)

            def level(c, s, i, hf):
                v.wait_ge(e_exp, 9 * c + i + 3)
                v.wait_ge(q_scaled, c + 1)
                v.wait_ge(a_ready, 8 * c + max(i - 1, 0))
                e = ee[:, i % 2, :, :].rearrange("p h (n two r) -> p (h n) two r", two=2, r=hf)
                x = xlev[:, i % 2, :, :].rearrange("p h (n two r) -> p (h n) two r", two=2, r=hf)
                for w, m0 in ((0, GH), (1, 0)):
                    src = qk_c[:, s, m0:m0 + GH, :].rearrange("p h (n two r) -> p (h n) two r", two=2, r=hf)
                    ins = v.tensor_tensor(x[:, :, w, :], src[:, :, w, :], e[:, :, w, :], ALU.mult)
                    if w == 0:
                        ch.link(ins)
                    else:
                        ins.then_inc(x_ready, 1)

            def pairs(c, i, mask):
                m = mask.bitcast(I32).to_broadcast([P, GH, P])
                wait_apart(v, passed_dve, (a_ready, 8 * c + i + 1), (a_used, 8 * c + i))
                v.copy_predicated(aT[:, :, :], m, ps[:, 4 + i % 2, :].rearrange("p (h i) -> p h i", i=P)).then_inc(a_used, 1)

            def low(c):
                v.wait_ge(mh_ready, c + 1)
                v.wait_ge(y_ready, 2 * c)
                v.tensor_tensor(ml[:, :, :], mt, rd(mh[:, :, :]), ALU.subtract).then_inc(ml_ready, 1)

            def residual(c, t, r):
                for n in range(2):
                    v.wait_ge(y_ready, 2 * c + n + 1)
                    x = x1[r, ds(t, 1), n * 512:(n + 1) * 512].rearrange("p a d -> p (a d)")
                    v.tensor_tensor(x, ps[r, 4 + n, :], x, ALU.add).then_inc(y_used, 1)

            def out_norm(c, t):
                v.wait_ge(y_rstd, c + 1)
                v.scalar_tensor_tensor(out=y_o[:, :], in0=x1[:, ds(t, 1), :].rearrange("p a d -> p (a d)"), scalar=rstd[:, 0:1],
                                       in1=norm_bc[:, :], op0=ALU.mult, op1=ALU.mult).then_inc(y_norm, 1)

            def levels(c, s, halves, after_first=None):
                L = len(halves)
                first = HALVES.index(halves[0])
                v.wait_ge(g_zero, 2 if isinstance(c, int) and c == NT else 1)
                v.wait_ge(oT_ready, c)
                for i in range(L + 1):
                    pairs(c, i, lvl_mask[:, first + i:first + i + 1, :] if i < L else ident[:, None, :])
                    if i + 2 < L:
                        level(c, s, i + 2, halves[i + 2])

            def state(c):
                v.wait_ge(sd_ready, c + 1)
                for h in range(GH):
                    v.scalar_tensor_tensor(out=st_g[:, h, :], in0=st_g[:, h, :], scalar=e_last[:, h, 0:1],
                                           in1=ps[:, 2 + h // 2, (h % 2) * DV:(h % 2 + 1) * DV],
                                           op0=ALU.mult, op1=ALU.add).then_inc(st_ready, 1)

            def body(c, s, halves):
                gate(c - 1)
                log_decay(c)
                low(c - 1)
                level(c, s, 0, halves[0])
                level(c, s, 1, halves[1])
                residual(c - 1, c - 1, slice(0, P))
                levels(c, s, halves)
                out_norm(c - 1, c - 1)

            v.wait_ge(norm_in, 48)
            log_decay(0)
            v.wait_ge(g_zero, 1)
            level(0, 0, 0, HALVES[0])
            level(0, 0, 1, HALVES[1])
            levels(0, 0, HALVES)
            state(0)
            with v.Fori(0, NT // 2 - 1) as j:
                ch.enter(j, 2 * (2 + 7))
                body(2 * j + 1, 1, HALVES)
                state(2 * j + 1)
                body(2 * j + 2, 0, HALVES)
                state(2 * j + 2)
            ch.leave(NT // 2 - 1)
            body(NT - 1, 1, HALVES)
            state(NT - 1)
            body(NT, 0, HALVES[4:])
            for b in range(DB):
                i = P - NS + b * DS + DS - 1
                if b:
                    v.wait_ge(sdb_ready, b)
                else:
                    v.wait_ge(y_out, 16 * NT)
                v.wait_ge(v_ready, 2 * NT + 2)
                v.tensor_scalar(v_m, v_tok[:, :], decay_m[:, 9, i:i + 1], None, ALU.mult).then_inc(vm_ready, 1)
                v.wait_ge(sdb_ready, b + 1)
                for h in range(GH):
                    ins = v.scalar_tensor_tensor(out=s0_b[:, b % 2, h, :], in0=s0_b[:, b % 2, h, :], scalar=e_last[:, h, b:b + 1],
                                                 in1=ps[:, 2 + h // 2, (h % 2) * DV:(h % 2 + 1) * DV],
                                                 op0=ALU.mult, op1=ALU.add)
                ins.then_inc(s0_new, 1)
            gate(NT)
            low(NT)
            residual(NT, NT, slice(64, P))
            out_norm(NT, NT)
            barrier(v, 6)

        @block.tensor
        def _(pe):
            def transposes(n):
                def tile(t, s):
                    pe.wait_ge(n.xs_ready, t + 1)
                    if not (isinstance(t, int) and t < 2):
                        pe.wait_ge(n.lo, 2 * t - 2)
                    for q in range(2):
                        for k in range(4):
                            ins = pe.transpose(ps[:, 2 * s + q, k * P:(k + 1) * P], xs[:, s, (4 * q + k) * P:(4 * q + k + 1) * P], ident[:, :])
                        ins.then_inc(n.T_ready, 1)
                tile(0, 0)
                tile(1, 1)
                with pe.Fori(1, NT // 2) as j:
                    tile(2 * j, 0)
                    tile(2 * j + 1, 1)
                tile(NT, 0)

            def split_product(out, lh, ll, rh, rl, k, last):
                pe.matmul(out, lh, rh, start=(k == 0), stop=False)
                pe.matmul(out, lh, rl, start=False, stop=False)
                return pe.matmul(out, ll, rh, start=False, stop=last)

            def project(p, n, norm, after=0):
                def unit(j, s, m):
                    if not (isinstance(j, int) and j == 0 and s == 0):
                        pe.wait_ge(p.acc_used, 4 * j + 2 * s + m - 1)
                    for k in range(KT):
                        w = (slice(None), s, k, slice(m * P, (m + 1) * P))
                        for wt, xt in ((wh, xh), (wh, xl), (wl, xh)):
                            for c0, c1 in TS:
                                ins = pe.matmul(acc(m)[:, c0:c1], wt[w], xt[:, k, c0:c1],
                                                start=(k == 0 and wt is wh and xt is xh),
                                                stop=(k == KT - 1 and wt is wl))
                    ins.then_inc(p.acc_ready, 1)

                def pair(j):
                    for s in range(2):
                        pe.wait_ge(p.lo, 2 * j + s + 1)
                        for m in range(2):
                            unit(j, s, m)

                pe.wait_ge(norm.lo, 2 * (NT + 1))
                pair(0)
                with pe.Fori(1, n // 2) as j:
                    pair(j)
                if after:
                    pe.wait_ge(p.lo, n + 1)
                    unit(n // 2, 0, 0)

            pe.wait_ge(pool_step, 5)
            pe.wait_ge(vec_in, 64)
            pe.transpose(ps[:, 7, 0:15], vec_rows[:, :], ident[0:15, 0:15]).then_inc(vecT_ready, 1)
            pe.wait_ge(st_in, 16)
            for j in range(4):
                ins = pe.transpose(ps[:, 6, j * 2 * DB:(j + 1) * 2 * DB], st_rows[:, j * P:(j + 1) * P], ident[0:2 * DB, 0:2 * DB])
            ins.then_inc(stT_ready, 1)
            transposes(norms[0])
            project(projs[0], NCH0, norms[0])
            barrier(pe, 0)

            def head(h):
                pe.wait_ge(att_in, 80 * h + 80)

                def bank_free(n):
                    if n < 2:
                        pe.wait_ge(probT_ready, 12 * h)
                    elif n < 8:
                        pe.wait_ge(rows_ready, 6 * h + n - 1)
                    else:
                        pe.wait_ge(probT_ready, 12 * h + n - 7)

                for n in range(6):
                    src, t0 = (k_in, v_in)[n // 3], 4 * (n % 3)
                    bank_free(n)
                    for t in range(t0, min(t0 + 4, NT + 1)):
                        c0 = t * P if t < NT else TOK - P
                        ins = pe.transpose(ps[:, 4 + n % 2, (t - t0) * P:(t - t0 + 1) * P], src[:, c0:c0 + P], ident[:, :])
                    ins.then_inc(kv_T, 1)

                def scores(i):
                    nk = (i + 1) * P
                    pe.wait_ge(p_exp, 2 * (NT * h + i))
                    for w in range(2):
                        r = slice(w * DH, (w + 1) * DH)
                        for b in range(0, nk, 512):
                            e = min(b + 512, nk)
                            bank = ps[:, 2 * w + b // 512, 0:e - b]
                            diag = e == nk
                            ins = pe.matmul(bank, q_in[r, i * P:(i + 1) * P], k_in[r, b:e], start=True, stop=not diag)
                            if diag:
                                ins = pe.matmul(bank[:, e - b - P:e - b], identb[:, :], causal[:, :], start=False, stop=True)
                    ins.then_inc(s_ready, 1)

                def values(i, n):
                    pe.wait_ge(p_mix, NT * h + i + 1)
                    for t0 in range(0, i + 1, 4):
                        bank_free(n)
                        for t in range(t0, min(t0 + 4, i + 1)):
                            ins = pe.transpose(ps[:, 4 + n % 2, (t - t0) * P:(t - t0 + 1) * P], prob[:, i % 2, 0, t * P:(t + 1) * P], ident[:, :])
                        ins.then_inc(kv_T, 1)
                        n += 1
                    pe.wait_ge(probT_ready, 12 * h + n - 6)
                    if i == 0:
                        pe.wait_ge(rows_ready, 6 * h + 6)
                    pe.wait_ge(o_used, NT * h + max(i - 1, 0))
                    for t in range(i + 1):
                        ins = pe.matmul(ps[:, 6 + i % 2, 0:P], v_row[:, t, :], probT[:, i % 2, t * P:(t + 1) * P],
                                        start=(t == 0), stop=(t == i))
                    ins.then_inc(o_ready, 1)
                    return n

                n = 6
                scores(0)
                for i in range(NT):
                    if i + 1 < NT:
                        scores(i + 1)
                    n = values(i, n)

            head(0)
            with pe.Fori(1, H) as h:
                head(h)
            barrier(pe, 1)

            def key_page(b, g):
                first = isinstance(b, int) and b == 0
                if g < PAGES and g % 4 == 0:
                    pe.wait_ge(k_page[g // 4], 64 * b + 64)
                if not (first and g < 2):
                    pe.wait_ge(kT_used[g % 2], (9, 8)[g % 2] * b + g // 2)
                n = P if g < PAGES else DS
                if g == PAGES:
                    wait_apart(pe, passed_pe, (new_in, 32 * b + 32))
                for h in range(H):
                    src = kring[:, g // 4, g % 4, h * P:(h + 1) * P] if g < PAGES else k_new[:, h * P:(h + 1) * P]
                    ins = pe.transpose(ps[:, g % 2, h * n:(h + 1) * n], src, ident[0:n, 0:n])
                ins.then_inc(kT_ready, 1)

            def key_group(b, s):
                for g in range(4 * s, 4 * s + 4):
                    key_page(b, g)

            def scores(b, s):
                if s == 0:
                    pe.wait_ge(q_ready, b + 1)
                if s < 4:
                    pe.wait_ge(kT_used[0], 9 * b + 2 * s + 2)
                    pe.wait_ge(kT_used[1], 8 * b + 2 * s + 2)
                else:
                    pe.wait_ge(kT_used[0], 9 * b + 9)
                out = ps[0:NQ, 2 + s, :] if s < 4 else ps[0:NQ, 7, 0:DS]
                for h in range(H):
                    keys = kT[:, s % 2, h, :] if s < 4 else kT_new[:, h, :]
                    ins = pe.matmul(out, q_b[:, h * NQ:(h + 1) * NQ], keys, start=(h == 0), stop=(s < 4 and h == H - 1))
                if s == 4:
                    ins = pe.matmul(out, new_mask[:, :], ident[0:DS, 0:DS], start=False, stop=True)
                ins.then_inc(sc_ready, 1)

            def batch(b, last):
                scores(b, 0)
                key_group(b, 2)
                scores(b, 1)
                key_group(b, 3)
                scores(b, 2)
                key_page(b, PAGES)
                scores(b, 3)
                scores(b, 4)
                if not last:
                    key_group(b + 1, 0)
                for n in range(2):
                    wait_apart(pe, passed_pe, (ps_exp, 5 * b + 2 * n + 2))
                    for g in range(8):
                        ins = pe.transpose(ps[:, 2 + n, g * NQ:(g + 1) * NQ], p_s[:, (8 * n + g) * P:(8 * n + g + 1) * P], ident[0:NQ, 0:NQ])
                    ins.then_inc(pT_ready, 1)
                wait_apart(pe, passed_pe, (ps_exp, 5 * b + 5))
                pe.transpose(ps[0:DS, 7, 64:64 + NQ], p_s[:, PAGES * P:PAGES * P + DS], ident[0:NQ, 0:NQ]).then_inc(pT_ready, 1)
                pe.wait_ge(pT_used[0], 2 * b + 2)
                for g in range(PAGES):
                    if g % 4 == 0:
                        pe.wait_ge(v_page[g // 4], 64 * b + 64)
                    if g == 8:
                        pe.wait_ge(pT_used[1], b + 1)
                    ins = pe.matmul(ps[0:NQ, 6, :], pT[:, g, :], vring[:, g // 4, g % 4, :], start=(g == 0), stop=False)
                    if g % 4 == 3:
                        ins.then_inc(v_used, 1)
                pe.matmul(ps[0:NQ, 6, :], pT_new[:, :], v_new[:, :], start=False, stop=True).then_inc(so_ready, 1)
                if not last:
                    key_group(b + 1, 1)
                pe.wait_ge(so_scaled, b + 1)
                for h in range(H):
                    ins = pe.matmul(ps[:, 7, 128 + h * DS:128 + (h + 1) * DS], s_out[:, h * P:(h + 1) * P], s_pick[:, h, :],
                                    start=True, stop=True)
                ins.then_inc(sp_ready, 1)

            key_group(0, 0)
            key_group(0, 1)
            with pe.Fori(0, DB - 1) as b:
                batch(b, False)
            batch(DB - 1, True)
            barrier(pe, 2)

            for h in range(H):
                pe.wait_ge(sq_ready, h + 1)
                if h >= 2:
                    pe.wait_ge(rs_ready, h - 1)
                for c0, c1 in TS:
                    ins = pe.matmul(acc(h % 2)[:, c0:c1], ones[:, :], sq0[:, h % 2, c0:c1], start=True, stop=True)
                ins.then_inc(sq_sum, 1)
            pe.wait_ge(u_ready, 1)
            for j in range(4):
                ins = pe.transpose(ps[0:2 * DB + 2, 7, j * P:(j + 1) * P], u_last[:, j, :], ident[:, :])
            ins.then_inc(ulT_ready, 1)
            barrier(pe, 3)

            with pe.Fori(0, D // CH // 2) as j:
                for s in range(2):
                    pe.wait_ge(po.lo, 2 * j + s + 1)
                    for t in range(NT + 1):
                        n = (NT + 1) * s + t
                        pe.wait_ge(po.acc_used, 2 * (NT + 1) * j + max(n - 5, 0) + 1)
                        c0 = t * P if t < NT else TOK - P
                        for k in range(KT):
                            ins = split_product(ps[:, n % 6, 0:CH], xh[:, k, c0:c0 + P], xl[:, k, c0:c0 + P],
                                                wh[:, s, k, :], wl[:, s, k, :], k, k == KT - 1)
                        ins.then_inc(po.acc_ready, 1)
            barrier(pe, 4)
            transposes(norms[1])
            project(projs[1], NCH1, norms[1], 1)
            barrier(pe, 5)

            def front(c, s, use):
                pe.wait_ge(g_in[s], 64 * (use + 1))
                pe.wait_ge(e_exp, 9 * c)
                pe.matmul(ps[:, 0, :], lr_c[:, s, :], w_up[:, :], start=True, stop=True).then_inc(z_ready, 1)
                if not (isinstance(c, int) and c == 0):
                    pe.wait_ge(st_ready, GH * c)
                for n in range(2):
                    for m in range(4):
                        ins = pe.transpose(ps[:, 2 + n, m * P:(m + 1) * P], v_c[:, s, 4 * n + m, :], ident[:, :])
                    ins.then_inc(vT_ready, 1)
                pe.wait_ge(la_ready, c + 1)

            def decay(c, l, mat):
                pe.wait_ge(e_exp, 9 * c + max(l - 1, 0))
                for h in range(GH):
                    ins = pe.matmul(ps[:, (1 + l) % 2, h * P:(h + 1) * P], la[:, h * P:(h + 1) * P], decay_m[:, mat, :], start=True, stop=True)
                ins.then_inc(e_ready, 1)

            def out_proj(c):
                pe.wait_ge(ml_ready, c + 1)
                for n in range(2):
                    for k in range(KT):
                        cs_ = slice(n * 512, (n + 1) * 512)
                        ins = split_product(ps[:, 4 + n, :], mh[:, k, :], ml[:, k, :], woh[:, k, cs_], wol[:, k, cs_], k, k == KT - 1)
                    ins.then_inc(y_ready, 1)

            def pair_products(c, s, i, diag):
                if i < 2:
                    pe.wait_ge(y_used, max_prev(c))
                else:
                    pe.wait_ge(a_used, 8 * c + i - 1)
                if not diag:
                    pe.wait_ge(x_ready, 7 * c + i + 1)
                for h in range(GH):
                    lt = qk_c[:, s, GH + h, :] if diag else xlev[:, i % 2, h, :]
                    rt = qk_c[:, s, h, :] if diag else xlev[:, i % 2, h, :]
                    ins = pe.matmul(ps[:, 4 + i % 2, h * P:(h + 1) * P], lt, rt, start=True, stop=True)
                ins.then_inc(a_ready, 1)

            def max_prev(c):
                return 2 * c

            def mats(L):
                return [0, 1] + list(range(2, 9)) if L == 7 else [9, 10, 6, 7, 8]

            def middle(c, s, L):
                m = mats(L)
                for i in range(L):
                    if i + 4 < L + 2:
                        decay(c, i + 4, m[i + 4])
                    pair_products(c, s, i, False)
                pe.wait_ge(q_scaled, c + 1)
                pair_products(c, s, L, True)
                pe.wait_ge(ks_ready, c + 1)
                pe.wait_ge(v_ready, 2 * c + 2)
                for h in range(GH):
                    ins = pe.transpose(ps[:, 2, h * P:(h + 1) * P], ks[:, h, :], ident[:, :])
                ins.then_inc(ksT_ready, 1)
                pe.wait_ge(a_used, 8 * c + L + 1)
                pe.wait_ge(qb_ready, c + 1)
                if not (isinstance(c, int) and c == 0):
                    pe.wait_ge(m_mixed, c)
                    pe.wait_ge(st_ready, GH * c)

            def out_prompt(c):
                for h in range(GH):
                    for d in range(2):
                        v0 = h * DV + d * P
                        out = ps[:, 6 + d, h * P:(h + 1) * P]
                        pe.matmul(out, v_tok[:, v0:v0 + P], aT[:, h, :], start=True, stop=False)
                        ins = pe.matmul(out, st_g[:, h, d * P:(d + 1) * P], qb[:, h, :], start=False, stop=True)
                ins.then_inc(oT_ready, 1)
                pe.wait_ge(kst_ready, c + 1)
                for h in range(GH):
                    ins = pe.matmul(ps[:, 2 + h // 2, (h % 2) * DV:(h % 2 + 1) * DV], kst[:, h * P:(h + 1) * P], v_tok[:, h * DV:(h + 1) * DV],
                                    start=True, stop=True)
                ins.then_inc(sd_ready, 1)

            def out_sample(c):
                for h in range(GH):
                    for d in range(2):
                        v0 = h * DV + d * P
                        pe.matmul(ps[:, 6 + d, h * P:(h + 1) * P], v_tok[:, v0:v0 + P], aT[:, h, :],
                                  start=(h == 0), stop=False, skip_group_check=True)
                for b in range(DB):
                    pe.wait_ge(s0_in[b % 2], 16 * (b // 2 + 1))
                    i0 = P - NS + b * DS
                    for h in range(GH):
                        for d in range(2):
                            ins = pe.matmul(ps[:, 6 + d, h * P + i0:h * P + i0 + DS], s0_b[:, b % 2, h, d * P:(d + 1) * P],
                                            qb[:, h, i0:i0 + DS], start=False, stop=(b == DB - 1), skip_group_check=True)
                    if b == DB - 1:
                        ins.then_inc(oT_ready, 1)
                    if b == 0:
                        pe.wait_ge(kst_ready, c + 1)
                    else:
                        pe.wait_ge(s0_new, b)
                    pe.wait_ge(vm_ready, b + 1)
                    for h in range(GH):
                        ins = pe.matmul(ps[:, 2 + h // 2, (h % 2) * DV:(h % 2 + 1) * DV], kst[:, h * P:(h + 1) * P], v_m[:, h * DV:(h + 1) * DV],
                                        start=True, stop=True)
                    ins.then_inc(sdb_ready, 1)

            def row_sums(c):
                pe.wait_ge(sq1_ready, 2 * c + 2)
                for h in range(GH):
                    for d in range(2):
                        ins = pe.matmul(ps[:, 5, h * P:(h + 1) * P], ones[:, :], sq1[:, d, h, :], start=(d == 0), stop=(d == 1))
                ins.then_inc(r_ready, 1)

            def chunk(c, s, use, L=7):
                m = mats(L)
                front(c, s, use)
                for l in range(4):
                    decay(c, l, m[l])
                if not (isinstance(c, int) and c == 0):
                    out_proj(c - 1)
                middle(c, s, L)
                if isinstance(c, int) and c == NT:
                    out_sample(c)
                else:
                    out_prompt(c)
                row_sums(c)

            pe.wait_ge(up_in, 32)
            pe.wait_ge(g_zero, 1)
            chunk(0, 0, 0)
            pe.wait_ge(wo_lo, D // P)
            with pe.Fori(0, NT // 2 - 1) as j:
                chunk(2 * j + 1, 1, j)
                chunk(2 * j + 2, 0, j + 1)
            chunk(NT - 1, 1, NT // 2 - 1)
            chunk(NT, 0, NT // 2, 3)
            out_proj(NT)
            barrier(pe, 6)


_INS = ['x_prompt', 'x_sample', 'cache_k', 'cache_v', 'state_conv', 'state_gla', 'page_table', 'norm_w', 'norm_f',
        'w_in_even', 'w_out_even', 'diff_lambda', 'diff_subln_w', 'conv_w', 'w_in_odd', 'w_gate_up', 'b_gate',
        'gla_norm_w', 'w_out_odd']


def kernel(**inputs):
    import numpy as _np
    import concourse.bacc as _bacc
    from concourse import mybir as _mybir
    from concourse.bass_utils import run_bass_kernel_spmd as _run

    nc = _bacc.Bacc("TRN2", target_bir_lowering=False, num_devices=1)
    arrays, a = {}, {}
    for name in _INS:
        v = _np.ascontiguousarray(inputs[name])
        arrays[f"in_{name}"] = v
        a[name] = nc.dram_tensor(f"in_{name}", v.shape, _mybir.dt.from_np(v.dtype), kind="ExternalInput").ap()
    B, T, D = inputs['x_prompt'].shape
    b, t, _ = inputs['x_sample'].shape
    L, _, _, H, K = inputs['cache_k'].shape
    V = inputs['cache_v'].shape[4]
    _, _, C1, CW = inputs['state_conv'].shape
    LO, _, GH, GK, GV = inputs['state_gla'].shape
    shapes = {
        'y_prompt': (B, T, D), 'y_sample': (b, t, D),
        'k_prompt': (L, B, T, H, K), 'v_prompt': (L, B, T, H, V),
        'k_sample': (L, b, t, H, K), 'v_sample': (L, b, t, H, V),
        'conv_prompt': (L, B, C1, CW), 'conv_sample': (L, b, C1, CW),
        'gla_prompt': (LO, B, GH, GK, GV), 'gla_sample': (LO, b, GH, GK, GV),
    }
    f32 = _mybir.dt.float32
    o = {n: nc.dram_tensor(f"out_{n}", s, f32, kind="ExternalOutput").ap() for n, s in shapes.items()}
    scr = [nc.dram_tensor(f"act{l}", (m * 128, T + b * t), f32, kind="Internal").ap() for l, m in ((0, 32), (1, 25))]
    build_step(nc, a, o, scr)
    r = _run(nc, [arrays], core_ids=[0])
    return tuple(r.results[0][f"out_{n}"] for n in shapes)
```

```python
import math
from contextlib import ExitStack

import concourse.bass as bass
from concourse import mybir

F32 = mybir.dt.float32
F32R = mybir.dt.float32r
BF16 = mybir.dt.bfloat16
I32 = mybir.dt.int32
ACT = mybir.ActivationFunctionType
ALU = mybir.AluOpType
AX = mybir.AxisListType.X
ds = bass.ds

P = 128
EPS = 1e-5
NEG = -1e30


class Chain:

    def __init__(self, eng, sem):
        self.eng, self.sem, self.base, self.k = eng, sem, 0, 0

    def link(self, ins):
        ins.then_inc(self.sem, 1)
        self.k += 1
        self.eng.wait_ge(self.sem, self.base + self.k)

    def enter(self, i, per, first=0):
        self.start = self.base + self.k
        self.base, self.k, self.per = i * per + (self.start - first * per), 0, per

    def leave(self, trips):
        assert self.k == self.per, (self.k, self.per)
        self.base, self.k = self.start + trips * self.per, 0


def build_step(nc, a, o, scr):
    D = a["norm_w"].shape[1]
    SEQ = a["x_prompt"].shape[1]
    DB, DS = a["x_sample"].shape[:2]
    NS = DB * DS
    TOK = SEQ + NS
    NT = SEQ // P
    KT = D // P
    PAGES = a["page_table"].shape[1]
    NPHYS, PAGE = a["cache_k"].shape[1:3]
    H = a["cache_k"].shape[3]
    DH = a["cache_k"].shape[4] // 2
    HW = H * 2 * DH
    DV = a["state_gla"].shape[4]
    GH = a["state_gla"].shape[2]
    CW = a["conv_w"].shape[2]
    CH = 256
    NCH0 = a["w_in_even"].shape[2] // CH
    NCH1 = (a["w_in_odd"].shape[2] - 16) // CH
    ODD = a["w_in_odd"].shape[2]
    ORDER0 = [(0, 4, 0), (4, 5, 6), (5, NCH0 // 2, -2)]
    ORDER1 = [0, 1, 2, 3, 8, 9, 10, 11, 4, 5, 6, 7]
    GATES = [(3, 4), (2, 3)]
    SC = DH ** -0.5
    LAM0 = 0.8 - 0.6 * math.exp(0.0)
    QK_SC = float(P) ** -0.5
    HALVES = [64, 32, 16, 8, 4, 2, 1]
    assert P == PAGE and NS == 64 and HW == 512 and D == 1024 and GH == H == 4
    NQ = H * 2 * DS
    QB = P + 2 * DS
    UP = 2 + SEQ
    UW = UP + DB * (2 + DS) - 2
    SG = 364
    TS = [(0, 512), (512, 1024), (1024, TOK)]

    act0, act1, log_a = scr
    la_d = log_a.rearrange("(t p) n -> t p n", p=P)
    a0 = act0.rearrange("(m p) t -> m p t", p=P)
    a1 = act1.rearrange("(m p) t -> m p t", p=P)

    top = ExitStack()
    with top:
        def sem(n):
            return top.enter_context(nc.semaphore(n))

        def sb(n, shape, dt=F32, where=top):
            return where.enter_context(nc.sbuf_tensor(n, shape, dt))

        ident = sb("ident", [P, P])
        ones = sb("ones", [P, P])
        identb = sb("identb", [P, P], BF16)
        causal = sb("causal", [P, P], BF16)
        new_mask = sb("new_mask", [DS, H * 2 * DS])
        decay_m = sb("decay_m", [P, 11, P])
        lvl_mask = sb("lvl_mask", [P, 7, P])
        norm_bc = sb("norm_bc", [P, D])
        vec_rows = sb("vec_rows", [15, P])
        vec = sb("vec", [P, 15])
        lam_s = sb("lam_s", [P, 4])
        neg_lam = lam_s[:, 3:4]
        eps_b = sb("eps_b", [P, 1])
        ssq = sb("ssq", [P, NT + 1])
        rstd = sb("rstd", [P, NT + 1])
        pages_sb = sb("pages_sb", [1, DB * PAGES], I32)
        u_last = sb("u_last", [P, 4, 2 * DB + 2])
        st_T = sb("st_T", [P, 4, 2 * DB])
        x1 = sb("x1", [P, NT + 1, D])
        attT = sb("attT", [P, H, TOK])

        pj = ExitStack()
        xh = sb("xh", [P, KT, TOK], F32R, pj)
        xl = sb("xl", [P, KT, TOK], F32R, pj)
        wraw = sb("wraw", [P, 2, KT, CH], F32, pj)
        wh = sb("wh", [P, 2, KT, CH], F32R, pj)
        wl = sb("wl", [P, 2, KT, CH], F32R, pj)
        stage = sb("stage", [P, 2, TOK], F32, pj)
        xs = sb("xs", [P, 2, D], F32, pj)
        gate_e = xs[:, :, :].rearrange("p s d -> p (s d)")[:, 0:TOK]
        st_rows = stage[0:2 * DB, 0, 0:CW]
        lam_in = stage[:, 1, 0:4 * DH].rearrange("p (a d) -> p a d", a=4)
        lam_pr = stage[:, 1, 4 * DH:6 * DH].rearrange("p (a d) -> p a d", a=2)
        pj.close()

        at = ExitStack()
        q_pair = sb("q_pair", [P, DB, H, 2 * DS], F32, at)
        q_b = sb("q_b", [P, H * QB], F32, at)
        q_bh = sb("q_bh", [P, H * QB], F32R, at)
        q_bl = sb("q_bl", [P, H * QB], F32R, at)
        kring = sb("kring", [P, 4, 4, HW], F32, at)
        cb = ExitStack()
        cin = sb("cin", [P, 4, TOK], F32, cb)
        u_pad = sb("u_pad", [P, UW + 2], F32, cb)
        conv = sb("conv", [P, UW], F32, cb)
        tap_u = sb("tap_u", [P, UW], F32, cb)
        cb.close()
        vring = sb("vring", [P, 4, 4, HW], F32, at)
        hd = ExitStack()
        q_in = sb("q_in", [P, TOK], F32, hd)
        k_in = sb("k_in", [P, TOK], F32, hd)
        v_in = sb("v_in", [P, TOK], F32, hd)
        k_row = sb("k_row", [P, NT + 1, P], F32, hd)
        v_row = sb("v_row", [P, NT + 1, P], F32, hd)
        prob = sb("prob", [P, 3, 2, SEQ], F32, hd)
        probT = sb("probT", [P, 2, SEQ], F32, hd)
        row_st = sb("row_st", [P, 2, 6], F32, hd)
        hd.close()
        k_new = sb("k_new", [DS, HW], F32, at)
        v_new = sb("v_new", [DS, HW], F32, at)
        kTh = sb("kTh", [P, 2, H, 4 * P], F32R, at)
        kTl = sb("kTl", [P, 2, H, 4 * P], F32R, at)
        kT_new = sb("kT_new", [P, H, DS], F32, at)
        p_s = sb("p_s", [NQ, PAGES * P + DS], F32, at)
        pT = sb("pT", [P, PAGES, NQ], F32, at)
        pT_new = sb("pT_new", [DS, NQ], F32, at)
        s_max = sb("s_max", [NQ, 6], F32, at)
        s_sum = sb("s_sum", [NQ, 6], F32, at)
        s_sign = sb("s_sign", [NQ, 3], F32, at)
        s_pick = sb("s_pick", [NQ, H, DS], F32, at)
        s_out = sb("s_out", [NQ, HW], F32, at)
        at.close()

        gt = ExitStack()
        sb("xh_hold", [P, 2 * KT, TOK], F32, gt)
        branch = sb("branch", [P, 2 * H, TOK], F32, gt)
        sq0 = sb("sq0", [P, 2, TOK], F32, gt)
        rs0 = sb("rs0", [P, 2, TOK], F32, gt)
        att_g = sb("att_g", [P, 2, TOK], F32, gt)
        u_rows = sb("u_rows", [2 * DB + 2, CW], F32, gt)
        gt.close()

        gl = ExitStack()
        woh = sb("woh", [P, KT, D], F32R, gl)
        wol = sb("wol", [P, KT, D], F32R, gl)
        qk_c = sb("qk_c", [P, 2, 2 * GH, P], F32, gl)
        v_c = sb("v_c", [P, 2, 2 * GH, P], F32, gl)
        g_c = sb("g_c", [P, 2, 2 * GH, P], F32, gl)
        la = sb("la", [P, 2, GH * P], F32, gl)
        ee = sb("ee", [P, 2, GH, P], F32, gl)
        e_last = sb("e_last", [P, GH, DB], F32, gl)
        qb = sb("qb", [P, GH, P], F32, gl)
        ks = sb("ks", [P, GH, P], F32, gl)
        kst = sb("kst", [P, GH * P], F32, gl)
        xlev = sb("xlev", [P, 2, GH, P], F32, gl)
        aT = sb("aT", [P, GH, P], F32, gl)
        v_tok = sb("v_tok", [P, GH * DV], F32, gl)
        st_g = sb("st_g", [P, GH, DV], F32, gl)
        sq1 = sb("sq1", [P, 2, GH, P], F32, gl)
        rs1 = sb("rs1", [P, GH * P], F32, gl)
        mh = sb("mh", [P, 2 * GH, P], F32R, gl)
        ml = sb("ml", [P, 2 * GH, P], F32R, gl)
        gl.close()
        free = attT[:, :, :].rearrange("p h t -> p (h t)")
        lr_all = free[0:17, 0:TOK]
        w_up = free[0:17, TOK:TOK + GH * P]
        zt = free[:, TOK + GH * P:TOK + 3 * GH * P].rearrange("p (s n) -> p s n", s=2)
        la_w = free[:, TOK + 3 * GH * P:TOK + 5 * GH * P].rearrange("p (s n) -> p s n", s=2)
        s0_b = [free[:, i * GH * DV:(i + 1) * GH * DV].rearrange("p (h v) -> p h v", h=GH) for i in range(2)]
        s0_b += [t[:, 1, :, :].rearrange("p (h a) t -> p h (a t)", h=GH) for t in (v_c, qk_c)]
        wo_raw = free[:, 0:2 * KT * P].rearrange("p (s k n) -> p s k n", s=2, k=KT)
        y_o = free[:, 2 * GH * DV:3 * GH * DV]
        kst_m = y_o.rearrange("p (s n) -> p s n", s=2)
        mt = free[:, 3 * GH * DV:4 * GH * DV].rearrange("p (m t) -> p m t", t=P)

        ps = top.enter_context(nc.psum_tensor("ps", [P, 8, 512], F32))

        phase_end = sem("phase_end")
        passed = sem("passed")
        x_in = [sem("x_in0"), sem("x_in1")]
        norm_in = sem("norm_in")
        vec_in = sem("vec_in")
        vecT_ready = sem("vecT_ready")
        lam_ready = sem("lam_ready")
        lam_exp = sem("lam_exp")
        act_step = sem("act_step")
        dve_step = sem("dve_step")
        pool_step = sem("pool_step")
        block = top.enter_context(nc.Block())
        def rd(t):
            return t.bitcast(F32)

        def wait_apart(eng, *waits):
            for q, n in waits:
                eng.wait_ge(q, n)
            eng.sem_inc(passed, 1)

        class Norm:
            def __init__(self, l):
                self.rstd = sem(f"n{l}_rstd")
                self.xs_ready = sem(f"n{l}_xs_ready")
                self.T_ready = sem(f"n{l}_T_ready")
                self.hi = sem(f"n{l}_hi")
                self.lo = sem(f"n{l}_lo")

        class Proj:
            def __init__(self, l):
                self.raw_in = [sem(f"p{l}_raw_in{s}") for s in range(2)]
                self.hi = sem(f"p{l}_hi")
                self.lo = sem(f"p{l}_lo")
                self.acc_ready = sem(f"p{l}_acc_ready")
                self.acc_used = sem(f"p{l}_acc_used")
                self.stored = [sem(f"p{l}_stored{s}") for s in range(2)] if l < 2 else None

        norms = [Norm(0), Norm(1)]
        projs = [Proj(0), Proj(1)]
        po = Proj(2)

        def barrier(eng, n):
            eng.drain().then_inc(phase_end, 1)
            eng.wait_ge(phase_end, 5 * (n + 1))

        def upper(t, hf):
            return t.rearrange("p (n two r) -> p n two r", two=2, r=hf)[:, :, 1, :]

        att_in = sem("att_in")
        kv_T = sem("kv_T")
        kv_out = sem("kv_out")
        rows_ready = sem("rows_ready")
        probT_ready = sem("probT_ready")
        s_ready = sem("s_ready")
        m_ready = sem("m_ready")
        p_exp = sem("p_exp")
        p_mix = sem("p_mix")
        o_ready = sem("o_ready")
        o_used = sem("o_used")
        qp_zero = sem("qp_zero")
        pt_in = sem("pt_in")
        k_page = [sem(f"k_page{s}") for s in range(4)]
        v_page = [sem(f"v_page{s}") for s in range(4)]
        new_in = sem("new_in")
        kT_ready = sem("kT_ready")
        kT_hi = sem("kT_hi")
        kT_lo = sem("kT_lo")
        q_ready = sem("q_ready")
        sc_ready = sem("sc_ready")
        mx_ready = sem("mx_ready")
        ps_exp = sem("ps_exp")
        pT_ready = sem("pT_ready")
        pT_used = [sem("pT_used_dve"), sem("pT_used_act")]
        v_used = sem("v_used")
        so_ready = sem("so_ready")
        so_scaled = sem("so_scaled")
        sp_ready = sem("sp_ready")
        gates_in = sem("gates_in")
        products_in = sem("products_in")
        cv_in = sem("cv_in")
        cv_out = sem("cv_out")
        sq_ready = sem("sq_ready")
        sq_sum = sem("sq_sum")
        rs_ready = sem("rs_ready")
        ge_ready = sem("ge_ready")
        mixed = sem("mixed")
        mix_hi = sem("mix_hi")
        br_hi = sem("br_hi")
        st_in = sem("st_in")
        stT_ready = sem("stT_ready")
        stT_rows = sem("stT_rows")
        u_ready = sem("u_ready")
        ulT_ready = sem("ulT_ready")
        ul_rows = sem("ul_rows")
        conv_out = sem("conv_out")
        wo_in = [sem(f"wo_in{s}") for s in range(2)]
        wo_hi = sem("wo_hi")
        wo_lo = sem("wo_lo")
        up_in = sem("up_in")
        g_in = [sem(f"g_in{s}") for s in range(2)]
        g_zero = sem("g_zero")
        g_ones = sem("g_ones")
        lr_w = sem("lr_w")
        lr_hi = sem("lr_hi")
        lr_lo = sem("lr_lo")
        lr_acc = sem("lr_acc")
        lr_used = sem("lr_used")
        lr_in = sem("lr_in")
        la_out = [sem("la_out0"), sem("la_out1")]
        z_ready = sem("z_ready")
        z_abs = sem("z_abs")
        la_ready = sem("la_ready")
        vT_ready = sem("vT_ready")
        v_ready = sem("v_ready")
        e_ready = sem("e_ready")
        e_exp = sem("e_exp")
        x_ready = sem("x_ready")
        a_ready = sem("a_ready")
        a_used = sem("a_used")
        ks_ready = sem("ks_ready")
        ksT_ready = sem("ksT_ready")
        kst_ready = sem("kst_ready")
        qb_ready = sem("qb_ready")
        oT_ready = sem("oT_ready")
        sd_ready = sem("sd_ready")
        st_ready = sem("st_ready")
        sq1_ready = sem("sq1_ready")
        r_ready = sem("r_ready")
        rs1_ready = sem("rs1_ready")
        m_mixed = sem("m_mixed")
        mh_ready = sem("mh_ready")
        ml_ready = sem("ml_ready")
        y_ready = sem("y_ready")
        y_used = sem("y_used")
        y_rstd = sem("y_rstd")
        y_norm = sem("y_norm")
        y_out = sem("y_out")
        s0_in = [sem(f"s0_in{s}") for s in range(4)]
        s0_out = [sem(f"s0_out{s}") for s in range(4)]
        km_ready = sem("km_ready")
        sdb_ready = sem("sdb_ready")
        s0_new = sem("s0_new")
        gp_out = sem("gp_out")

        xp_v = a["x_prompt"][0].rearrange("(t p) d -> p t d", p=P)
        xs_v = a["x_sample"].rearrange("b s d -> (b s) d")
        w0_v = a["w_in_even"][0].rearrange("(k p) n -> p k n", p=P)
        w1_v = a["w_in_odd"][0].rearrange("(k p) n -> p k n", p=P)
        wo0_v = a["w_out_even"][0].rearrange("(k p) n -> p k n", p=P)
        wo1_v = a["w_out_odd"][0].rearrange("(k p) n -> p k n", p=P)
        kp_o = o["k_prompt"][0, 0].rearrange("(t p) h d -> p t h d", p=P)
        vp_o = o["v_prompt"][0, 0].rearrange("(t p) h d -> p t h d", p=P)
        ks_o = o["k_sample"][0].rearrange("b s h d -> (b s) h d")
        vs_o = o["v_sample"][0].rearrange("b s h d -> (b s) h d")
        ks_b = o["k_sample"][0].rearrange("b s h d -> b s (h d)")
        vs_b = o["v_sample"][0].rearrange("b s h d -> b s (h d)")
        ck = a["cache_k"][0].rearrange("n p h d -> n p (h d)")
        cv_ = a["cache_v"][0].rearrange("n p h d -> n p (h d)")
        yp_o = o["y_prompt"][0].rearrange("(t p) d -> t p d", p=P)
        ys_o = o["y_sample"].rearrange("b s d -> (b s) d")

        def acc(m):
            return ps[:, 3 * m:3 * m + 3, :].rearrange("p a b -> p (a b)")

        def unit_parts(m, row):
            return [(ps[:, 3 * m:3 * m + 2, 0:SG], row[:, 0:2 * SG].rearrange("p (a b) -> p a b", a=2)),
                    (ps[:, 3 * m + 2, 0:TOK - 2 * SG], row[:, 2 * SG:TOK])]

        @block.sync
        def _(sp):
            sp.dma_start(x1[:, 0:4, :], xp_v[:, 0:4, :]).then_inc(x_in[0], 16)
            sp.dma_start(norm_bc[:, :], a["norm_w"][0:1, :].to_broadcast([P, D])).then_inc(norm_in, 16)
            sp.dma_start(x1[:, 4:NT, :], xp_v[:, 4:NT, :]).then_inc(x_in[1], 16)
            sp.dma_start(x1[64:P, NT, :], xs_v).then_inc(x_in[1], 16)
            sp.dma_start(vec_rows[0:12, :], a["conv_w"][0].rearrange("k (j p) -> (k j) p", p=P)).then_inc(vec_in, 16)
            sp.dma_start(vec_rows[12:13, :], a["diff_subln_w"]).then_inc(vec_in, 16)
            sp.dma_start(vec_rows[13:15, :], a["gla_norm_w"].rearrange("a (d p) -> (a d) p", p=P)).then_inc(vec_in, 16)
            sp.dma_start(stage[:, 1, 0:4 * DH],
                         a["diff_lambda"].rearrange("a b d -> a (b d)").to_broadcast([P, 4 * DH])).then_inc(vec_in, 16)
            sp.dma_start(st_rows, a["state_conv"][0].rearrange("b r c -> (b r) c")).then_inc(st_in, 16)
            sp.dma_start(pages_sb[:, :], a["page_table"].rearrange("(a b) g -> a (b g)", a=1)).then_inc(pt_in, 16)

            def stream(p, view, order):
                for s in range(2):
                    sp.dma_start(wraw[:, s], view[:, :, s * CH:(s + 1) * CH]).then_inc(p.raw_in[s], 16)
                for first, end, ahead in order:
                    with sp.Fori(max(first, 1), end) as j:
                        for s in range(2):
                            sp.wait_ge(p.lo, 2 * j + s - 1)
                            sp.dma_start(wraw[:, s], view[:, :, ds((2 * j + s + ahead) * CH, CH)]).then_inc(p.raw_in[s], 16)

            stream(projs[0], w0_v, ORDER0)
            barrier(sp, 0)

            def head_loads(h):
                if not (isinstance(h, int) and h == 0):
                    wait_apart(sp, (s_ready, 2 * NT * h))
                    wait_apart(sp, (rows_ready, 6 * h))
                for dst, first in ((q_in, 0), (k_in, 2 * H * DH)):
                    for half in range(2):
                        sp.dma_start(dst[half * DH:(half + 1) * DH, :],
                                     act0[ds(h * DH + first + half * H * DH, DH), :]).then_inc(att_in, 16)
                sp.dma_start(v_in[:, :], act0[ds(h * P + 4 * H * DH, P), :]).then_inc(att_in, 16)

            def key_pages(b, first):
                for s in range(4):
                    if not first:
                        sp.wait_ge(kT_ready, (PAGES + 1) * b + 4 * s + 4 - (PAGES + 1))
                    for g in range(4):
                        page = sp.value_load(pages_sb[0:1, ds(b * PAGES + 4 * s + g, 1)], min_val=0, max_val=NPHYS - 1)
                        sp.dma_start(kring[:, s, g, :], ck[ds(page, 1), :, :].rearrange("a p d -> p (a d)")).then_inc(k_page[s], 16)

            head_loads(0)
            sp.wait_ge(pt_in, 16)
            key_pages(0, True)
            with sp.Fori(1, H) as h:
                head_loads(h)
            barrier(sp, 1)

            with sp.Fori(1, DB) as b:
                key_pages(b, False)
            barrier(sp, 2)

            for u in range(2 * H):
                sp.dma_start(branch[:, u, :], a0[12 + u]).then_inc(gates_in if u < H else products_in, 16)
            sp.wait_ge(norms[0].xs_ready, NT + 1)
            sp.dma_start(norm_bc[:, :], a["norm_w"][1:2, :].to_broadcast([P, D])).then_inc(norm_in, 16)
            barrier(sp, 3)
            stream(po, wo0_v, [(0, D // CH // 2, 0)])
            sp.wait_ge(po.lo, D // CH)
            sp.dma_start(wraw[:, 1, :, 0:P], w1_v[:, :, ODD - P:ODD]).then_inc(lr_w, 16)
            sp.dma_start(w_up[0:16, :], a["w_gate_up"][0]).then_inc(up_in, 16)
            sp.dma_start(w_up[16:17, :], a["b_gate"]).then_inc(up_in, 16)

            def weights(c):
                if c == 1:
                    sp.wait_ge(lr_lo, 1)
                if c >= 2:
                    sp.wait_ge(projs[1].lo, c - 1)
                sp.dma_start(wraw[:, c % 2], w1_v[:, :, ORDER1[c] * CH:(ORDER1[c] + 1) * CH]).then_inc(projs[1].raw_in[c % 2], 16)

            def log_decay_store(t):
                sp.wait_ge(la_ready, t + 1)
                sp.dma_start(la_d[t], la_w[:, t % 2, :]).then_inc(la_out[t % 2], 16)

            for c in range(4):
                weights(c)
                if c == 1:
                    sp.wait_ge(lr_used, 1)
                    sp.wait_ge(g_ones, 1)
                    sp.dma_start(lr_all[0:16, :], stage[P - 16:P, 1, :]).then_inc(lr_in, 16)
            log_decay_store(0)
            log_decay_store(1)
            weights(4)
            for t in range(2, 6):
                log_decay_store(t)
            weights(5)
            for t in range(6, NT + 1):
                log_decay_store(t)
            sp.wait_ge(la_out[0], 16 * (NT // 2 + 1))
            sp.wait_ge(la_out[1], 16 * (NT // 2))
            for c in range(6, NCH1):
                weights(c)
            sp.wait_ge(norms[1].xs_ready, NT + 1)
            sp.dma_start(norm_bc[:, :], a["norm_f"].rearrange("(a d) -> a d", a=1).to_broadcast([P, D])).then_inc(norm_in, 16)
            barrier(sp, 4)

            def chunk_loads(s, lo, t, t0, n):
                for dst, m in ((qk_c, 0), (v_c, 4 * GH), (g_c, 2 * GH)):
                    sp.dma_start(dst[:, s, :, lo:P], a1[m:m + 2 * GH, :, ds(t0, n)].rearrange("m p t -> p m t")).then_inc(g_in[s], 16)
                sp.dma_start(la[:, s, :], la_d[ds(t, 1), :, :].rearrange("a p n -> p (a n)")).then_inc(g_in[s], 16)

            def y_store(c):
                sp.wait_ge(y_norm, c + 1)
                if isinstance(c, int) and c == NT:
                    sp.dma_start(ys_o, y_o[P - NS:P, :]).then_inc(y_out, 16)
                else:
                    sp.dma_start(yp_o[ds(c, 1), :, :].rearrange("a p d -> p (a d)"), y_o[:, :]).then_inc(y_out, 16)

            chunk_loads(0, 0, 0, 0, P)
            for n in range(2):
                sp.dma_start(wo_raw[:, n], wo1_v[:, :, n * P:(n + 1) * P]).then_inc(wo_in[n], 16)
            chunk_loads(1, 0, 1, P, P)
            for n in range(2, D // P):
                sp.wait_ge(wo_lo, n - 1)
                sp.dma_start(wo_raw[:, n % 2], wo1_v[:, :, n * P:(n + 1) * P]).then_inc(wo_in[n % 2], 16)
            def next_loads(c, s):
                sp.wait_ge(m_mixed, c - 1)
                chunk_loads(s, 0, c, c * P, P)

            next_loads(2, 0)
            next_loads(3, 1)
            y_store(0)
            with sp.Fori(2, NT // 2) as j:
                next_loads(2 * j, 0)
                y_store(2 * j - 3)
                next_loads(2 * j + 1, 1)
                y_store(2 * j - 2)
            sp.wait_ge(m_mixed, NT - 1)
            chunk_loads(0, P - NS, NT, SEQ, NS)
            s0v = a["state_gla"][0].rearrange("b h k v -> b k h v")
            s0o = o["gla_sample"][0].rearrange("b h k v -> b k h v")
            def state_load(b):
                sp.dma_start(s0_b[b % 4], s0v[b]).then_inc(s0_in[b % 4], 16)

            state_load(0)
            state_load(1)
            y_store(NT - 3)
            sp.wait_ge(vT_ready, 2 * NT)
            state_load(2)
            sp.wait_ge(a_ready, 8 * NT)
            sp.wait_ge(ks_ready, NT)
            state_load(3)
            y_store(NT - 2)
            y_store(NT - 1)
            for b in range(DB):
                sp.wait_ge(s0_new, b + 1)
                sp.dma_start(s0o[b], s0_b[b % 4]).then_inc(s0_out[b % 4], 16)
                if 1 <= b <= DB - 4:
                    sp.wait_ge(s0_out[(b - 1) % 4], 16)
                    state_load(b + 3)
            y_store(NT)
            sp.wait_ge(y_out, 16 * (NT + 1))
            for s in range(4):
                sp.wait_ge(s0_out[s], 16 * DB // 4)
            barrier(sp, 5)

        @block.gpsimd
        def _(pool):
            ch = Chain(pool, pool_step)

            def sel(view, pattern, base, mult, fill, op=ALU.is_ge):
                ch.link(pool.affine_select(out=view, in_=view, pattern=pattern, compare_op=op, fill=fill,
                                           base=base, channel_multiplier=mult))

            ch.link(pool.memset(x1[0:64, NT, :], 0.0))
            ch.link(pool.memset(eps_b[:, :], EPS))
            ch.link(pool.memset(ones[:, :], 1.0))
            ch.link(pool.memset(ident[:, :], 0.0))
            sel(ident[:, :], [[-1, P]], 0, 1, 1.0, ALU.not_equal)
            ch.link(pool.memset(identb[:, :], 0.0))
            sel(identb[:, :], [[-1, P]], 0, 1, 1.0, ALU.not_equal)
            ch.link(pool.memset(causal[:, :], 0.0))
            sel(causal[:, :], [[-1, P]], 0, 1, NEG)
            ch.link(pool.memset(new_mask[:, :], 0.0))
            nm = new_mask[:, :].rearrange("p (n i) -> p n i", i=DS)
            sel(nm, [[0, 2 * H], [1, DS]], 0, -1, NEG)
            def low_parts(p, n):
                with pool.Fori(0, n // 2) as j:
                    for s in range(2):
                        pool.wait_ge(p.hi, 2 * j + s + 1)
                        pool.tensor_tensor(wl[:, s], wraw[:, s], rd(wh[:, s]), ALU.subtract).then_inc(p.lo, 1)

            low_parts(projs[0], NCH0)
            barrier(pool, 0)

            ch.link(pool.memset(q_pair[:, :, :, :], 0.0))
            pool.memset(q_b[:, :], 0.0).then_inc(qp_zero, 1)

            def value_pages(b, first):
                for s in range(4):
                    if not first:
                        pool.wait_ge(v_used, 4 * b + s - 3)
                    for g in range(4):
                        page = pool.value_load(pages_sb[0:1, ds(b * PAGES + 4 * s + g, 1)], min_val=0, max_val=NPHYS - 1)
                        pool.dma_start(vring[:, s, g, :], cv_[ds(page, 1), :, :].rearrange("a p d -> p (a d)")).then_inc(v_page[s], 16)

            ch.link(pool.memset(u_pad[:, 0:2], 0.0))
            pool.wait_ge(stT_rows, 1)
            for h in range(H):
                pool.wait_ge(rows_ready, 6 * h + 6)
                pool.dma_start(kp_o[:, :, h, :], k_row[:, 0:NT, :]).then_inc(kv_out, 16)
                pool.dma_start(ks_o[:, h, :], k_row[64:P, NT, :]).then_inc(kv_out, 16)
                pool.dma_start(vp_o[:, :, h, :], v_row[:, 0:NT, :]).then_inc(kv_out, 16)
                pool.dma_start(vs_o[:, h, :], v_row[64:P, NT, :]).then_inc(kv_out, 16)
                if h:
                    pool.wait_ge(cv_out, 16 * h)
                for n, u in enumerate((20, 24, 28, 16)):
                    pool.dma_start(cin[:, n, :], a0[u + h]).then_inc(cv_in, 16)
                pool.wait_ge(cv_in, 64 * (h + 1))
                u_s = u_pad[:, UP:UP + DB * (2 + DS)].rearrange("p (b s) -> p b s", s=2 + DS)
                ch.link(pool.tensor_copy(u_s[:, :, 0:2], st_T[:, h, :].rearrange("p (b r) -> p b r", r=2)))
                ch.link(pool.tensor_tensor(u_s[:, :, 2:2 + DS], cin[:, 1, SEQ:TOK].rearrange("p (b s) -> p b s", s=DS),
                                           cin[:, 2, SEQ:TOK].rearrange("p (b s) -> p b s", s=DS), ALU.mult))
                ch.link(pool.tensor_tensor(u_pad[:, 2:UP], cin[:, 1, 0:SEQ], cin[:, 2, 0:SEQ], ALU.mult))
                ch.link(pool.tensor_copy(u_last[:, h, 0:2 * DB].rearrange("p (b r) -> p b r", r=2), u_s[:, :, DS:DS + 2]))
                ch.link(pool.tensor_copy(u_last[:, h, 2 * DB:2 * DB + 2], u_pad[:, SEQ:SEQ + 2]))
                for k in range(3):
                    dst = tap_u if k else conv
                    ch.link(pool.tensor_scalar(dst[:, :], u_pad[:, k:k + UW], vec[:, 4 * k + h:4 * k + h + 1], None, ALU.mult))
                    if k:
                        ch.link(pool.tensor_tensor(conv[:, :], conv[:, :], tap_u[:, :], ALU.add))
                ch.link(pool.tensor_tensor(cin[:, 3, :], cin[:, 3, :], cin[:, 0, :], ALU.mult))
                ch.link(pool.tensor_tensor(cin[:, 3, 0:SEQ], cin[:, 3, 0:SEQ], conv[:, 0:SEQ], ALU.mult))
                prod_s = cin[:, 3, SEQ:TOK].rearrange("p (b s) -> p b s", s=DS)
                for b in range(DB):
                    c0 = UP + b * (2 + DS)
                    ins = pool.tensor_tensor(prod_s[:, b, :], prod_s[:, b, :], conv[:, c0:c0 + DS], ALU.mult)
                ch.link(ins)
                pool.dma_start(a0[16 + h], cin[:, 3, :]).then_inc(cv_out, 16)
            pool.sem_inc(u_ready, 1)
            pool.wait_ge(cv_out, 16 * H)
            pool.wait_ge(kv_out, 64 * H)
            barrier(pool, 1)

            def new_rows(b):
                pool.dma_start(k_new[:, :], ks_b[ds(b, 1), :, :].rearrange("a s d -> (a s) d")).then_inc(new_in, 16)
                pool.dma_start(v_new[:, :], vs_b[ds(b, 1), :, :].rearrange("a s d -> (a s) d")).then_inc(new_in, 16)

            new_rows(0)
            value_pages(0, True)
            with pool.Fori(1, DB) as b:
                value_pages(b, False)
                pool.wait_ge(so_ready, b)
                new_rows(b)
            barrier(pool, 2)

            pool.wait_ge(ul_rows, 1)
            pool.dma_start(o["conv_sample"][0].rearrange("b r c -> (b r) c"), u_rows[0:2 * DB, :]).then_inc(conv_out, 16)
            pool.dma_start(o["conv_prompt"][0, 0], u_rows[2 * DB:2 * DB + 2, :]).then_inc(conv_out, 16)
            for j in range(4):
                pool.wait_ge(br_hi, j + 1)
                pool.tensor_tensor(xl[:, H + j, :], branch[:, H + j, :], rd(xh[:, H + j, :]), ALU.subtract)
            pool.wait_ge(conv_out, 32)
            barrier(pool, 3)
            low_parts(po, D // CH)
            ch.link(pool.memset(decay_m[:, :, :], 1.0))
            sel(decay_m[:, 0, :], [[1, P]], 0, -1, 0.0)
            sel(decay_m[:, 1, :], [[-1, P]], -1, 1, 0.0)
            blk = decay_m[:, 9, :].rearrange("p (n i) -> p n i", i=DS)
            sel(blk, [[DS, P // DS], [1, DS]], 0, -1, 0.0)
            sel(blk, [[-DS, P // DS], [0, DS]], 0, 1, 0.0)
            blk = decay_m[:, 10, :].rearrange("p (n i) -> p n i", i=DS)
            sel(blk, [[-DS, P // DS], [-1, DS]], -1, 1, 0.0)
            sel(blk, [[DS, P // DS], [0, DS]], DS - 1, -1, 0.0)
            ch.link(pool.memset(lvl_mask[:, :, :], 1.0))
            for l, hf in enumerate(HALVES):
                n = P // (2 * hf)
                v = decay_m[:, 2 + l, :].rearrange("p (n two r) -> p n two r", two=2, r=hf)
                sel(v[:, :, 1, :], [[-2 * hf, n], [0, hf]], -hf, 1, 0.0)
                sel(v[:, :, 1, :], [[2 * hf, n], [1, hf]], hf, -1, 0.0)
                sel(v[:, :, 0, :], [[-2 * hf, n], [-1, hf]], -1, 1, 0.0)
                sel(v[:, :, 0, :], [[2 * hf, n], [0, hf]], hf - 1, -1, 0.0)
                m = lvl_mask[:, l, :].rearrange("p (n two r) -> p n two r", two=2, r=hf)
                sel(m[:, :, 1, :], [[-2 * hf, n], [0, hf]], 0, 1, 0.0)
                sel(m[:, :, 1, :], [[2 * hf, n], [0, hf]], hf - 1, -1, 0.0)
                ch.link(pool.memset(m[:, :, 0, :], 0.0))
            pool.memset(lr_all, 1.0).then_inc(g_ones, 1)
            pool.wait_ge(lr_hi, 1)
            pool.tensor_tensor(wl[:, 1, :, 0:P], wraw[:, 1, :, 0:P], rd(wh[:, 1, :, 0:P]), ALU.subtract).then_inc(lr_lo, 1)
            low_parts(projs[1], NCH1)
            barrier(pool, 4)

            ch.link(pool.memset(st_g[:, :, :], 0.0))
            pool.memset(aT[:, :, :], 0.0).then_inc(g_zero, 1)
            def chunk(c, s):
                wait_apart(pool, (e_exp, 9 * c + 1),
                           *([] if isinstance(c, int) and c == 0 else [(st_ready, GH * c)]))
                if isinstance(c, int) and c == NT:
                    ch.link(pool.tensor_copy(e_last[:, :, :], ee[:, 0, :, P - NS + DS - 1:P:DS]))
                else:
                    ch.link(pool.tensor_copy(e_last[:, :, 0:1], ee[:, 0, :, P - 1:P]))
                pool.tensor_tensor(qb[:, :, :], qk_c[:, s, 0:GH, :], ee[:, 0, :, :], ALU.mult).then_inc(qb_ready, 1)
                pool.wait_ge(e_exp, 9 * c + 2)
                pool.tensor_tensor(ks[:, :, :], qk_c[:, s, GH:2 * GH, :], ee[:, 1, :, :], ALU.mult).then_inc(ks_ready, 1)
            chunk(0, 0)
            for n in range(D // P):
                pool.wait_ge(wo_hi, n + 1)
                pool.tensor_tensor(wol[:, :, n * P:(n + 1) * P], wo_raw[:, n % 2],
                                   rd(woh[:, :, n * P:(n + 1) * P]), ALU.subtract).then_inc(wo_lo, 1)
            chunk(1, 1)
            with pool.Fori(1, NT // 2) as j:
                ch.enter(j, 2, 1)
                chunk(2 * j, 0)
                chunk(2 * j + 1, 1)
            ch.leave(NT // 2 - 1)
            pool.wait_ge(st_ready, GH * NT)
            pool.dma_start(o["gla_prompt"][0, 0].rearrange("h k v -> k h v"), st_g[:, :, :]).then_inc(gp_out, 16)
            pool.wait_ge(oT_ready, NT)
            pool.memset(aT[:, :, :], 0.0).then_inc(g_zero, 1)
            chunk(NT, 0)
            pool.wait_ge(gp_out, 16)
            barrier(pool, 5)

        @block.scalar
        def _(act):
            ch = Chain(act, act_step)

            def rsqrt(out, src, mean, sem_=None):
                ch.link(act.activation(out, src, ACT.Ln, bias=eps_b[:, :], scale=mean))
                ins = act.activation(out, out, ACT.Exp, scale=-0.5)
                ins.then_inc(sem_, 1)

            def norm_high(n):
                def high(t, slot, c0, n0):
                    for q in range(2):
                        act.wait_ge(n.T_ready, 2 * t + q + 1)
                        src = ps[:, 2 * slot + q, :].rearrange("p (k i) -> p k i", i=P)[:, :, P - n0:P]
                        act.activation(xh[:, 4 * q:4 * q + 4, ds(c0, n0)], src, ACT.Copy).then_inc(n.hi, 1)
                with act.Fori(0, NT // 2) as j:
                    for s in range(2):
                        high(2 * j + s, s, (2 * j + s) * P, P)
                high(NT, 0, SEQ, NS)

            def norm_stats(n):
                for t in range(NT + 1):
                    if n is norms[0] and t in (0, 4):
                        act.wait_ge(x_in[t // 4], 16 if t == 0 else 32)
                        if t == 4:
                            act.wait_ge(pool_step, 2)
                    if n is norms[1]:
                        act.wait_ge(po.acc_used, (NT + 1) * (D // CH - 1) + t + 2)
                    ch.link(act.activation(xs[:, t % 2, :], x1[:, t, :], ACT.Square, accum_out=ssq[:, t:t + 1]))
                rsqrt(rstd[:, :], ssq[:, :], 1.0 / D, n.rstd)

            def high_parts(p, n, view, base, gates=(), aside=None):
                def hi(j, s):
                    act.wait_ge(p.raw_in[s], 16 * (j + 1))
                    if not (isinstance(j, int) and j == 0):
                        act.wait_ge(p.acc_ready, base * (2 * j + s - 1))
                    elif aside and s == 1:
                        act.wait_ge(lr_acc, 1)
                    act.activation(wh[:, s], wraw[:, s], ACT.Copy).then_inc(p.hi, 1)

                def store(j, s, gate=False):
                    if view is None:
                        return
                    for m in range(2):
                        u = 4 * j + 2 * s + m
                        if gate:
                            act.wait_ge(p.acc_ready, u + 1)
                            act.wait_ge(p.acc_used, u)
                            for bank, e in unit_parts(m, gate_e):
                                ins = act.activation(e, bank, ACT.Exp, scale=-1.0)
                            ins.then_inc(ge_ready, 1)
                        act.wait_ge(p.acc_used, u + 1)
                        act.dma_start(view[ds(u, 1), :, :].rearrange("a p t -> p (a t)"), stage[:, m]).then_inc(p.stored[m], 16)

                def pair(j):
                    fixed = isinstance(j, int)
                    hi(j, 0)
                    store(j - 1, 1, fixed and j - 1 in gates)
                    hi(j, 1)
                    store(j, 0, fixed and j in gates)

                hi(0, 1)
                store(0, 0)
                start = 1
                if aside:
                    aside(0, 2)
                    hi(1, 0)
                    aside(2, 4)
                    store(0, 1)
                    aside(4, 6)
                    hi(1, 1)
                    aside(6, 8)
                    store(1, 0)
                    aside(8, 9)
                    start = 2
                for g in (*gates, n // 2):
                    if start < g:
                        with act.Fori(start, g) as j:
                            pair(j)
                    start = max(start, g)
                    while start < n // 2 and (start in gates or start - 1 in gates):
                        pair(start)
                        start += 1
                store(n // 2 - 1, 1, n // 2 - 1 in gates)
                if view is not None:
                    act.wait_ge(p.stored[0], 16 * n)
                    act.wait_ge(p.stored[1], 16 * n)

            def first_high(p):
                act.wait_ge(p.raw_in[0], 16)
                act.activation(wh[:, 0], wraw[:, 0], ACT.Copy).then_inc(p.hi, 1)

            norm_stats(norms[0])
            act.wait_ge(lam_ready, 1)
            act.activation(lam_s[:, 0:2], lam_s[:, 0:2], ACT.Exp).then_inc(lam_exp, 1)
            first_high(projs[0])
            norm_high(norms[0])
            high_parts(projs[0], NCH0, a0, 2, gates=GATES[0])
            barrier(act, 0)

            def head(h):
                def group(n, dst, width, sem_):
                    act.wait_ge(kv_T, 18 * h + n + 1)
                    act.activation(dst, ps[:, 4 + n % 2, 0:width], ACT.Copy).then_inc(sem_, 1)

                exponential(h, 0, 0)
                exponential(h, 0, 1)
                act.wait_ge(kv_out, 64 * h)
                act.wait_ge(o_ready, NT * h)
                for n in range(6):
                    row, t0 = (k_row, v_row)[n // 3], 4 * (n % 3)
                    nt = min(4, NT + 1 - t0)
                    group(n, row[:, t0:t0 + nt, :].rearrange("p t d -> p (t d)"), nt * P, rows_ready)
                n = 6
                for i in range(1, NT + 2):
                    if i < NT:
                        exponential(h, i, 0)
                    if i >= 2:
                        for t0 in range(0, i - 1, 4):
                            nt = min(4, i - 1 - t0)
                            group(n, probT[:, i % 2, t0 * P:(t0 + nt) * P], nt * P, probT_ready)
                            n += 1
                    if i < NT:
                        exponential(h, i, 1)
                    if i >= 2:
                        act.wait_ge(o_ready, NT * h + i - 1)
                        act.activation(attT[:, ds(h, 1), (i - 2) * P:(i - 1) * P].rearrange("p a t -> p (a t)"),
                                       ps[:, 6 + i % 2, 0:P], ACT.Copy).then_inc(o_used, 1)

            def exponential(h, i, w):
                nk = (i + 1) * P
                act.wait_ge(m_ready, 2 * (NT * h + i) + w + 1)
                act.activation(prob[:, i % 3, w, 0:nk], ps[:, 2 * w:2 * w + 2, :].rearrange("p a b -> p (a b)")[:, 0:nk],
                               ACT.Exp, bias=row_st[:, i % 2, 2 + w:3 + w], scale=SC,
                               accum_out=row_st[:, i % 2, 4 + w:5 + w]).then_inc(p_exp, 1)

            head(0)
            with act.Fori(1, H) as h:
                head(h)
            barrier(act, 1)

            def key_page(b, g):
                act.wait_ge(kT_ready, (PAGES + 1) * b + g + 1)
                if g < PAGES:
                    s = g // 4
                    act.activation(kTh[:, s % 2, :, (g % 4) * P:(g % 4 + 1) * P],
                                   ps[:, g % 2, :].rearrange("p (h k) -> p h k", h=H), ACT.Copy).then_inc(kT_hi, 1)
                else:
                    act.activation(kT_new[:, :, :], ps[:, 0, 0:H * DS].rearrange("p (h k) -> p h k", h=H),
                                   ACT.Copy).then_inc(kT_hi, 1)

            def batch(b, last):
                for g in range(8, PAGES + 1):
                    key_page(b, g)
                if not last:
                    key_page(b + 1, 0)
                    key_page(b + 1, 1)
                act.wait_ge(mx_ready, b + 1)
                for s in range(4):
                    act.activation(p_s[:, s * 512:(s + 1) * 512], ps[0:NQ, 2 + s, :], ACT.Exp, bias=s_max[:, 5:6], scale=SC,
                                   accum_out=s_sum[:, s:s + 1]).then_inc(ps_exp, 1)
                act.activation(p_s[:, PAGES * P:PAGES * P + DS], ps[0:NQ, 7, 0:DS], ACT.Exp, bias=s_max[:, 5:6], scale=SC,
                               accum_out=s_sum[:, 4:5]).then_inc(ps_exp, 1)
                act.wait_ge(pT_ready, 3 * b + 2)
                act.activation(pT[:, 8:16, :].rearrange("p g q -> p (g q)"), ps[:, 3, :], ACT.Copy).then_inc(pT_used[1], 1)
                if not last:
                    for g in range(2, 8):
                        key_page(b + 1, g)

            for g in range(8):
                key_page(0, g)
            with act.Fori(0, DB - 1) as b:
                batch(b, False)
            batch(DB - 1, True)
            barrier(act, 2)

            def squares(h):
                if h >= 2:
                    act.wait_ge(sq_sum, h - 1)
                act.activation(sq0[:, h % 2, :], attT[:, h, :], ACT.Square).then_inc(sq_ready, 1)

            squares(0)
            squares(1)
            for h in range(0, H, 2):
                for g in (h, h + 1):
                    act.wait_ge(sq_sum, g + 1)
                    if h:
                        act.wait_ge(mixed, g - 1)
                    ch.link(act.activation(rs0[:, g % 2, :], acc(g % 2)[:, 0:TOK], ACT.Ln, bias=eps_b[:, :], scale=1.0 / P))
                for g in (h, h + 1):
                    act.activation(rs0[:, g % 2, :], rs0[:, g % 2, :], ACT.Exp, scale=-0.5).then_inc(rs_ready, 1)
                if h + 2 < H:
                    squares(h + 2)
                    squares(h + 3)
                for g in (h, h + 1):
                    act.wait_ge(mixed, g + 1)
                    act.activation(xh[:, g, :], att_g[:, g % 2, :], ACT.Copy).then_inc(mix_hi, 1)
            barrier(act, 3)
            first_high(po)
            high_parts(po, D // CH, None, NT + 1)
            norm_stats(norms[1])
            act.wait_ge(lr_w, 16)
            act.wait_ge(po.acc_ready, (NT + 1) * D // CH)
            act.activation(wh[:, 1, :, 0:P], wraw[:, 1, :, 0:P], ACT.Copy).then_inc(lr_hi, 1)
            first_high(projs[1])
            norm_high(norms[1])

            def log_sums(t0, t1):
                for t in range(t0, t1):
                    act.wait_ge(z_ready, t + 1)
                    if t >= 2:
                        act.wait_ge(la_ready, t - 1)
                    z = zt[:, t % 2, :]
                    ch.link(act.activation(z, ps[:, 6 + t % 2, :], ACT.Abs))
                    ch.link(act.activation(z, z, ACT.Exp, scale=-1.0))
                    act.activation(z, z, ACT.Ln, bias=1.0).then_inc(z_abs, 1)

            high_parts(projs[1], NCH1, a1, 2, GATES[1], log_sums)
            barrier(act, 4)

            def values(c):
                for n in range(2):
                    act.wait_ge(vT_ready, 2 * c + n + 1)
                    act.activation(v_tok[:, n * 512:(n + 1) * 512], ps[:, 2 + n, :], ACT.Copy).then_inc(v_ready, 1)

            def exps(c, l0, l1):
                for l in range(l0, l1):
                    act.wait_ge(e_ready, 9 * c + l + 1)
                    if l >= 4:
                        act.wait_ge(x_ready, 7 * c + l - 3)
                    elif l >= 2:
                        act.wait_ge((qb_ready, ks_ready)[l - 2], c + 1)
                    else:
                        act.wait_ge(x_ready, 7 * c)
                    act.activation(ee[:, l % 2, :, :].rearrange("p h i -> p (h i)"), ps[:, (1 + l) % 2, :],
                                   ACT.Exp, scale=1.0 / 16).then_inc(e_exp, 1)

            def gated(c):
                act.wait_ge(m_mixed, c + 1)
                act.wait_ge(y_ready, 2 * c)
                act.activation(mh[:, :, :], mt[:, :, :], ACT.Copy).then_inc(mh_ready, 1)

            def final(c):
                act.wait_ge(y_used, 2 * c + 2)
                if not (isinstance(c, int) and c == 0):
                    act.wait_ge(y_norm, c)
                    act.wait_ge(y_out, 16 * c)
                ch.link(act.activation(y_o[:, :], x1[:, ds(c, 1), :].rearrange("p a d -> p (a d)"), ACT.Square, accum_out=ssq[:, 0:1]))
                rsqrt(rstd[:, 0:1], ssq[:, 0:1], 1.0 / D, y_rstd)

            def back(c):
                act.wait_ge(ksT_ready, c + 1)
                act.activation(kst[:, :], ps[:, 2, :], ACT.Copy).then_inc(kst_ready, 1)
                act.wait_ge(oT_ready, c + 1)
                for d in range(2):
                    act.activation(sq1[:, d, :, :].rearrange("p h i -> p (h i)"), ps[:, 6 + d, :], ACT.Square).then_inc(sq1_ready, 1)

            def stats(c):
                act.wait_ge(r_ready, c + 1)
                rsqrt(rs1[:, :], ps[:, 5, :], 1.0 / DV, rs1_ready)

            def body(c, with_final=True):
                stats(c - 1)
                exps(c, 2, 4)
                values(c)
                gated(c - 1)
                last = isinstance(c, int) and c == NT
                exps(c, 4, 5 if last else 6)
                if with_final:
                    final(c - 2)
                if not last:
                    exps(c, 6, 9)
                if last:
                    final(c - 1)
                else:
                    exps(c + 1, 0, 2)
                back(c)

            def split_weights(n):
                act.wait_ge(wo_in[n % 2], 16 * (n // 2 + 1))
                act.activation(woh[:, :, n * P:(n + 1) * P], wo_raw[:, n % 2], ACT.Copy).then_inc(wo_hi, 1)

            exps(0, 0, 2)
            values(0)
            exps(0, 2, 4)
            for l in range(4, 9):
                split_weights(l - 4)
                exps(0, l, l + 1)
            exps(1, 0, 2)
            back(0)
            for n in range(5, D // P):
                split_weights(n)
            body(1, False)
            with act.Fori(1, NT // 2 - 1) as j:
                ch.enter(j, 2 * 3, 1)
                body(2 * j)
                body(2 * j + 1)
            ch.leave(NT // 2 - 2)
            body(NT - 2)
            body(NT - 1)
            body(NT)
            stats(NT)
            gated(NT)
            final(NT)
            barrier(act, 5)

        @block.vector
        def _(v):
            ch = Chain(v, dve_step)

            def normalize(n, ready):
                def scale(t, s):
                    if not (isinstance(t, int) and t < 2):
                        v.wait_ge(n.T_ready, 2 * t - 2)
                    src = x1[:, ds(t, 1), :].rearrange("p a d -> p (a d)")
                    v.scalar_tensor_tensor(out=xs[:, s, :], in0=src, scalar=rstd_col(t), in1=norm_bc[:, :],
                                           op0=ALU.mult, op1=ALU.mult).then_inc(n.xs_ready, 1)

                def rstd_col(t):
                    return rstd[:, ds(t, 1)]

                def low(t, slot, c0, n0):
                    for q in range(2):
                        v.wait_ge(n.hi, 2 * t + q + 1)
                        src = ps[:, 2 * slot + q, :].rearrange("p (k i) -> p k i", i=P)[:, :, P - n0:P]
                        v.tensor_tensor(xl[:, 4 * q:4 * q + 4, ds(c0, n0)], src, rd(xh[:, 4 * q:4 * q + 4, ds(c0, n0)]),
                                        ALU.subtract).then_inc(n.lo, 1)

                v.wait_ge(n.rstd, 1)
                v.wait_ge(norm_in, ready)
                scale(0, 0)
                scale(1, 1)
                with v.Fori(0, NT // 2 - 1) as j:
                    for s in range(2):
                        low(2 * j + s, s, (2 * j + s) * P, P)
                        scale(2 * j + s + 2, s)
                low(NT - 2, 0, (NT - 2) * P, P)
                scale(NT, 0)
                low(NT - 1, 1, (NT - 1) * P, P)
                low(NT, 0, SEQ, NS)

            def units_out(p, n, gates, aside=None):
                def unit(j, s, m):
                    fixed = isinstance(j, int)
                    v.wait_ge(p.acc_ready, 4 * j + 2 * s + m + 1)
                    if not (fixed and j == 0 and s == 0):
                        v.wait_ge(p.stored[m], 16 * (2 * j + s))
                    elif aside and m == 1:
                        v.wait_ge(lr_in, 16)
                    if fixed and j in gates:
                        v.wait_ge(ge_ready, 4 * (gates.index(j) + (len(GATES[0]) if aside else 0)) + 2 * s + m + 1)
                        ch.link(v.tensor_scalar(gate_e, gate_e, 1.0, None, ALU.add))
                        ch.link(v.reciprocal(gate_e, gate_e))
                        for (bank, out), (_, e) in zip(unit_parts(m, stage[:, m]), unit_parts(m, gate_e)):
                            ins = v.tensor_tensor(out, bank, e, ALU.mult)
                    else:
                        for bank, out in unit_parts(m, stage[:, m]):
                            if aside and fixed and j == 0:
                                ins = v.tensor_scalar(out, bank, QK_SC, None, ALU.mult)
                            else:
                                ins = v.tensor_copy(out, bank)
                    ins.then_inc(p.acc_used, 1)

                def pair(j):
                    for s in range(2):
                        for m in range(2):
                            unit(j, s, m)

                if aside:
                    for u in range(8):
                        unit(u // 4, u // 2 % 2, u % 2)
                        if 1 <= u <= 5:
                            aside(2 * u - 2)
                            if u < 5:
                                aside(2 * u - 1)
                else:
                    pair(0)
                start = 2 if aside else 1
                for g in (*gates, n // 2):
                    if start < g:
                        with v.Fori(start, g) as j:
                            pair(j)
                    if g < n // 2:
                        pair(g)
                    start = g + 1

            v.wait_ge(vec_in, 64)
            lp = lam_in.rearrange("p (a b) d -> p a b d", b=2)
            ch.link(v.tensor_tensor(lam_pr, lp[:, :, 0, :], lp[:, :, 1, :], ALU.mult))
            v.tensor_reduce(lam_s[:, 0:2], lam_pr, AX, ALU.add).then_inc(lam_ready, 1)
            normalize(norms[0], 16)
            v.wait_ge(lam_exp, 1)
            ch.link(v.scalar_tensor_tensor(out=neg_lam, in0=lam_s[:, 1:2], scalar=LAM0, in1=lam_s[:, 0:1],
                                           op0=ALU.subtract, op1=ALU.subtract))
            v.wait_ge(vecT_ready, 1)
            ch.link(v.tensor_copy(vec[:, :], ps[:, 7, 0:15]))
            ch.link(v.tensor_scalar(vec[:, 12:13], vec[:, 12:13], 1.0 - LAM0, None, ALU.mult))
            v.wait_ge(stT_ready, 1)
            v.tensor_copy(st_T[:, :, :], ps[:, 6, 0:8 * DB].rearrange("p (j r) -> p j r", r=2 * DB)).then_inc(stT_rows, 1)
            units_out(projs[0], NCH0, GATES[0])
            barrier(v, 0)

            v.wait_ge(qp_zero, 1)

            def head(h):
                v.wait_ge(att_in, 80 * h + 80)
                for w in range(2):
                    r = slice(w * DH, (w + 1) * DH)
                    ch.link(v.tensor_copy(q_pair[r, :, ds(h, 1), w * DS:(w + 1) * DS].rearrange("p b a s -> p b (a s)"),
                                          q_in[r, SEQ:TOK].rearrange("p (b s) -> p b s", s=DS)))
                for i in range(NT):
                    maxima(h, i)
                    if i:
                        mix(h, i - 1)
                mix(h, NT - 1)

            def maxima(h, i):
                st = row_st[:, i % 2, :]
                for w in range(2):
                    v.wait_ge(s_ready, 2 * (NT * h + i) + w + 1)
                    ch.link(v.tensor_reduce(st[:, w:w + 1], ps[:, 2 * w:2 * w + 2, :].rearrange("p a b -> p (a b)")[:, 0:(i + 1) * P],
                                            AX, ALU.max))
                    v.tensor_scalar(st[:, 2 + w:3 + w], st[:, w:w + 1], -SC, None, ALU.mult).then_inc(m_ready, 1)

            def mix(h, i):
                nk = (i + 1) * P
                st = row_st[:, i % 2, :]
                v.wait_ge(p_exp, 2 * (NT * h + i + 1))
                ch.link(v.reciprocal(st[:, 4:6], st[:, 4:6]))
                ch.link(v.tensor_scalar(st[:, 5:6], st[:, 5:6], neg_lam, None, ALU.mult))
                ch.link(v.tensor_scalar(prob[:, i % 3, 0, 0:nk], prob[:, i % 3, 0, 0:nk], st[:, 4:5], None, ALU.mult))
                v.scalar_tensor_tensor(out=prob[:, i % 3, 0, 0:nk], in0=prob[:, i % 3, 1, 0:nk], scalar=st[:, 5:6],
                                       in1=prob[:, i % 3, 0, 0:nk], op0=ALU.mult, op1=ALU.add).then_inc(p_mix, 1)

            head(0)
            with v.Fori(1, H) as h:
                ch.enter(h, 2 + 5 * NT, 1)
                head(h)
            ch.leave(H - 1)
            barrier(v, 1)

            idv = ident[0:NQ, 0:NQ].rearrange("p (h w s) -> p h w s", h=H, w=2)
            ch.link(v.tensor_tensor(s_pick[:, :, :], idv[:, :, 0, :], idv[:, :, 1, :], ALU.add))
            ch.link(v.tensor_reduce(s_sign[:, 0:1], idv[:, :, 1, :], mybir.AxisListType.XY, ALU.add))
            ch.link(v.tensor_scalar(s_sign[:, 1:2], neg_lam[0:NQ], -1.0, None, ALU.add))
            ch.link(v.tensor_scalar(s_sign[:, 2:3], s_sign[:, 0:1], s_sign[:, 1:2], 1.0, ALU.mult, ALU.add))

            def key_page(b, g):
                s = g // 4
                v.wait_ge(kT_hi, (PAGES + 1) * b + g + 1)
                cs_ = slice((g % 4) * P, (g % 4 + 1) * P)
                v.tensor_tensor(kTl[:, s % 2, :, cs_], ps[:, g % 2, :].rearrange("p (h k) -> p h k", h=H),
                                rd(kTh[:, s % 2, :, cs_]), ALU.subtract).then_inc(kT_lo, 1)

            def batch_query(b):
                ch.link(v.tensor_copy(q_b[:, :].rearrange("p (h c) -> p h c", h=H)[:, :, 0:2 * DS],
                                      q_pair[:, ds(b, 1), :, :].rearrange("p a h c -> p (a h) c")))
                ch.link(v.tensor_copy(q_bh[:, :], q_b[:, :]))
                v.tensor_tensor(q_bl[:, :], q_b[:, :], rd(q_bh[:, :]), ALU.subtract).then_inc(q_ready, 1)

            def group_max(b, s):
                v.wait_ge(sc_ready, 5 * b + s + 1)
                src = ps[0:NQ, 2 + s, :] if s < 4 else ps[0:NQ, 7, 0:DS]
                ch.link(v.tensor_reduce(s_max[:, s:s + 1], src, AX, ALU.max))

            def batch(b, last):
                group_max(b, 0)
                for g in range(8, 12):
                    key_page(b, g)
                group_max(b, 1)
                for g in range(12, 16):
                    key_page(b, g)
                for s in range(2, 5):
                    group_max(b, s)
                ch.link(v.tensor_reduce(s_max[:, 5:6], s_max[:, 0:5], AX, ALU.max))
                v.tensor_scalar(s_max[:, 5:6], s_max[:, 5:6], -SC, None, ALU.mult).then_inc(mx_ready, 1)
                if not last:
                    key_page(b + 1, 0)
                    key_page(b + 1, 1)
                v.wait_ge(pT_ready, 3 * b + 1)
                v.tensor_copy(pT[:, 0:8, :].rearrange("p g q -> p (g q)"), ps[:, 2, :]).then_inc(pT_used[0], 1)
                if not last:
                    key_page(b + 1, 2)
                    key_page(b + 1, 3)
                v.wait_ge(pT_ready, 3 * b + 3)
                v.tensor_copy(pT_new[:, :], ps[0:DS, 7, 64:64 + NQ]).then_inc(pT_used[0], 1)
                if not last:
                    batch_query(b + 1)
                    for g in range(4, 8):
                        key_page(b + 1, g)
                v.wait_ge(ps_exp, 5 * b + 5)
                ch.link(v.tensor_reduce(s_sum[:, 5:6], s_sum[:, 0:5], AX, ALU.add))
                ch.link(v.reciprocal(s_sum[:, 5:6], s_sum[:, 5:6]))
                ch.link(v.tensor_tensor(s_sum[:, 5:6], s_sum[:, 5:6], s_sign[:, 2:3], ALU.mult))
                v.wait_ge(so_ready, b + 1)
                v.tensor_scalar(s_out[:, :], ps[0:NQ, 6, :], s_sum[:, 5:6], None, ALU.mult).then_inc(so_scaled, 1)
                v.wait_ge(sp_ready, b + 1)
                v.tensor_copy(attT[:, :, ds(b * DS + SEQ, DS)],
                              ps[:, 7, 128:128 + H * DS].rearrange("p (h s) -> p h s", h=H))

            batch_query(0)
            for g in range(8):
                key_page(0, g)
            with v.Fori(0, DB - 1) as b:
                ch.enter(b, 11)
                batch(b, False)
            ch.leave(DB - 1)
            batch(DB - 1, True)
            barrier(v, 2)

            v.wait_ge(ulT_ready, 1)
            v.tensor_copy(u_rows[:, :], ps[0:2 * DB + 2, 7, :]).then_inc(ul_rows, 1)
            def lows(h):
                v.wait_ge(mix_hi, h + 1)
                ch.link(v.tensor_tensor(xl[:, h, :], att_g[:, h % 2, :], rd(xh[:, h, :]), ALU.subtract))

            for h in range(H):
                v.wait_ge(rs_ready, h + 1)
                ch.link(v.scalar_tensor_tensor(out=att_g[:, h % 2, :], in0=attT[:, h, :], scalar=vec[:, 12:13], in1=rs0[:, h % 2, :],
                                               op0=ALU.mult, op1=ALU.mult))
                v.wait_ge(gates_in, 16 * H)
                v.tensor_tensor(att_g[:, h % 2, :], att_g[:, h % 2, :], branch[:, h, :], ALU.mult).then_inc(mixed, 1)
                if h == 1:
                    v.wait_ge(products_in, 16 * H)
                    for j in range(4):
                        v.tensor_copy(xh[:, H + j, :], branch[:, H + j, :]).then_inc(br_hi, 1)
                if h:
                    lows(h - 1)
            lows(H - 1)
            barrier(v, 3)

            v.sem_inc(po.acc_used, 1)
            with v.Fori(0, D // CH // 2) as j:
                for s in range(2):
                    for t in range(NT + 1):
                        n = (NT + 1) * s + t
                        r = slice(0, P) if t < NT else slice(64, P)
                        v.wait_ge(po.acc_ready, 2 * (NT + 1) * j + n + 1)
                        x = x1[r, t, ds((2 * j + s) * CH, CH)]
                        v.tensor_tensor(x, ps[r, n % 6, 0:CH], x, ALU.add).then_inc(po.acc_used, 1)
            normalize(norms[1], 32)
            v.wait_ge(lr_acc, 1)
            for bank, out in unit_parts(1, stage[:, 1]):
                ins = v.tensor_copy(out, bank)
            ins.then_inc(lr_used, 1)

            def log_decay(t):
                v.wait_ge(z_abs, t + 1)
                if t >= 2:
                    v.wait_ge(la_out[t % 2], 16 * (t // 2))
                v.scalar_tensor_tensor(out=la_w[:, t % 2, :], in0=ps[:, 6 + t % 2, :], scalar=0.0, in1=zt[:, t % 2, :],
                                       op0=ALU.min, op1=ALU.subtract).then_inc(la_ready, 1)

            units_out(projs[1], NCH1, GATES[1], log_decay)
            barrier(v, 4)

            def gate(c, s):
                v.wait_ge(rs1_ready, c + 1)
                v.wait_ge(mh_ready, c)
                for d in range(2):
                    out = mt.rearrange("p (h d) i -> p h d i", d=2)[:, :, d, :]
                    ch.link(v.scalar_tensor_tensor(out=out, in0=ps[:, 6 + d, :].rearrange("p (h i) -> p h i", i=P),
                                                   scalar=vec[:, 13 + d:14 + d], in1=rs1[:, :].rearrange("p (h i) -> p h i", i=P),
                                                   op0=ALU.mult, op1=ALU.mult))
                v.tensor_tensor(mt, mt, g_c[:, s, :, :], ALU.mult).then_inc(m_mixed, 1)

            def level(c, s, i, hf):
                v.wait_ge(e_exp, 9 * c + i + 3)
                v.wait_ge(a_ready, 8 * c + max(i - 1, 0))
                e = ee[:, i % 2, :, :].rearrange("p h (n two r) -> p (h n) two r", two=2, r=hf)
                x = xlev[:, i % 2, :, :].rearrange("p h (n two r) -> p (h n) two r", two=2, r=hf)
                for w, m0 in ((0, GH), (1, 0)):
                    src = qk_c[:, s, m0:m0 + GH, :].rearrange("p h (n two r) -> p (h n) two r", two=2, r=hf)
                    ins = v.tensor_tensor(x[:, :, w, :], src[:, :, w, :], e[:, :, w, :], ALU.mult)
                    if w == 0:
                        ch.link(ins)
                    else:
                        ins.then_inc(x_ready, 1)

            def pairs(c, i, halves):
                wait_apart(v, (a_ready, 8 * c + i + 1), (a_used, 8 * c + i))
                src = ps[:, 4 + i % 2, :].rearrange("p (h i) -> p h i", i=P)
                if i == len(halves):
                    mask = ident[:, None, :].bitcast(I32).to_broadcast([P, GH, P])
                    v.copy_predicated(aT[:, :, :], mask, src).then_inc(a_used, 1)
                else:
                    hf = halves[i]
                    l = HALVES.index(hf)
                    split = "p h (n two r) -> p h n two r"
                    mask = lvl_mask[:, l:l + 1, :].bitcast(I32).rearrange(split, two=2, r=hf)[:, :, :, 1, :]
                    out = aT[:, :, :].rearrange(split, two=2, r=hf)[:, :, :, 1, :]
                    v.copy_predicated(out, mask.to_broadcast([P, GH, P // 2 // hf, hf]),
                                      src.rearrange(split, two=2, r=hf)[:, :, :, 1, :]).then_inc(a_used, 1)

            def low(c):
                v.wait_ge(mh_ready, c + 1)
                v.wait_ge(y_ready, 2 * c)
                v.tensor_tensor(ml[:, :, :], mt, rd(mh[:, :, :]), ALU.subtract).then_inc(ml_ready, 1)

            def residual(c, n, bank, r=slice(0, P)):
                v.wait_ge(y_ready, 2 * c + n + 1)
                x = x1[r, ds(c, 1), n * 512:(n + 1) * 512].rearrange("p a d -> p (a d)")
                v.tensor_tensor(x, ps[r, bank, :], x, ALU.add).then_inc(y_used, 1)

            def out_norm(c):
                v.wait_ge(y_rstd, c + 1)
                v.scalar_tensor_tensor(out=y_o[:, :], in0=x1[:, ds(c, 1), :].rearrange("p a d -> p (a d)"), scalar=rstd[:, 0:1],
                                       in1=norm_bc[:, :], op0=ALU.mult, op1=ALU.mult).then_inc(y_norm, 1)

            def levels(c, s, halves, first):
                L = len(halves)
                for i in range(first, L + 1):
                    pairs(c, i, halves)
                    if i + 2 < L:
                        level(c, s, i + 2, halves[i + 2])

            def state(c):
                v.wait_ge(sd_ready, c + 1)
                for h in range(GH):
                    v.scalar_tensor_tensor(out=st_g[:, h, :], in0=st_g[:, h, :], scalar=e_last[:, h, 0:1],
                                           in1=ps[:, 2 + h // 2, (h % 2) * DV:(h % 2 + 1) * DV],
                                           op0=ALU.mult, op1=ALU.add).then_inc(st_ready, 1)

            def body(c, s, halves, with_final=True):
                L = len(halves)
                level(c, s, 0, halves[0])
                level(c, s, 1, halves[1])
                if with_final:
                    residual(c - 2, 1, 4)
                gate(c - 1, 1 - s)
                v.wait_ge(g_zero, 2 if isinstance(c, int) and c == NT else 1)
                v.wait_ge(oT_ready, c)
                for i in range(2):
                    pairs(c, i, halves)
                low(c - 1)
                for i in range(2, min(4, L)):
                    level(c, s, i, halves[i])
                residual(c - 1, 0, 4)
                levels(c, s, halves, 2)
                if with_final:
                    out_norm(c - 2)

            v.wait_ge(norm_in, 48)
            v.wait_ge(g_zero, 1)
            level(0, 0, 0, HALVES[0])
            level(0, 0, 1, HALVES[1])
            levels(0, 0, HALVES, 0)
            state(0)
            body(1, 1, HALVES, False)
            state(1)
            with v.Fori(1, NT // 2) as j:
                ch.enter(j, 2 * (2 + 7), 1)
                body(2 * j, 0, HALVES)
                state(2 * j)
                body(2 * j + 1, 1, HALVES)
                state(2 * j + 1)
            ch.leave(NT // 2 - 1)
            body(NT, 0, HALVES[4:])
            residual(NT - 1, 1, 4)
            out_norm(NT - 1)
            def batch_keys(b):
                i = P - NS + b * DS + DS - 1
                if b >= 2:
                    v.wait_ge(sdb_ready, b - 1)
                v.tensor_scalar(kst_m[:, b % 2, :], kst[:, :], decay_m[:, 9, i:i + 1], None, ALU.mult).then_inc(km_ready, 1)

            v.wait_ge(y_out, 16 * NT)
            v.wait_ge(kst_ready, NT + 1)
            batch_keys(0)
            batch_keys(1)
            for b in range(DB):
                v.wait_ge(sdb_ready, b + 1)
                for h in range(GH):
                    ins = v.scalar_tensor_tensor(out=s0_b[b % 4][:, h, :], in0=s0_b[b % 4][:, h, :], scalar=e_last[:, h, b:b + 1],
                                                 in1=ps[:, (2, 0)[b % 2] + h // 2, (h % 2) * DV:(h % 2 + 1) * DV],
                                                 op0=ALU.mult, op1=ALU.add)
                ins.then_inc(s0_new, 1)
                if b + 2 < DB:
                    batch_keys(b + 2)
            gate(NT, 0)
            low(NT)
            for n in range(2):
                residual(NT, n, 4 + n, slice(64, P))
            out_norm(NT)
            barrier(v, 5)

        @block.tensor
        def _(pe):
            def transposes(n):
                def tile(t, s):
                    pe.wait_ge(n.xs_ready, t + 1)
                    if not (isinstance(t, int) and t < 2):
                        pe.wait_ge(n.lo, 2 * t - 2)
                    for q in range(2):
                        for k in range(4):
                            ins = pe.transpose(ps[:, 2 * s + q, k * P:(k + 1) * P], xs[:, s, (4 * q + k) * P:(4 * q + k + 1) * P], ident[:, :])
                        ins.then_inc(n.T_ready, 1)
                tile(0, 0)
                tile(1, 1)
                with pe.Fori(1, NT // 2) as j:
                    tile(2 * j, 0)
                    tile(2 * j + 1, 1)
                tile(NT, 0)

            def split_product(out, lh, ll, rh, rl, k, last):
                pe.matmul(out, lh, rh, start=(k == 0), stop=False)
                pe.matmul(out, lh, rl, start=False, stop=False)
                return pe.matmul(out, ll, rh, start=False, stop=last)

            def unit_products(s, m, mm):
                for k in range(KT):
                    w = (slice(None), s, k, slice(m * P, (m + 1) * P))
                    for wt, xt in ((wh, xh), (wh, xl), (wl, xh)):
                        for b in range(3):
                            c0, c1 = b * SG, min((b + 1) * SG, TOK)
                            ins = pe.matmul(ps[:, 3 * mm + b, 0:c1 - c0], wt[w], xt[:, k, c0:c1],
                                            start=(k == 0 and wt is wh and xt is xh),
                                            stop=(k == KT - 1 and wt is wl))
                return ins

            def project(p, n, aside=None):
                def unit(j, s, m):
                    if m == 0:
                        pe.wait_ge(p.lo, 2 * j + s + 1)
                    if not (isinstance(j, int) and j == 0 and s == 0):
                        pe.wait_ge(p.acc_used, 4 * j + 2 * s + m - 1)
                    elif aside and m == 1:
                        pe.wait_ge(lr_used, 1)
                    unit_products(s, m, m).then_inc(p.acc_ready, 1)

                def pair(j):
                    for s in range(2):
                        for m in range(2):
                            unit(j, s, m)

                if aside:
                    for u in range(8):
                        unit(u // 4, u // 2 % 2, u % 2)
                        if 1 <= u <= 5:
                            aside(2 * u - 2)
                            if u < 5:
                                aside(2 * u - 1)
                else:
                    pair(0)
                with pe.Fori(2 if aside else 1, n // 2) as j:
                    pair(j)

            pe.wait_ge(pool_step, 5)
            pe.wait_ge(vec_in, 64)
            pe.transpose(ps[:, 7, 0:15], vec_rows[:, :], ident[0:15, 0:15]).then_inc(vecT_ready, 1)
            pe.wait_ge(st_in, 16)
            for j in range(4):
                ins = pe.transpose(ps[:, 6, j * 2 * DB:(j + 1) * 2 * DB], st_rows[:, j * P:(j + 1) * P], ident[0:2 * DB, 0:2 * DB])
            ins.then_inc(stT_ready, 1)
            transposes(norms[0])
            pe.wait_ge(norms[0].lo, 2 * (NT + 1))
            project(projs[0], NCH0)
            barrier(pe, 0)

            def head(h):
                pe.wait_ge(att_in, 80 * h + 80)

                def bank_free(n):
                    if n < 2:
                        pe.wait_ge(probT_ready, 12 * h)
                    elif n < 8:
                        pe.wait_ge(rows_ready, 6 * h + n - 1)
                    else:
                        pe.wait_ge(probT_ready, 12 * h + n - 7)

                def rows(n):
                    src, t0 = (k_in, v_in)[n // 3], 4 * (n % 3)
                    bank_free(n)
                    for t in range(t0, min(t0 + 4, NT + 1)):
                        c0 = t * P if t < NT else TOK - P
                        ins = pe.transpose(ps[:, 4 + n % 2, (t - t0) * P:(t - t0 + 1) * P], src[:, c0:c0 + P], ident[:, :])
                    ins.then_inc(kv_T, 1)

                def scores(i, w):
                    nk = (i + 1) * P
                    if not (isinstance(h, int) and h == 0 and i == 0):
                        pe.wait_ge(p_exp, 2 * (NT * h + i - 1) + w + 1)
                    r = slice(w * DH, (w + 1) * DH)
                    for b in range(0, nk, 512):
                        e = min(b + 512, nk)
                        bank = ps[:, 2 * w + b // 512, 0:e - b]
                        diag = e == nk
                        ins = pe.matmul(bank, q_in[r, i * P:(i + 1) * P], k_in[r, b:e], start=True, stop=not diag)
                        if diag:
                            ins = pe.matmul(bank[:, e - b - P:e - b], identb[:, :], causal[:, :], start=False, stop=True)
                    ins.then_inc(s_ready, 1)

                def turn(i, n):
                    pe.wait_ge(p_mix, NT * h + i + 1)
                    for t0 in range(0, i + 1, 4):
                        bank_free(n)
                        for t in range(t0, min(t0 + 4, i + 1)):
                            ins = pe.transpose(ps[:, 4 + n % 2, (t - t0) * P:(t - t0 + 1) * P], prob[:, i % 3, 0, t * P:(t + 1) * P], ident[:, :])
                        ins.then_inc(kv_T, 1)
                        n += 1
                    return n

                def output(i, n):
                    pe.wait_ge(probT_ready, 12 * h + n - 6)
                    if i == 0:
                        pe.wait_ge(rows_ready, 6 * h + 6)
                    pe.wait_ge(o_used, NT * h + max(i - 1, 0))
                    for t in range(i + 1):
                        ins = pe.matmul(ps[:, 6 + i % 2, 0:P], v_row[:, t, :], probT[:, i % 2, t * P:(t + 1) * P],
                                        start=(t == 0), stop=(t == i))
                    ins.then_inc(o_ready, 1)

                scores(0, 0)
                scores(0, 1)
                for n in range(6):
                    rows(n)
                n = 6
                for i in range(1, NT + 2):
                    if i < NT:
                        scores(i, 0)
                    if i >= 2:
                        n = turn(i - 2, n)
                    if i < NT:
                        scores(i, 1)
                    if i >= 2:
                        output(i - 2, n)

            head(0)
            with pe.Fori(1, H) as h:
                head(h)
            barrier(pe, 1)

            def key_page(b, g):
                first = isinstance(b, int) and b == 0
                if g < PAGES and g % 4 == 0:
                    pe.wait_ge(k_page[g // 4], 64 * b + 64)
                if g >= 2:
                    pe.wait_ge(kT_lo, PAGES * b + g - 1)
                elif not first:
                    pe.wait_ge(*((kT_hi, (PAGES + 1) * b), (kT_lo, PAGES * b))[g])
                n = P if g < PAGES else DS
                if g == PAGES:
                    wait_apart(pe, (new_in, 32 * b + 32))
                for h in range(H):
                    src = kring[:, g // 4, g % 4, h * P:(h + 1) * P] if g < PAGES else k_new[:, h * P:(h + 1) * P]
                    ins = pe.transpose(ps[:, g % 2, h * n:(h + 1) * n], src, ident[0:n, 0:n])
                ins.then_inc(kT_ready, 1)

            def key_group(b, s):
                for g in range(4 * s, 4 * s + 4):
                    key_page(b, g)

            def scores(b, s, pages=()):
                if s == 0:
                    pe.wait_ge(q_ready, b + 1)
                if s < 4:
                    pe.wait_ge(kT_lo, PAGES * b + 4 * s + 4)
                    for h in range(H):
                        if pages:
                            key_page(b, pages[h])
                        qc = slice(h * P, (h + 1) * P)
                        ins = split_product(ps[:, 2 + s, :], q_bh[:, qc], q_bl[:, qc], kTh[:, s % 2, h, :], kTl[:, s % 2, h, :],
                                            h, h == H - 1)
                else:
                    pe.wait_ge(kT_hi, (PAGES + 1) * (b + 1))
                    out = ps[0:NQ, 7, 0:DS]
                    for h in range(H):
                        pe.matmul(out, q_b[:, h * P:h * P + NQ], kT_new[:, h, :], start=(h == 0), stop=False)
                if s == 4:
                    ins = pe.matmul(out, new_mask[:, :], ident[0:DS, 0:DS], start=False, stop=True)
                ins.then_inc(sc_ready, 1)

            def batch(b, last):
                scores(b, 1, range(8, 12))
                scores(b, 2, range(12, 16))
                key_page(b, PAGES)
                scores(b, 3)
                scores(b, 4)
                if not last:
                    key_group(b + 1, 0)
                for n in range(2):
                    wait_apart(pe, (ps_exp, 5 * b + 2 * n + 2))
                    for g in range(8):
                        ins = pe.transpose(ps[:, 2 + n, g * NQ:(g + 1) * NQ], p_s[:, (8 * n + g) * P:(8 * n + g + 1) * P], ident[0:NQ, 0:NQ])
                    ins.then_inc(pT_ready, 1)
                wait_apart(pe, (ps_exp, 5 * b + 5))
                pe.transpose(ps[0:DS, 7, 64:64 + NQ], p_s[:, PAGES * P:PAGES * P + DS], ident[0:NQ, 0:NQ]).then_inc(pT_ready, 1)
                pe.wait_ge(pT_used[0], 2 * b + 1)
                for g in range(PAGES):
                    if g % 4 == 0:
                        pe.wait_ge(v_page[g // 4], 64 * b + 64)
                    if g == 8:
                        pe.wait_ge(pT_used[1], b + 1)
                    ins = pe.matmul(ps[0:NQ, 6, :], pT[:, g, :], vring[:, g // 4, g % 4, :], start=(g == 0), stop=False)
                    if g % 4 == 3:
                        ins.then_inc(v_used, 1)
                        if not last:
                            key_page(b + 1, 4 + g // 4)
                pe.wait_ge(pT_used[0], 2 * b + 2)
                pe.matmul(ps[0:NQ, 6, :], pT_new[:, :], v_new[:, :], start=False, stop=True).then_inc(so_ready, 1)
                if not last:
                    scores(b + 1, 0)
                pe.wait_ge(so_scaled, b + 1)
                for h in range(H):
                    ins = pe.matmul(ps[:, 7, 128 + h * DS:128 + (h + 1) * DS], s_out[:, h * P:(h + 1) * P], s_pick[:, h, :],
                                    start=True, stop=True)
                ins.then_inc(sp_ready, 1)

            key_group(0, 0)
            key_group(0, 1)
            scores(0, 0)
            with pe.Fori(0, DB - 1) as b:
                batch(b, False)
            batch(DB - 1, True)
            barrier(pe, 2)

            pe.wait_ge(u_ready, 1)
            for j in range(4):
                ins = pe.transpose(ps[0:2 * DB + 2, 7, j * P:(j + 1) * P], u_last[:, j, :], ident[:, :])
            ins.then_inc(ulT_ready, 1)
            for h in range(H):
                pe.wait_ge(sq_ready, h + 1)
                if h >= 2:
                    pe.wait_ge(rs_ready, h - 1)
                for c0, c1 in TS:
                    ins = pe.matmul(acc(h % 2)[:, c0:c1], ones[:, :], sq0[:, h % 2, c0:c1], start=True, stop=True)
                ins.then_inc(sq_sum, 1)
            barrier(pe, 3)

            with pe.Fori(0, D // CH // 2) as j:
                for s in range(2):
                    pe.wait_ge(po.lo, 2 * j + s + 1)
                    for t in range(NT + 1):
                        n = (NT + 1) * s + t
                        pe.wait_ge(po.acc_used, 2 * (NT + 1) * j + max(n - 5, 0) + 1)
                        c0 = t * P if t < NT else TOK - P
                        for k in range(KT):
                            ins = split_product(ps[:, n % 6, 0:CH], xh[:, k, c0:c0 + P], xl[:, k, c0:c0 + P],
                                                wh[:, s, k, :], wl[:, s, k, :], k, k == KT - 1)
                        ins.then_inc(po.acc_ready, 1)
            transposes(norms[1])
            pe.wait_ge(norms[1].lo, 2 * (NT + 1))
            pe.wait_ge(lr_lo, 1)
            unit_products(1, 0, 1).then_inc(lr_acc, 1)

            def decay_logits(t):
                pe.wait_ge(lr_in, 16)
                pe.wait_ge(up_in, 32)
                if t >= 2:
                    pe.wait_ge(la_ready, t - 1)
                c0 = t * P if t < NT else TOK - P
                pe.matmul(ps[:, 6 + t % 2, :], lr_all[:, c0:c0 + P], w_up, start=True, stop=True).then_inc(z_ready, 1)

            project(projs[1], NCH1, decay_logits)
            barrier(pe, 4)

            def front(c, s):
                if not (isinstance(c, int) and c == 0):
                    pe.wait_ge(st_ready, GH * c)
                for n in range(2):
                    for m in range(4):
                        ins = pe.transpose(ps[:, 2 + n, m * P:(m + 1) * P], v_c[:, s, 4 * n + m, :], ident[:, :])
                    ins.then_inc(vT_ready, 1)

            def first_decays(c, s, use, m):
                pe.wait_ge(g_in[s], 64 * (use + 1))
                for l in range(2):
                    decay(c, s, l, m[l])

            def decay(c, s, l, mat):
                pe.wait_ge(e_exp, 9 * c + max(l - 1, 0))
                for h in range(GH):
                    ins = pe.matmul(ps[:, (1 + l) % 2, h * P:(h + 1) * P], la[:, s, h * P:(h + 1) * P], decay_m[:, mat, :], start=True, stop=True)
                ins.then_inc(e_ready, 1)

            def out_proj(c, n, bank):
                pe.wait_ge(ml_ready, c + 1)
                if isinstance(c, int) and c == 0:
                    pe.wait_ge(wo_lo, D // P)
                for k in range(KT):
                    cs_ = slice(n * 512, (n + 1) * 512)
                    ins = split_product(ps[:, bank, :], mh[:, k, :], ml[:, k, :], woh[:, k, cs_], wol[:, k, cs_], k, k == KT - 1)
                ins.then_inc(y_ready, 1)

            def pair_products(c, s, i, hf):
                if i >= 2:
                    pe.wait_ge(a_used, 8 * c + i - 1)
                if i == 0 and not (isinstance(c, int) and c < 2):
                    pe.wait_ge(y_used, 2 * c - 2)
                if i == 1 and not (isinstance(c, int) and c == 0):
                    pe.wait_ge(rs1_ready, c)
                if i == 2 and not (isinstance(c, int) and c == 0):
                    pe.wait_ge(y_used, 2 * c - 1)
                if hf:
                    pe.wait_ge(x_ready, 7 * c + i + 1)
                for h in range(GH):
                    out = ps[:, 4 + i % 2, h * P:(h + 1) * P]
                    if hf:
                        ins = pe.matmul(upper(out, hf), xlev[:, i % 2, h, :], upper(xlev[:, i % 2, h, :], hf), start=True, stop=True)
                    else:
                        ins = pe.matmul(out, qk_c[:, s, GH + h, :], qk_c[:, s, h, :], start=True, stop=True)
                ins.then_inc(a_ready, 1)

            def mats(L):
                return [0, 1] + list(range(2, 9)) if L == 7 else [9, 10, 6, 7, 8]

            def middle(c, s, L, next_use):
                m = mats(L)
                for i in range(L):
                    if i == 2 and not (isinstance(c, int) and c == 0):
                        pe.wait_ge(a_used, 8 * c + 1)
                        out_proj(c - 1, 0, 4)
                    if i + 4 < L + 2:
                        decay(c, s, i + 4, m[i + 4])
                    pair_products(c, s, i, HALVES[i - L])
                pair_products(c, s, L, 0)
                pe.wait_ge(ks_ready, c + 1)
                pe.wait_ge(v_ready, 2 * c + 2)
                for h in range(GH):
                    ins = pe.transpose(ps[:, 2, h * P:(h + 1) * P], ks[:, h, :], ident[:, :])
                ins.then_inc(ksT_ready, 1)
                if next_use is not None:
                    first_decays(c + 1, 1 - s, next_use, mats(3 if isinstance(c, int) and c == NT - 1 else 7))
                pe.wait_ge(a_used, 8 * c + L + 1)
                if next_use is None:
                    out_proj(c - 1, 1, 4)
                pe.wait_ge(qb_ready, c + 1)
                if not (isinstance(c, int) and c == 0):
                    pe.wait_ge(m_mixed, c)
                    pe.wait_ge(st_ready, GH * c)

            def out_prompt(c):
                for h in range(GH):
                    for d in range(2):
                        v0 = h * DV + d * P
                        out = ps[:, 6 + d, h * P:(h + 1) * P]
                        pe.matmul(out, v_tok[:, v0:v0 + P], aT[:, h, :], start=True, stop=False)
                        ins = pe.matmul(out, st_g[:, h, d * P:(d + 1) * P], qb[:, h, :], start=False, stop=True)
                ins.then_inc(oT_ready, 1)
                pe.wait_ge(kst_ready, c + 1)
                for h in range(GH):
                    ins = pe.matmul(ps[:, 2 + h // 2, (h % 2) * DV:(h % 2 + 1) * DV], kst[:, h * P:(h + 1) * P], v_tok[:, h * DV:(h + 1) * DV],
                                    start=True, stop=True)
                ins.then_inc(sd_ready, 1)

            def out_sample(c):
                for h in range(GH):
                    for d in range(2):
                        v0 = h * DV + d * P
                        pe.matmul(ps[:, 6 + d, h * P:(h + 1) * P], v_tok[:, v0:v0 + P], aT[:, h, :],
                                  start=(h == 0), stop=False, skip_group_check=True)
                pe.wait_ge(kst_ready, c + 1)
                for b in range(DB):
                    pe.wait_ge(s0_in[b % 4], 16 * (b // 4 + 1))
                    i0 = P - NS + b * DS
                    for h in range(GH):
                        for d in range(2):
                            ins = pe.matmul(ps[:, 6 + d, h * P + i0:h * P + i0 + DS], s0_b[b % 4][:, h, d * P:(d + 1) * P],
                                            qb[:, h, i0:i0 + DS], start=False, stop=(b == DB - 1), skip_group_check=True)
                    if b == DB - 1:
                        ins.then_inc(oT_ready, 1)
                    if b == 1:
                        pe.wait_ge(e_exp, 9 * c + 5)
                    if b >= 2:
                        pe.wait_ge(s0_new, b - 1)
                    pe.wait_ge(km_ready, b + 1)
                    for h in range(GH):
                        ins = pe.matmul(ps[:, (2, 0)[b % 2] + h // 2, (h % 2) * DV:(h % 2 + 1) * DV],
                                        kst_m[:, b % 2, h * P:(h + 1) * P], v_tok[:, h * DV:(h + 1) * DV], start=True, stop=True)
                    ins.then_inc(sdb_ready, 1)

            def row_sums(c):
                pe.wait_ge(sq1_ready, 2 * c + 2)
                for h in range(GH):
                    for d in range(2):
                        ins = pe.matmul(ps[:, 5, h * P:(h + 1) * P], ones[:, :], sq1[:, d, h, :], start=(d == 0), stop=(d == 1))
                ins.then_inc(r_ready, 1)

            def chunk(c, s, next_use, L=7):
                m = mats(L)
                for l in range(2, 4):
                    decay(c, s, l, m[l])
                if not (isinstance(c, int) and c < 2):
                    out_proj(c - 2, 1, 4)
                front(c, s)
                middle(c, s, L, next_use)
                if isinstance(c, int) and c == NT:
                    out_sample(c)
                else:
                    out_prompt(c)
                row_sums(c)

            pe.wait_ge(g_zero, 1)
            first_decays(0, 0, 0, mats(7))
            chunk(0, 0, 0)
            chunk(1, 1, 1)
            with pe.Fori(1, NT // 2 - 1) as j:
                chunk(2 * j, 0, j)
                chunk(2 * j + 1, 1, j + 1)
            chunk(NT - 2, 0, NT // 2 - 1)
            chunk(NT - 1, 1, NT // 2)
            chunk(NT, 0, None, 3)
            for n in range(2):
                out_proj(NT, n, 4 + n)
            barrier(pe, 5)


_INS = ['x_prompt', 'x_sample', 'cache_k', 'cache_v', 'state_conv', 'state_gla', 'page_table', 'norm_w', 'norm_f',
        'w_in_even', 'w_out_even', 'diff_lambda', 'diff_subln_w', 'conv_w', 'w_in_odd', 'w_gate_up', 'b_gate',
        'gla_norm_w', 'w_out_odd']


def kernel(**inputs):
    import numpy as _np
    import concourse.bacc as _bacc
    from concourse import mybir as _mybir
    from concourse.bass_utils import run_bass_kernel_spmd as _run

    nc = _bacc.Bacc("TRN2", target_bir_lowering=False, num_devices=1)
    arrays, a = {}, {}
    for name in _INS:
        v = _np.ascontiguousarray(inputs[name])
        arrays[f"in_{name}"] = v
        a[name] = nc.dram_tensor(f"in_{name}", v.shape, _mybir.dt.from_np(v.dtype), kind="ExternalInput").ap()
    B, T, D = inputs['x_prompt'].shape
    b, t, _ = inputs['x_sample'].shape
    L, _, _, H, K = inputs['cache_k'].shape
    V = inputs['cache_v'].shape[4]
    _, _, C1, CW = inputs['state_conv'].shape
    LO, _, GH, GK, GV = inputs['state_gla'].shape
    shapes = {
        'y_prompt': (B, T, D), 'y_sample': (b, t, D),
        'k_prompt': (L, B, T, H, K), 'v_prompt': (L, B, T, H, V),
        'k_sample': (L, b, t, H, K), 'v_sample': (L, b, t, H, V),
        'conv_prompt': (L, B, C1, CW), 'conv_sample': (L, b, C1, CW),
        'gla_prompt': (LO, B, GH, GK, GV), 'gla_sample': (LO, b, GH, GK, GV),
    }
    f32 = _mybir.dt.float32
    o = {n: nc.dram_tensor(f"out_{n}", s, f32, kind="ExternalOutput").ap() for n, s in shapes.items()}
    scr = [nc.dram_tensor(f"act{l}", (m * 128, T + b * t), f32, kind="Internal").ap() for l, m in ((0, 32), (1, 24))]
    scr.append(nc.dram_tensor("log_a", (T + 128, GH * GK), f32, kind="Internal").ap())
    build_step(nc, a, o, scr)
    r = _run(nc, [arrays], core_ids=[0])
    return tuple(r.results[0][f"out_{n}"] for n in shapes)
```
